# Optimizing a Trainium2 kernel written in Bass

```python
import jax
import jax.numpy as jnp
from jax import lax
import numpy as np

D_MODEL = 1024
BATCH = 1
SEQ = 1024
DEPTH = 1
DEC_BATCH = 8
DEC_SEQ = 16
PAST_LEN = 512

CHUNK = 64
SB_HEADS = 8
SB_HEAD_DIM = 64
SB_WIDTH = SB_HEADS * SB_HEAD_DIM
SB_Q_BLOCK = 128
HG_HEADS = 4
HG_KEY_DIM = 128
HG_VAL_DIM = 128
HG_KEY_WIDTH = HG_HEADS * HG_KEY_DIM
HG_VAL_WIDTH = HG_HEADS * HG_VAL_DIM
HG_BLOCK = 16
NORM_EPS = 1e-6
IN_SIZES = (SB_WIDTH, SB_WIDTH, SB_WIDTH, SB_WIDTH,
            HG_KEY_WIDTH, HG_KEY_WIDTH, HG_VAL_WIDTH, HG_VAL_WIDTH,
            D_MODEL, D_MODEL)
IN_WIDTH = sum(IN_SIZES)

kernel_name = 'stickbreak_hgrn2_streaming_step'

def rms_norm(x, g):
    xf = x.astype(jnp.float32)
    y = xf * lax.rsqrt(jnp.mean(xf * xf, axis=-1, keepdims=True) + NORM_EPS)
    return (y * g.astype(jnp.float32)).astype(x.dtype)

def stick_breaking_block(q, k, v, q_pos, k_pos):
    z = jnp.einsum('bthd,bshd->bhts', q.astype(jnp.float32), k.astype(jnp.float32)) * (SB_HEAD_DIM ** -0.5)
    mask = k_pos[None, :] < q_pos[:, None]
    log_fail = jnp.where(mask, jax.nn.log_sigmoid(-z), 0.0)
    after = lax.cumsum(log_fail, axis=3, reverse=True) - log_fail
    a = jnp.where(mask, jnp.exp(jax.nn.log_sigmoid(z) + after), 0.0)
    return jnp.einsum('bhts,bshd->bthd', a, v.astype(jnp.float32))

def stick_breaking_prompt(q, k, v):
    B, T, H, Dh = q.shape
    nq = T // SB_Q_BLOCK
    qb = q.reshape(B, nq, SB_Q_BLOCK, H, Dh).transpose(1, 0, 2, 3, 4)
    k_pos = jnp.arange(T)
    starts = jnp.arange(nq) * SB_Q_BLOCK

    def one_block(args):
        qi, s0 = args
        return stick_breaking_block(qi, k, v, s0 + jnp.arange(SB_Q_BLOCK), k_pos)

    o = lax.map(one_block, (qb, starts))
    return o.transpose(1, 0, 2, 3, 4).reshape(B, T, H, Dh)

def stick_breaking_cached(q, k, v, cache_k, cache_v):
    T = q.shape[1]
    P = cache_k.shape[1]
    k_all = jnp.concatenate([cache_k.astype(k.dtype), k], axis=1)
    v_all = jnp.concatenate([cache_v.astype(v.dtype), v], axis=1)
    return stick_breaking_block(q, k_all, v_all, P + jnp.arange(T), jnp.arange(P + T))

def hgrn2_chunkwise(q, log_f, v, s0):
    B, T, H, _ = q.shape
    pad = (-T) % HG_BLOCK
    if pad:
        widths = ((0, 0), (0, pad), (0, 0), (0, 0))
        q, log_f, v = jnp.pad(q, widths), jnp.pad(log_f, widths), jnp.pad(v, widths)
    n = (T + pad) // HG_BLOCK

    def to_blocks(a):
        return a.reshape(B, n, HG_BLOCK, H, a.shape[-1]).transpose(1, 0, 2, 3, 4)

    tril = jnp.tril(jnp.ones((HG_BLOCK, HG_BLOCK), dtype=bool))

    def step(S, blk):
        qb, lfb, vb = blk
        b = jnp.cumsum(lfb, axis=1)
        kb = -jnp.expm1(lfb)
        b_end = b[:, -1:]
        q_dec = qb * jnp.exp(b)
        k_inv = kb * jnp.exp(-b)
        att = jnp.where(tril, jnp.einsum('bthc,bshc->bhts', q_dec, k_inv), 0.0)
        o = jnp.einsum('bhts,bshv->bthv', att, vb) + jnp.einsum('bthc,bhcv->bthv', q_dec, S)
        k_end = kb * jnp.exp(b_end - b)
        S_new = jnp.exp(b_end[:, 0])[..., None] * S + jnp.einsum('bshc,bshv->bhcv', k_end, vb)
        return S_new, o

    S_fin, o = lax.scan(step, s0, (to_blocks(q), to_blocks(log_f), to_blocks(v)))
    o = o.transpose(1, 0, 2, 3, 4).reshape(B, T + pad, H, HG_VAL_DIM)[:, :T]
    return o, S_fin

def trunk_layer(x, cache_k, cache_v, s0, g_pre, w_in, b_gate, lb, hg_norm_g,
                w_branch_a, w_branch_b, w_out, g_post):
    B, T, _ = x.shape
    xn = rms_norm(x, g_pre)
    h = xn @ w_in
    points = np.cumsum(IN_SIZES)[:-1].tolist()
    sb_q, sb_k, sb_v, sb_z, hg_q, hg_f, hg_i, hg_z, gate_a, gate_b = jnp.split(h, points, axis=-1)
    b_a, b_b = jnp.split(b_gate, 2, axis=-1)

    q = sb_q.reshape(B, T, SB_HEADS, SB_HEAD_DIM)
    k = sb_k.reshape(B, T, SB_HEADS, SB_HEAD_DIM)
    v = sb_v.reshape(B, T, SB_HEADS, SB_HEAD_DIM)
    if cache_k is None:
        o_sb = stick_breaking_prompt(q, k, v)
    else:
        o_sb = stick_breaking_cached(q, k, v, cache_k, cache_v)

    f = lb + (1.0 - lb) * jax.nn.sigmoid(hg_f.astype(jnp.float32))
    log_f = jnp.log(f).reshape(B, T, HG_HEADS, HG_KEY_DIM)
    s_init = jnp.zeros((B, HG_HEADS, HG_KEY_DIM, HG_VAL_DIM), jnp.float32) if s0 is None else s0.astype(jnp.float32)
    o_hg, S_new = hgrn2_chunkwise(hg_q.astype(jnp.float32).reshape(B, T, HG_HEADS, HG_KEY_DIM), log_f,
                                  hg_i.astype(jnp.float32).reshape(B, T, HG_HEADS, HG_VAL_DIM), s_init)
    o_hg = rms_norm(o_hg, hg_norm_g)

    u_a = (o_sb.reshape(B, T, SB_WIDTH) * jax.nn.silu(sb_z)) @ w_branch_a
    u_b = (o_hg.reshape(B, T, HG_VAL_WIDTH) * jax.nn.silu(hg_z)) @ w_branch_b
    merged = jax.nn.sigmoid(gate_a + b_a) * u_a + jax.nn.sigmoid(gate_b + b_b) * u_b
    y = (x.astype(jnp.float32) + rms_norm((merged @ w_out).astype(jnp.float32), g_post)).astype(x.dtype)
    s_dtype = x.dtype if s0 is None else s0.dtype
    return y, k, v, S_new.astype(s_dtype)

def setup_inputs(seed: int = 0) -> dict:
    key = jax.random.key(seed)
    ks = jax.random.split(key, 16)
    f32 = jnp.float32
    nrm = lambda k, shape: jax.random.normal(k, shape, f32)
    return {
        'x_prompt': nrm(ks[0], (BATCH, SEQ, D_MODEL)),
        'x_sample': nrm(ks[1], (DEC_BATCH, DEC_SEQ, D_MODEL)),
        'cache_sb_k': nrm(ks[2], (DEPTH, DEC_BATCH, PAST_LEN, SB_HEADS, SB_HEAD_DIM)),
        'cache_sb_v': nrm(ks[3], (DEPTH, DEC_BATCH, PAST_LEN, SB_HEADS, SB_HEAD_DIM)),
        'state_hgrn': 0.5 * nrm(ks[4], (DEPTH, DEC_BATCH, HG_HEADS, HG_KEY_DIM, HG_VAL_DIM)),
        'g_pre': 1.0 + 0.02 * nrm(ks[5], (DEPTH, D_MODEL)),
        'w_in': nrm(ks[6], (DEPTH, D_MODEL, IN_WIDTH)) * D_MODEL ** -0.5,
        'b_gate': 0.02 * nrm(ks[7], (DEPTH, 2 * D_MODEL)),
        'hg_lb_raw': 0.1 * nrm(ks[8], (DEPTH + 1, HG_KEY_WIDTH)),
        'hg_norm_g': 1.0 + 0.02 * nrm(ks[9], (DEPTH, HG_HEADS, HG_VAL_DIM)),
        'w_branch_a': nrm(ks[10], (DEPTH, SB_WIDTH, D_MODEL)) * SB_WIDTH ** -0.5,
        'w_branch_b': nrm(ks[11], (DEPTH, HG_VAL_WIDTH, D_MODEL)) * HG_VAL_WIDTH ** -0.5,
        'w_out': nrm(ks[12], (DEPTH, D_MODEL, D_MODEL)) * D_MODEL ** -0.5,
        'g_post': 1.0 + 0.02 * nrm(ks[13], (DEPTH, D_MODEL)),
    }

def reference(x_prompt, x_sample, cache_sb_k, cache_sb_v, state_hgrn, g_pre, w_in, b_gate,
              hg_lb_raw, hg_norm_g, w_branch_a, w_branch_b, w_out, g_post):
    lb_all = jnp.cumsum(jax.nn.softmax(hg_lb_raw.astype(jnp.float32), axis=0), axis=0)
    y_p, y_s = x_prompt, x_sample
    kp_l, vp_l, sp_l, ks_l, vs_l, ss_l = [], [], [], [], [], []
    for l in range(DEPTH):
        y_p, kp, vp, sp = trunk_layer(y_p, None, None, None, g_pre[l], w_in[l], b_gate[l], lb_all[l],
                                      hg_norm_g[l], w_branch_a[l], w_branch_b[l], w_out[l], g_post[l])
        y_s, ksm, vsm, ssm = trunk_layer(y_s, cache_sb_k[l], cache_sb_v[l], state_hgrn[l], g_pre[l], w_in[l],
                                         b_gate[l], lb_all[l], hg_norm_g[l], w_branch_a[l], w_branch_b[l],
                                         w_out[l], g_post[l])
        kp_l.append(kp); vp_l.append(vp); sp_l.append(sp)
        ks_l.append(ksm); vs_l.append(vsm); ss_l.append(ssm)
    new_k_prompt = jnp.stack(kp_l)
    new_v_prompt = jnp.stack(vp_l)
    new_state_prompt = jnp.stack(sp_l)
    new_k_sample = jnp.stack(ks_l)
    new_v_sample = jnp.stack(vs_l)
    new_state_sample = jnp.stack(ss_l)
    return (y_p, y_s, new_k_prompt, new_v_prompt, new_state_prompt, new_k_sample, new_v_sample, new_state_sample)


_drawn_inputs = setup_inputs


def setup_inputs(seed=0):
    import zlib

    import numpy as np

    out = dict(_drawn_inputs(seed))
    spreads = {}
    factors = {}
    for name, (base, spread) in spreads.items():
        noise = np.random.default_rng([zlib.crc32(name.encode()), seed]).standard_normal(out[name].shape)
        drawn = base * np.exp(spread * noise) if base else spread * noise
        out[name] = jnp.asarray(drawn.astype(out[name].dtype))
    for name, factor in factors.items():
        out[name] = (out[name] * factor).astype(out[name].dtype)
    return out
```

```python
from contextlib import ExitStack

import numpy as np

import concourse.bass as bass
from concourse import mybir

F32 = mybir.dt.float32
F32R = mybir.dt.float32r
ALU = mybir.AluOpType
ACT = mybir.ActivationFunctionType

P = 128
D = 1024
SEQ, STREAMS, DSEQ, PAST = 1024, 8, 16, 512
TOK = SEQ + STREAMS * DSEQ
WIN = 384
NW = TOK // WIN
KT_N = D // P
PAIRS = 4
DH = 64
QW = 512
NS = 24
PIECES = 3
EPS = 1e-6
BIG = 3.0e38
BLK = 32
NBLK = SEQ // BLK
NT = TOK // P

GATE_W0 = 108
OUT_W0 = 144

C1 = {"ident": (0, 128), "bgate": (128, 16), "lbraw": (144, 8), "hgn": (152, 4), "gpre": (156, 8), "gpost": (164, 8),
      "eps": (172, 1)}
C1_W = 173
C2 = {"negtri": (0, 128), "negones": (128, 128), "causal": (256, 128), "hgmask": (384, 128), "hgmask_s": (512, 128),
      "smask": (640, 256), "reset": (896, 128), "reset_s": (1024, 128), "rows4": (1152, 4), "rows8": (1156, 8)}
C2_W = 1164


def attention_steps():
    return [(wd, j, h) for wd in range(SEQ // QW) for j in range(4 * wd + 3, -1, -1) for h in range(2)]


STEPS = attention_steps()
assert len(STEPS) == NS


def diagonal(n):
    wd, j, _ = STEPS[n]
    return j >= 4 * wd


def first_col(n):
    wd, j, _ = STEPS[n]
    return P * max(j - 4 * wd, 0)


def diagonals_until(n):
    return sum(diagonal(i) for i in range(n + 1))


DIAGS = diagonals_until(NS - 1)


def sums_until(n):
    return sum(STEPS[i][1] > 0 for i in range(n + 1))


SUMS = sums_until(NS - 1)


def spread(weights, total):
    out, acc, done = [], 0.0, 0
    for w in weights:
        acc += w
        upto = int(round(total * acc / sum(weights)))
        out.append(list(range(done, upto)))
        done = upto
    return out


B_STEPS = NS + 2
B_PIECES = spread([max(QW - first_col(n), 200) if n < NS else 300 for n in range(B_STEPS)], 12 * PIECES)
A_STEPS = 3 + NT + 3
A_PIECES = spread([4, 4, 4] + [2] * (A_STEPS - 3), 12 * PIECES)


def ended(pieces):
    return [x // PIECES for x in pieces if x % PIECES == PIECES - 1]


def win_of(g):
    if g < 36:
        return 3 * g
    if g >= 56:
        return OUT_W0 + 3 * (g - 56)
    dm, kind = (g - 38) // 3 + 2, (g - 38) % 3
    return GATE_W0 + 6 * (dm - 2) + 3 * kind


def gate_b_slot(dm):
    return 7 if dm in (1, 3, 5) else 8


def is_branch(g):
    return g in (36, 37) or (38 <= g < 56 and (g - 38) % 3 == 2)


def branch_of(g):
    return g - 36 if g < 38 else (g - 38) // 3 + 2


def x_use_tile(c):
    return c if c <= 6 else c + 1


X_USE_MS = (7, 10, 11)
MS_STEP = (6, 10, 11)
GROUPS = ((0, 4), (4, 8), (8, 9))


def build(nc, xT, wch, ckT, cv, st, c1, c2, yT, okT, ov, osp, oss, spill):
    with ExitStack() as ctx:
        off = [0]
        base = nc.sbuf_base + (-nc.sbuf_base) % 32
        arena = ctx.enter_context(nc.sbuf_tensor("arena", [P, (nc.sbuf_usable_end - base) // 4 - 16], F32))
        limit = (nc.sbuf_usable_end - base) - 64

        def at(name, shape, dt, offset):
            size = 4 * int(np.prod(shape[1:]))
            assert offset + size <= limit, (name, offset + size, limit)
            return nc.alloc_sbuf_tensor_at(name, shape, dt, offset=base + offset)

        def take(name, shape, dt=F32):
            o = off[0]
            off[0] += 4 * int(np.prod(shape[1:]))
            off[0] += (-off[0]) % 32
            return at(name, shape, dt, o), o

        def sem(name):
            return ctx.enter_context(nc.semaphore(name))

        xh, _ = take("xh", [P, KT_N, TOK], F32R)
        xl, _ = take("xl", [P, KT_N, TOK], F32R)
        wr, wl, wh = [], [], []
        for i in range(3):
            t, o = take(f"wr{i}", [P, KT_N, P])
            wr.append(t)
            wl.append(at(f"wl{i}", [P, KT_N, P], F32R, o))
        for i in range(2):
            wh.append(take(f"wh{i}", [P, KT_N, P], F32R)[0])
        k1, _ = take("k1", [P, C1_W])
        lbv, _ = take("lbv", [P, 5, 4])
        ngate, _ = take("ngate", [P, 16])
        slot_order = (0, 1, 7, 8, 2, 3, 4, 5, 6)
        stage, slots = [], {}
        for name, m in zip(("qT", "kT", "zA", "v_nat", "hq", "kb", "lf", "i_nat", "zB"), slot_order):
            t, o = take(name, [P, TOK])
            stage.append(t)
            slots[m] = at(f"slot{m}", [P, TOK], F32, o)
            if m == 0:
                slots_base = o
        qT, kT, zA, v_nat, hq, kb, lf, i_nat, zB = stage
        xres = at("xres", [P, KT_N, TOK], F32, slots_base)
        work = off[0]
        KT_, kt_o = take("KTc", [P, STREAMS, PAST])
        V_, v_o = take("Vc", [P, STREAMS, 4, P])
        k2, _ = take("k2", [P, C2_W])
        qbd, _ = take("qbd", [P, STREAMS, 2, DSEQ])
        kTs, _ = take("kTs", [P, P])
        vs, _ = take("vs", [P, P])
        zAs, _ = take("zAs", [P, P])
        tmpT = [take(f"tmpT{i}", [P, WIN])[0] for i in range(2)]
        hsq, _ = take("hsq", [P, 4 * P])
        hrs, _ = take("hrs", [P, 4 * P])
        bm, _ = take("bm", [P, NBLK + STREAMS])
        be, _ = take("be", [P, NBLK + STREAMS])
        gg, _ = take("gg", [P, NBLK + STREAMS])
        em, _ = take("em", [P, STREAMS])
        bt_o = off[0]
        E = [take(f"E{i}", [P, QW])[0] for i in range(2)]
        SPb = [take(f"SP{i}", [P, QW])[0] for i in range(3)]
        SUM = [[take(f"SUM{h}{i}", [P, QW])[0] for i in range(2)] for h in range(2)]
        Aw = [take(f"Aw{i}", [P, QW])[0] for i in range(2)]
        Es = at("Es", [P, 5, 256], F32, bt_o)
        SPs = at("SPs", [P, 5, 256], F32, bt_o + 5120)
        SUs = at("SUs", [P, 3, 256], F32, bt_o + 10240)
        EK = at("EK", [P, TOK], F32, bt_o + 13312)
        EQ = at("EQ", [P, TOK], F32, bt_o + 17920)
        St = [at(f"St{i}", [P, P], F32, kt_o + 512 * i) for i in range(8)]
        kendN = [at(f"kendN{i}", [P, P], F32, kt_o + 4096 + 512 * i) for i in range(2)]
        attm = [at(f"attm{i}", [P, P], F32, kt_o + 5120 + 512 * i) for i in range(2)]
        imask = at("imask", [P, 8, P], F32, kt_o + 6144)
        S0s = at("S0s", [P, STREAMS, P], F32, kt_o + 10240)
        oc = at("oc", [P, 4 * P], F32, kt_o + 14336)
        xw = [at(f"xw{i}", [P, KT_N, WIN], F32, kt_o + 12288 * i) for i in range(2)]
        xsq = [at(f"xsq{i}", [P, WIN], F32, kt_o + 24576 + 1536 * i) for i in range(4)]
        xrs = SUM[0][0]
        gh = at("gh", [P, KT_N, TOK], F32R, work)
        gl = at("gl", [P, KT_N, TOK], F32R, work + 4 * KT_N * TOK)
        yb = at("yb", [P, KT_N, TOK], F32, work)
        ysq = [at(f"ysq{i}", [P, WIN], F32, work + 4 * KT_N * TOK + 1536 * i) for i in range(3)]
        yrs = [at(f"yrs{i}", [P, WIN], F32, work + 4 * KT_N * TOK + 1536 * (3 + i)) for i in range(3)]
        no4 = at("no4", [P, P], F32, work + 4 * KT_N * TOK + 1536 * 6)

        bank = [ctx.enter_context(nc.psum_tensor(f"bank{i}", [P, 512], F32)) for i in range(8)]
        CH, Z, OB, TB, XB = bank[0:2], bank[2:5], bank[5], bank[6], bank[7]
        UA, UB = (bank[2], bank[4]), (bank[3], bank[5])

        def cst(d, t, name):
            o, n = d[name]
            return t[:, o:o + n]

        ident = cst(C1, k1, "ident")
        bgate, lbraw, hgn, gpre, gpost, eps_col = (cst(C1, k1, n) for n in ("bgate", "lbraw", "hgn", "gpre", "gpost", "eps"))
        negtri, negones, causal, hgmask, hgmask_s, smask, reset, reset_s, rows4, rows8 = (
            cst(C2, k2, n) for n in ("negtri", "negones", "causal", "hgmask", "hgmask_s", "smask", "reset", "reset_s", "rows4", "rows8"))

        s_c = sem("consts_loaded")
        s_x = [sem(f"x_loaded{i}") for i in range(2)]
        s_raw = [sem(f"chunk_loaded{i}") for i in range(3)]
        s_whi = sem("weights_high")
        s_wlo = sem("weights_low")
        s_xsq = sem("x_squared")
        s_xms = sem("x_meansq_step")
        s_xln = sem("x_log")
        s_xrs = sem("x_rstd")
        s_xn = sem("x_normed")
        s_xhi = sem("x_high")
        s_xlo = sem("x_low")
        s_win = sem("window_product")
        s_ev = sem("window_out_of_psum")
        s_ex = sem("window_exp")
        s_tr = sem("window_transposed")
        s_te = sem("transposed_in_sbuf")
        s_sg1 = sem("silu_plus_one")
        s_sg = sem("silu_reciprocal")
        s_silu = sem("silu_done")
        s_f1 = sem("forget_denominator")
        s_f = sem("forget_complement")
        s_lf = sem("forget_log")
        s_lb = sem("lower_bound_step")
        s_lbe = sem("lower_bound_exp")
        s_qk = sem("scores")
        s_E = sem("scores_exp")
        s_L = sem("scores_log")
        s_sp1 = sem("softplus_raw")
        s_sp = sem("softplus")
        s_S = sem("later_sum")
        s_cum = sem("log_weights")
        s_a = sem("weights")
        s_am = sem("weights_masked")
        s_av = sem("values_added")
        s_gA = sem("attention_gated")
        s_cp = sem("sample_copies")
        s_qz = sem("qbd_zeroed")
        s_kv = [sem("keysT_cached"), sem("values_cached")]
        s_kout = sem("k_stored")
        s_vout = sem("v_stored")
        s_spA = sem("gated_a_spilled")
        s_spB = sem("gated_b_spilled")
        s_zs = sem("sample_scores")
        s_Es = sem("sample_exp")
        s_Ls = sem("sample_log")
        s_sps = sem("sample_softplus")
        s_spm = sem("sample_softplus_masked")
        s_Ss = sem("sample_later_sum")
        s_cs = sem("sample_log_weights")
        s_as = sem("sample_weights")
        s_asm = sem("sample_weights_masked")
        s_os = sem("sample_values_added")
        s_gs = sem("sample_gated")
        s_scan = sem("decay_scanned")
        s_bmc = sem("block_ends_copied")
        s_A = sem("decay_centred")
        s_ge = sem("block_decay_log")
        s_EX = sem("decay_exp")
        s_hqd = sem("queries_decayed")
        s_hki = sem("keys_grown")
        s_hke = sem("keys_to_block_end")
        s_S0 = sem("state_zeroed")
        s_S0l = sem("state_loaded")
        s_S0m = sem("state_scaled")
        s_im = sem("values_by_block")
        s_kt = sem("keys_transposed")
        s_kn = sem("keys_natural")
        s_at = sem("hgrn_scores")
        s_atm = sem("hgrn_scores_masked")
        s_KV = sem("block_updates")
        s_ch = sem("state_step")
        s_h3 = sem("hgrn_out")
        s_oc = sem("hgrn_out_copied")
        s_hs = sem("hgrn_squared")
        s_hm = sem("hgrn_meansq")
        s_hl = sem("hgrn_log")
        s_hr = sem("hgrn_rstd")
        s_hg1 = sem("hgrn_normed")
        s_hg = sem("hgrn_gated")
        s_ss1 = sem("sample_state_decayed")
        s_ss = sem("sample_state")
        s_so = sem("prompt_state_stored")
        s_sso = sem("sample_state_stored")
        s_gr = [sem(f"gated_reloaded{i}") for i in range(5)]
        s_gh = sem("gated_high")
        s_gl = sem("gated_low")
        s_g1 = sem("gate_plus_one")
        s_sig = sem("gate_sigmoid")
        s_u = sem("branch_products")
        s_ma = sem("branch_a_gated")
        s_mb = sem("branch_b_gated")
        s_mg = sem("merged")
        s_mh = sem("merged_high")
        s_ml = sem("merged_low")
        s_xr = sem("residual_loaded")
        s_no = sem("minus_ones")
        s_yq = sem("y_squared")
        s_yn = sem("y_meansq_step")
        s_yl = sem("y_log")
        s_yr = sem("y_rstd")
        s_yg = sem("y_scaled")
        s_yo = sem("y_done")
        s_out = sem("y_stored")

        def need(eng, s, v):
            if v > 0:
                eng.wait_ge(s, v)

        def chunk_done(eng, g):
            if g < 0:
                return
            if is_branch(g):
                eng.wait_ge(s_u, 3 * branch_of(g) + 3)
            else:
                eng.wait_ge(s_win, win_of(g) + 3)

        def attention_over(eng, p):
            need(eng, s_a, NS * (p + 1))
            need(eng, s_am, DIAGS * (p + 1))
            need(eng, s_av, NS * (p + 1))
            need(eng, s_gA, 2 * (p + 1))
            need(eng, s_S, SUMS * (p + 1))

        def recurrence_over(eng, p):
            need(eng, s_ss, 2 * (p + 1))
            need(eng, s_hg, 3 * (p + 1))
            need(eng, s_gs, 2 * (p + 1))
            need(eng, s_ch, NBLK * (p + 1))
            need(eng, s_hki, p + 1)
            need(eng, s_hqd, p + 1)

        block = ctx.enter_context(nc.Block())

        @block.sync
        def _(sp):
            def load_chunk(g):
                chunk_done(sp, g - 3)
                sp.dma_start(wr[g % 3][:, :, :], wch[g].rearrange("p (k c) -> p k c", c=P)).then_inc(s_raw[g % 3], 16)

            def load_x(w):
                if w == 2:
                    sp.wait_ge(s_xlo, KT_N)
                sp.dma_start(xw[w % 2][:, :, :], xT[:, :, w * WIN:(w + 1) * WIN]).then_inc(s_x[w % 2], 16)

            def store_kv(pp):
                sp.wait_ge(s_ev, win_of(1 + (8 * pp if pp else 0)) + 3)
                sp.dma_start(okT[pp], kT[:, :]).then_inc(s_kout, 16)
                sp.wait_ge(s_te, 6 * pp + 3)
                sp.dma_start(ov[pp].rearrange("(t s) c -> s t c", s=P), v_nat[:, :].rearrange("s (t c) -> s t c", c=P)).then_inc(s_vout, 16)

            load_x(0)
            sp.dma_start(k1[:, :], c1).then_inc(s_c, 16)
            load_x(1)
            load_chunk(0)
            sp.dma_start(k2[:, :], c2).then_inc(s_c, 16)
            load_chunk(1)
            load_x(2)
            for g in range(2, 7):
                load_chunk(g)
            store_kv(0)
            for p in range(PAIRS):
                recurrence_over(sp, p - 1)
                if p:
                    sp.wait_ge(s_sso, 16 * p)
                    sp.wait_ge(s_so, 16 * p)
                    sp.wait_ge(s_os, p)
                else:
                    sp.wait_ge(s_xlo, NW * KT_N)
                    sp.wait_ge(s_xms, NW * KT_N)
                sp.dma_start(KT_[:, :, :], ckT[p].rearrange("i d s -> d i s")).then_inc(s_kv[0], 16)
                sp.dma_start(V_[:, :, :, :].rearrange("s i j c -> s i (j c)"), cv[p].rearrange("i s n -> s i n")).then_inc(s_kv[1], 16)
                for g in range(4 + 8 * p + 3, 8 + 8 * p + 3):
                    load_chunk(g)
                sp.wait_ge(s_gA, 2 * (p + 1))
                sp.dma_start(spill[p, :, 0:SEQ], zA[:, 0:SEQ]).then_inc(s_spA, 16)
                sp.wait_ge(s_zs, 3 * (p + 1))
                recurrence_over(sp, p - 1)
                sp.dma_start(S0s[:, :, :], st[p].rearrange("i c v -> c i v")).then_inc(s_S0l, 16)
                sp.wait_ge(s_gs, 2 * (p + 1))
                sp.dma_start(spill[p, :, SEQ:TOK], zAs[:, :]).then_inc(s_spA, 16)
                for g in range(8 + 8 * p + 3, 12 + 8 * p + 3):
                    load_chunk(g)
                sp.wait_ge(s_ch, NBLK * (p + 1))
                sp.dma_start(osp[p], St[NBLK % 8][:, :]).then_inc(s_so, 16)
                sp.wait_ge(s_hg, 3 * (p + 1))
                sp.dma_start(spill[PAIRS + p], zB[:, :]).then_inc(s_spB, 16)
                sp.wait_ge(s_ss, 2 * (p + 1))
                sp.dma_start(oss[p].rearrange("i c v -> c i v"), S0s[:, :, :]).then_inc(s_sso, 16)
                if p + 1 < PAIRS:
                    store_kv(p + 1)
            recurrence_over(sp, PAIRS - 1)
            sp.wait_ge(s_h3, NT * PAIRS)
            sp.wait_ge(s_spA, 2 * 16 * PAIRS)
            sp.wait_ge(s_spB, 16 * PAIRS)
            for kk in range(8):
                if kk >= 5:
                    sp.wait_ge(s_gl, kk - 4)
                sp.dma_start(slots[2 + kk % 5][:, :], spill[kk]).then_inc(s_gr[kk % 5], 16)
            for g in range(39, 64):
                load_chunk(g)
            sp.wait_ge(s_ml, 8)
            sp.dma_start(xres[:, :, :], xT).then_inc(s_xr, 16)
            for w in range(NW):
                for half in range(2):
                    sp.wait_ge(s_yo, KT_N * w + 4 * half + 4)
                    sp.dma_start(yT[:, 4 * half:4 * half + 4, w * WIN:(w + 1) * WIN],
                                 yb[:, 4 * half:4 * half + 4, w * WIN:(w + 1) * WIN]).then_inc(s_out, 16)
            sp.wait_ge(s_out, 16 * 2 * NW)
            sp.wait_ge(s_kout, 16 * PAIRS)
            sp.wait_ge(s_vout, 16 * PAIRS)
            sp.wait_ge(s_so, 16 * PAIRS)
            sp.wait_ge(s_sso, 16 * PAIRS)

        @block.tensor
        def _(pe):
            def product(g, w, q):
                n = win_of(g) + w
                if q == 0:
                    if w == 0:
                        pe.wait_ge(s_whi, g + 1)
                        pe.wait_ge(s_wlo, g + 1)
                    need(pe, s_ev, n - 1)
                for m in range(8 * q, 8 * q + 8):
                    k, part = m // 3, m % 3
                    if g == 0 and part == 0:
                        pe.wait_ge(s_xhi, KT_N * w + k + 1)
                    if g == 0 and part == 1:
                        pe.wait_ge(s_xlo, KT_N * w + k + 1)
                    if g == 56 and q == 0 and m == 0 and w == 0:
                        pe.wait_ge(s_mh, 8)
                        pe.wait_ge(s_ml, 8)
                    weights = wl[g % 3] if part == 2 else wh[g % 2]
                    rows = xl if part == 1 else xh
                    i = nc.tensor.matmul(CH[n % 2][:, 0:WIN], weights[:, k, :], rows[:, k, w * WIN:(w + 1) * WIN],
                                         start=(m == 0), stop=(m == 23))
                    if m == 23:
                        i.then_inc(s_win, 1)

            def transpose_window(n, idx, src):
                pe.wait_ge(s_ev, n + 1)
                need(pe, s_te, idx)
                for t in range(3):
                    i = nc.tensor.transpose(TB[:, t * P:(t + 1) * P], src[:, t * P:(t + 1) * P], ident)
                i.then_inc(s_tr, 1)

            def turn_attention(pp, w12):
                c, w = divmod(w12, 3)
                if c == 2:
                    transpose_window(win_of(8 * pp if pp else 0) + w12, 6 * pp + w, tmpT[(12 * pp + w) % 2])

            def turn_recurrence(p, w12):
                c, w = divmod(w12, 3)
                if c == 2:
                    transpose_window(win_of(4 + 8 * p) + w12, 6 * p + 3 + w, tmpT[(12 * p + 6 + w) % 2])

            pe.wait_ge(s_c, 32)
            for w in range(NW):
                for k in range(KT_N):
                    pe.wait_ge(s_xsq, KT_N * w + k + 1)
                    nc.tensor.matmul(Z[w][:, 0:WIN], negones, xsq[(KT_N * w + k) % 4][:, :],
                                     start=(k == 0), stop=(k == KT_N - 1)).then_inc(s_xms, 1)
            for w12 in range(12):
                for q in range(PIECES):
                    product(w12 // 3, w12 % 3, q)
                if w12:
                    turn_attention(0, w12 - 1)
            turn_attention(0, 11)

            for p in range(PAIRS):
                recurrence_over(pe, p - 1)
                late = []
                for n in range(B_STEPS):
                    if n < NS:
                        wd, j, h = STEPS[n]
                        c0, t = first_col(n), NS * p + n
                        if n == 0:
                            pe.wait_ge(s_ev, win_of(8 * p if p else 0) + 6)
                        need(pe, s_a, t - 2)
                        nc.tensor.matmul(Z[n % 3][:, c0:QW], kT[DH * h:DH * h + DH, j * P:(j + 1) * P],
                                         qT[DH * h:DH * h + DH, wd * QW + c0:(wd + 1) * QW],
                                         start=True, stop=True).then_inc(s_qk, 1)
                    mid = len(B_PIECES[n]) // 2
                    for x in B_PIECES[n][:mid]:
                        product(4 + 8 * p + x // 9, x // 3 % 3, x % 3)
                    if 1 <= n <= NS:
                        m = n - 1
                        wd, j, h = STEPS[m]
                        c0, t = first_col(m), NS * p + m
                        pe.wait_ge(s_sp, t + 1)
                        i = nc.tensor.matmul(Z[m % 3][:, c0:QW], negtri, SPb[m % 3][:, c0:QW],
                                             start=False, stop=True, skip_group_check=True)
                        q = 4 * wd + 3 - j
                        if q:
                            pe.wait_ge(s_S, SUMS * p + sums_until(m - 2))
                            cs = first_col(m - 2)
                            i = nc.tensor.matmul(Z[m % 3][:, cs:QW], negones, SUM[h][q % 2][:, cs:QW],
                                                 start=False, stop=True, skip_group_check=True)
                        i.then_inc(s_cum, 1)
                    for x in B_PIECES[n][mid:]:
                        product(4 + 8 * p + x // 9, x // 3 % 3, x % 3)
                    if n >= 2:
                        m = n - 2
                        wd, j, h = STEPS[m]
                        c0, t = first_col(m), NS * p + m
                        if m == 0:
                            pe.wait_ge(s_te, 6 * p + 3)
                        if j == 4 * wd + 3 and h == 0:
                            need(pe, s_gA, 2 * p + wd)
                        pe.wait_ge(s_a, t + 1)
                        if diagonal(m):
                            pe.wait_ge(s_am, DIAGS * p + diagonals_until(m))
                        nc.tensor.matmul(OB[DH * h:DH * h + DH, c0:QW], v_nat[:, j * P + DH * h:j * P + DH * h + DH],
                                         Aw[m % 2][:, c0:QW], start=(j == 4 * wd + 3), stop=(j == 0),
                                         skip_group_check=True).then_inc(s_av, 1)
                    for w12 in late:
                        turn_recurrence(p, w12)
                    late = ended(B_PIECES[n])
                for w12 in late:
                    turn_recurrence(p, w12)

                late = []
                for m in range(A_STEPS):
                    if m == 0:
                        attention_over(pe, p)
                        pe.wait_ge(s_cp, 5 * (p + 1))
                        pe.wait_ge(s_kv[0], 16 * (p + 1))
                        qall = qbd[:, :, :, :].rearrange("p i h t -> p (i h t)")
                        nc.tensor.matmul(Z[2][:, 0:256], kTs[:, :], qall, start=True, stop=True).then_inc(s_zs, 1)
                        for half in (1, 0):
                            for j2 in range(2):
                                for s in range(STREAMS):
                                    o = 256 * j2 + 32 * s
                                    i = nc.tensor.matmul(Z[half][:, o:o + 32], KT_[:, s, P * (2 * half + j2):P * (2 * half + j2 + 1)],
                                                         qall[:, 32 * s:32 * s + 32], start=(j2 == 0 and s == 0), stop=True,
                                                         skip_group_check=True)
                            i.then_inc(s_zs, 1)
                    if m == 1:
                        pe.wait_ge(s_spm, p + 1)
                        nc.tensor.matmul(Z[2][:, 0:256], negtri, SPs[:, 4, :], start=False, stop=True,
                                         skip_group_check=True).then_inc(s_cs, 1)
                        pe.wait_ge(s_sps, 3 * (p + 1))
                        for j in (3, 2, 1, 0):
                            bk = Z[j // 2][:, 256 * (j % 2):256 * (j % 2) + 256]
                            nc.tensor.matmul(bk, negtri, SPs[:, j, :], start=False, stop=True, skip_group_check=True)
                            if j < 3:
                                pe.wait_ge(s_Ss, 3 * p + 3 - j)
                            i = nc.tensor.matmul(bk, negones, SPs[:, 4, :] if j == 3 else SUs[:, 2 - j, :],
                                                 start=False, stop=True, skip_group_check=True)
                            if j % 2 == 0:
                                i.then_inc(s_cs, 1)
                    if m == 2:
                        pe.wait_ge(s_asm, p + 1)
                        nc.tensor.matmul(OB[:, 0:256], vs[:, :], Es[:, 4, :], start=True, stop=True)
                        pe.wait_ge(s_kv[1], 16 * (p + 1))
                        pe.wait_ge(s_as, 3 * (p + 1))
                        for j in (3, 2, 1, 0):
                            for s in range(STREAMS):
                                i = nc.tensor.matmul(OB[:, 32 * s:32 * s + 32], V_[:, s, j, :], Es[:, j, 32 * s:32 * s + 32],
                                                     start=False, stop=True, skip_group_check=True)
                        i.then_inc(s_os, 1)
                    if m >= 3:
                        c = m - 3
                        if c < NT:
                            u = 12 * p + x_use_tile(c)
                            pe.wait_ge(s_hke, 2 * (p + 1))
                            need(pe, s_kn, 9 * p + c)
                            if c >= 7:
                                pe.wait_ge(s_hl, 3 * p + 1)
                            nc.tensor.transpose(XB[:, 0:P], lf[:, c * P:(c + 1) * P], ident).then_inc(s_kt, 1)
                            pe.wait_ge(s_hqd, p + 1)
                            pe.wait_ge(s_hki, p + 1)
                            if c == 0:
                                pe.wait_ge(s_as, 3 * (p + 1))
                            need(pe, s_atm, 9 * p + c)
                            nc.tensor.matmul(Z[2][:, 0:P], kb[:, c * P:(c + 1) * P], hq[:, c * P:(c + 1) * P],
                                             start=True, stop=True).then_inc(s_at, 1)
                        mid = len(A_PIECES[m]) // 2
                        for x in A_PIECES[m][:mid]:
                            product(8 + 8 * p + x // 9, x // 3 % 3, x % 3)
                        if 1 <= c <= NT:
                            b = c - 1
                            pe.wait_ge(s_kn, 9 * p + b + 1)
                            pe.wait_ge(s_im, 9 * p + b + 1)
                            if b < 8:
                                if b >= 2:
                                    pe.wait_ge(s_ch, NBLK * p + 4 * (b - 1))
                                nc.tensor.matmul(Z[b % 2][:, :], kendN[b % 2][:, :],
                                                 imask[:, 4 * (b % 2):4 * (b % 2) + 4, :].rearrange("s b v -> s (b v)"),
                                                 start=True, stop=True).then_inc(s_KV, 1)
                            else:
                                pe.wait_ge(s_ch, NBLK * (p + 1))
                                for half in range(2):
                                    i = nc.tensor.matmul(Z[half][:, :], kendN[b % 2][:, :],
                                                         imask[:, 4 * half:4 * half + 4, :].rearrange("s b v -> s (b v)"),
                                                         start=True, stop=True)
                                i.then_inc(s_KV, 1)
                        for x in A_PIECES[m][mid:]:
                            product(8 + 8 * p + x // 9, x // 3 % 3, x % 3)
                        if 2 <= c <= NT + 1:
                            b = c - 2
                            if b == 0:
                                pe.wait_ge(s_gs, 2 * (p + 1))
                                pe.wait_ge(s_S0, p + 1)
                            if b in (4, 8):
                                pe.wait_ge(s_oc, 3 * p + b // 4)
                            pe.wait_ge(s_atm, 9 * p + b + 1)
                            o0 = P * (b % 4)
                            nc.tensor.matmul(OB[:, o0:o0 + P], i_nat[:, b * P:(b + 1) * P], attm[b % 2][:, :],
                                             start=True, stop=True)
                            if b < 8:
                                for s in range(4):
                                    nb = 4 * b + s
                                    if nb:
                                        pe.wait_ge(s_ch, NBLK * p + nb)
                                    i = nc.tensor.matmul(OB[:, o0 + BLK * s:o0 + BLK * s + BLK], St[nb % 8][:, :],
                                                         hq[:, nb * BLK:(nb + 1) * BLK], start=False, stop=True,
                                                         skip_group_check=True)
                            else:
                                pe.wait_ge(s_S0m, p + 1)
                                for s in range(STREAMS):
                                    i = nc.tensor.matmul(OB[:, o0 + DSEQ * s:o0 + DSEQ * s + DSEQ], S0s[:, s, :],
                                                         hq[:, SEQ + DSEQ * s:SEQ + DSEQ * s + DSEQ], start=False, stop=True,
                                                         skip_group_check=True)
                            i.then_inc(s_h3, 1)
                        if c in MS_STEP:
                            g = MS_STEP.index(c)
                            n = P * (GROUPS[g][1] - GROUPS[g][0])
                            pe.wait_ge(s_hs, 3 * p + g + 1)
                            pe.wait_ge(s_kn, 9 * p + (7 if g == 0 else 9))
                            if g:
                                pe.wait_ge(s_hl, 3 * p + g)
                            nc.tensor.matmul(XB[:, 0:n], negones, hsq[:, 0:n], start=True, stop=True).then_inc(s_hm, 1)
                    else:
                        for x in A_PIECES[m]:
                            product(8 + 8 * p + x // 9, x // 3 % 3, x % 3)
                    if p + 1 < PAIRS:
                        for w12 in late:
                            turn_attention(p + 1, w12)
                        late = ended(A_PIECES[m])
                if p + 1 < PAIRS:
                    for w12 in late:
                        turn_attention(p + 1, w12)

            recurrence_over(pe, PAIRS - 1)
            for g in range(36, 56):
                if not is_branch(g):
                    for w in range(NW):
                        for q in range(PIECES):
                            product(g, w, q)
                    continue
                dm = branch_of(g)
                pe.wait_ge(s_whi, g + 1)
                pe.wait_ge(s_wlo, g + 1)
                for w in range(NW):
                    n = 3 * dm + w
                    need(pe, s_mb, n - 1)
                    need(pe, s_ma, n - 1)
                    for half, bk in ((0, UA[n % 2]), (1, UB[n % 2])):
                        for m in range(12):
                            k, part = 4 * half + m // 3, m % 3
                            if g == 36 and w == 0 and part == 0:
                                pe.wait_ge(s_gh, k + 1)
                                pe.wait_ge(s_gl, k + 1)
                            weights = wl[g % 3] if part == 2 else wh[g % 2]
                            rows = gl if part == 1 else gh
                            i = nc.tensor.matmul(bk[:, 0:WIN], weights[:, k, :], rows[:, k, w * WIN:(w + 1) * WIN],
                                                 start=(m == 0), stop=(m == 11))
                    i.then_inc(s_u, 1)

            def y_square_sum(n):
                k, w = divmod(n, 3)
                pe.wait_ge(s_yq, n + 1)
                nc.tensor.matmul(Z[w][:, 0:WIN], no4[:, :], ysq[n % 3][:, :], start=(k == 0), stop=(k == KT_N - 1),
                                 skip_group_check=True).then_inc(s_yn, 1)

            pe.wait_ge(s_no, 1)
            for n in range(3 * KT_N):
                for q in range(PIECES):
                    product(56 + n // 3, n % 3, q)
                if n == 1:
                    pe.wait_ge(s_mb, 3 * KT_N)
                    pe.wait_ge(s_ma, 3 * KT_N)
                if n >= 1:
                    y_square_sum(n - 1)
            y_square_sum(3 * KT_N - 1)

        @block.scalar
        def _(act):
            def evacuate(n, dst, waits):
                for s, v in waits:
                    need(act, s, v)
                act.wait_ge(s_win, n + 1)
                nc.scalar.activation(dst, CH[n % 2][:, 0:WIN], ACT.Copy).then_inc(s_ev, 1)

            def tmp_free(idx):
                pair, r = divmod(idx - 2, 12)
                if idx < 2:
                    return
                half, r = divmod(r, 6)
                act.wait_ge(s_silu if r >= 3 else s_tr, 6 * pair + 3 * half + r % 3 + 1)

            def silu(n, idx, half, dst, waits):
                t = tmpT[idx % 2][:, :]
                tmp_free(idx)
                act.wait_ge(s_win, n + 1)
                nc.scalar.activation(t, CH[n % 2][:, 0:WIN], ACT.Exp, scale=-1.0).then_inc(s_ex, 1)
                evacuate(n, dst, waits)
                act.wait_ge(s_ex, half + 1)
                nc.scalar.activation(t, t, ACT.Ln, bias=1.0).then_inc(s_sg1, 1)
                act.wait_ge(s_sg1, half + 1)
                nc.scalar.activation(t, t, ACT.Exp, scale=-1.0).then_inc(s_sg, 1)

            def window_attention(pp, w12):
                c, w = divmod(w12, 3)
                n = win_of(8 * pp if pp else 0) + w12
                cols = slice(w * WIN, (w + 1) * WIN)
                copies = (s_cp, 5 * pp)
                if c == 0:
                    for s, v in ((s_qk, NS * pp), copies):
                        need(act, s, v)
                    act.wait_ge(s_win, n + 1)
                    nc.scalar.activation(qT[:, cols], CH[n % 2][:, 0:WIN], ACT.Copy, scale=DH ** -0.5).then_inc(s_ev, 1)
                elif c == 1:
                    evacuate(n, kT[:, cols], ((s_qk, NS * pp), copies, (s_kout, 16 * pp)))
                elif c == 2:
                    tmp_free(12 * pp + w)
                    evacuate(n, tmpT[(12 * pp + w) % 2][:, :], ())
                else:
                    silu(n, 12 * pp + 3 + w, 6 * pp + w, zA[:, cols], (copies, (s_spA, 32 * pp)))

            def window_recurrence(p, w12):
                c, w = divmod(w12, 3)
                n = win_of(4 + 8 * p) + w12
                cols = slice(w * WIN, (w + 1) * WIN)
                if c == 0:
                    evacuate(n, hq[:, cols], ((s_h3, NT * p),))
                elif c == 1:
                    need(act, s_at, NT * p)
                    need(act, s_hke, 2 * p)
                    act.wait_ge(s_win, n + 1)
                    nc.scalar.activation(kb[:, cols], CH[n % 2][:, 0:WIN], ACT.Exp).then_inc(s_ev, 1)
                elif c == 2:
                    tmp_free(12 * p + 6 + w)
                    evacuate(n, tmpT[(12 * p + 6 + w) % 2][:, :], ())
                else:
                    silu(n, 12 * p + 9 + w, 6 * p + 3 + w, zB[:, cols], ((s_spB, 16 * p),))

            def forget(p, w):
                k = kb[:, w * WIN:(w + 1) * WIN]
                act.wait_ge(s_ev, win_of(5 + 8 * p) + w + 1)
                nc.scalar.activation(k, k, ACT.Ln, bias=1.0).then_inc(s_f1, 1)
                act.wait_ge(s_f1, 3 * p + w + 1)
                nc.scalar.activation(k, k, ACT.Exp, scale=-1.0, bias=lbv[:, 4, p:p + 1]).then_inc(s_f, 1)
                act.wait_ge(s_f, 3 * p + w + 1)
                need(act, s_kt, NT * p)
                nc.scalar.activation(lf[:, w * WIN:(w + 1) * WIN], k, ACT.Ln, scale=-1.0, bias=1.0).then_inc(s_lf, 1)

            def window_gate(dm, kind, w):
                n = win_of(32 + 2 * dm + kind) + w if dm < 2 else GATE_W0 + 6 * (dm - 2) + 3 * kind + w
                dst = slots[dm] if kind == 0 else slots[gate_b_slot(dm)]
                if w == 0:
                    gate_slot_free(dm, kind)
                act.wait_ge(s_win, n + 1)
                nc.scalar.activation(dst[:, w * WIN:(w + 1) * WIN], CH[n % 2][:, 0:WIN], ACT.Exp, scale=-1.0,
                                     bias=ngate[:, 8 * kind + dm:8 * kind + dm + 1]).then_inc(s_ev, 1)
                s = dst[:, w * WIN:(w + 1) * WIN]
                act.wait_ge(s_ev, n + 1)
                nc.scalar.activation(s, s, ACT.Ln, bias=1.0).then_inc(s_g1, 1)
                act.wait_ge(s_g1, 6 * dm + 3 * kind + w + 1)
                nc.scalar.activation(s, s, ACT.Exp, scale=-1.0).then_inc(s_sig, 1)

            def gate_slot_free(dm, kind):
                if dm < 2:
                    act.wait_ge(s_qk, NS * PAIRS)
                    act.wait_ge(s_av, NS * PAIRS)
                    act.wait_ge(s_cp, 5 * PAIRS)
                    act.wait_ge(s_kout, 16 * PAIRS)
                    act.wait_ge(s_vout, 16 * PAIRS)
                    act.wait_ge(s_spA, 16 * (2 * PAIRS - 1))
                elif kind == 0:
                    act.wait_ge(s_gl, 8)
                    if dm == 7:
                        act.wait_ge(s_mg, 3 * 6)
                else:
                    act.wait_ge(s_mg, 3 * (dm - 1 if dm < 7 else 7))

            nc.scalar.preload_act_table_set("natural_log_exp_and_others")
            act.wait_ge(s_c, 32)
            act.wait_ge(s_lb, 3)
            nc.scalar.activation(lbv[:, 1:3, :], lbv[:, 1:3, :], ACT.Exp).then_inc(s_lbe, 1)
            act.wait_ge(s_lb, 6)
            nc.scalar.activation(lbv[:, 4, :], lbv[:, 4, :], ACT.Ln).then_inc(s_lbe, 1)
            act.wait_ge(s_lbe, 2)
            for w in range(NW):
                for k in range(KT_N):
                    n = KT_N * w + k
                    if k == 0:
                        act.wait_ge(s_x[w % 2], 16 * (w // 2 + 1))
                    need(act, s_xms, n - 3)
                    nc.scalar.activation(xsq[n % 4][:, :], xw[w % 2][:, k, :], ACT.Square).then_inc(s_xsq, 1)
                act.wait_ge(s_xms, KT_N * (w + 1))
                need(act, s_xn, KT_N * w)
                nc.scalar.activation(xrs[:, 0:WIN], Z[w][:, 0:WIN], ACT.Ln, scale=-1.0 / D, bias=eps_col).then_inc(s_xln, 1)
                act.wait_ge(s_xln, w + 1)
                nc.scalar.activation(xrs[:, 0:WIN], xrs[:, 0:WIN], ACT.Exp, scale=-0.5).then_inc(s_xrs, 1)
                for k in range(KT_N):
                    act.wait_ge(s_xn, KT_N * w + k + 1)
                    nc.scalar.activation(xh[:, k, w * WIN:(w + 1) * WIN], xw[w % 2][:, k, :], ACT.Copy).then_inc(s_xhi, 1)
            for w12 in range(12):
                window_attention(0, w12)

            for p in range(PAIRS):
                recurrence_over(act, p - 1)
                late = []
                for n in range(B_STEPS):
                    if n < NS:
                        c0, t = first_col(n), NS * p + n
                        act.wait_ge(s_qk, t + 1)
                        need(act, s_sp, t - 1)
                        nc.scalar.activation(E[n % 2][:, c0:QW], Z[n % 3][:, c0:QW], ACT.Exp).then_inc(s_E, 1)
                        act.wait_ge(s_E, t + 1)
                        nc.scalar.activation(E[n % 2][:, c0:QW], E[n % 2][:, c0:QW], ACT.Ln, bias=1.0).then_inc(s_L, 1)
                    if 1 <= n <= NS:
                        m = n - 1
                        c0, t = first_col(m), NS * p + m
                        act.wait_ge(s_cum, t + 1)
                        need(act, s_av, t - 1)
                        nc.scalar.activation(Aw[m % 2][:, c0:QW], Z[m % 3][:, c0:QW], ACT.Exp).then_inc(s_a, 1)
                    for c, w in late:
                        if c == 1:
                            forget(p, w)
                    late = []
                    for w12 in ended(B_PIECES[n]):
                        window_recurrence(p, w12)
                        late.append(divmod(w12, 3))
                attention_over(act, p)
                for m in range(A_STEPS):
                    if m == 0:
                        for r, (bk, lo, n) in enumerate(((Z[2], 4, 1), (Z[1], 2, 2), (Z[0], 0, 2))):
                            e = Es[:, lo:lo + n, :].rearrange("s j c -> s (j c)")
                            act.wait_ge(s_zs, 3 * p + r + 1)
                            nc.scalar.activation(e, bk[:, 0:256 * n], ACT.Exp).then_inc(s_Es, 1)
                            act.wait_ge(s_Es, 3 * p + r + 1)
                            nc.scalar.activation(e, e, ACT.Ln, bias=1.0).then_inc(s_Ls, 1)
                        act.wait_ge(s_ge, 2 * (p + 1))
                        nc.scalar.activation(gg[:, :], be[:, :], ACT.Exp).then_inc(s_EX, 1)
                        nc.scalar.activation(em[:, :], bm[:, NBLK:], ACT.Exp).then_inc(s_EX, 1)
                        act.wait_ge(s_A, 2 * (p + 1))
                        nc.scalar.activation(EK[:, :], lf[:, :], ACT.Exp, scale=-1.0).then_inc(s_EX, 1)
                        nc.scalar.activation(EQ[:, :], lf[:, :], ACT.Exp).then_inc(s_EX, 1)
                    if m == 1:
                        act.wait_ge(s_sps, 3 * (p + 1))
                        for r, (bk, lo, n) in enumerate(((Z[2], 4, 1), (Z[1], 2, 2), (Z[0], 0, 2))):
                            act.wait_ge(s_cs, 3 * p + r + 1)
                            nc.scalar.activation(Es[:, lo:lo + n, :].rearrange("s j c -> s (j c)"), bk[:, 0:256 * n],
                                                 ACT.Exp).then_inc(s_as, 1)
                    if m >= 3:
                        c = m - 3
                        if c < NT:
                            act.wait_ge(s_kt, NT * p + c + 1)
                            need(act, s_KV, NT * p + c - 1 if c >= 2 else 0)
                            nc.scalar.activation(kendN[c % 2][:, :], XB[:, 0:P], ACT.Copy).then_inc(s_kn, 1)
                        for g in range(3):
                            if c == MS_STEP[g]:
                                n = P * (GROUPS[g][1] - GROUPS[g][0])
                                act.wait_ge(s_hm, 3 * p + g + 1)
                                need(act, s_hg1, 3 * p + g)
                                nc.scalar.activation(hrs[:, 0:n], XB[:, 0:n], ACT.Ln, scale=-1.0 / P, bias=eps_col).then_inc(s_hl, 1)
                                act.wait_ge(s_hl, 3 * p + g + 1)
                                nc.scalar.activation(hrs[:, 0:n], hrs[:, 0:n], ACT.Exp, scale=-0.5).then_inc(s_hr, 1)
                        if c in (5, 9, 10):
                            g = (5, 9, 10).index(c)
                            n = P * (GROUPS[g][1] - GROUPS[g][0])
                            act.wait_ge(s_h3, NT * p + GROUPS[g][1])
                            need(act, s_hg, 3 * p + g)
                            nc.scalar.activation(oc[:, 0:n], OB[:, 0:n], ACT.Copy).then_inc(s_oc, 1)
                            act.wait_ge(s_oc, 3 * p + g + 1)
                            need(act, s_hm, 3 * p + g)
                            nc.scalar.activation(hsq[:, 0:n], oc[:, 0:n], ACT.Square).then_inc(s_hs, 1)
                    for w12 in ended(A_PIECES[m]):
                        if p + 1 < PAIRS:
                            window_attention(p + 1, w12)
                        else:
                            window_gate(w12 // 6, w12 // 3 % 2, w12 % 3)
            for kk in range(8):
                act.wait_ge(s_gr[kk % 5], 16 * (kk // 5 + 1))
                if kk == 0:
                    recurrence_over(act, PAIRS - 1)
                    act.wait_ge(s_os, PAIRS)
                    act.wait_ge(s_sso, 16 * PAIRS)
                    act.wait_ge(s_so, 16 * PAIRS)
                    act.wait_ge(s_hm, 3 * PAIRS)
                nc.scalar.activation(gh[:, kk, :], slots[2 + kk % 5][:, :], ACT.Copy).then_inc(s_gh, 1)
            for dm in range(2, 8):
                for kind in range(2):
                    for w in range(NW):
                        window_gate(dm, kind, w)
            act.wait_ge(s_win, OUT_W0)
            for dm in range(8):
                act.wait_ge(s_mg, 3 * dm + 3)
                nc.scalar.activation(xh[:, dm, :], slots[dm][:, :], ACT.Copy).then_inc(s_mh, 1)
            act.wait_ge(s_u, 24)
            for n in range(3 * KT_N):
                k, w = divmod(n, 3)
                act.wait_ge(s_win, OUT_W0 + n + 1)
                need(act, s_yn, n - 2)
                nc.scalar.activation(ysq[n % 3][:, :], CH[n % 2][:, 0:WIN], ACT.Square).then_inc(s_yq, 1)
                nc.scalar.activation(yb[:, k, w * WIN:(w + 1) * WIN], CH[n % 2][:, 0:WIN], ACT.Copy).then_inc(s_ev, 1)
            for w in range(NW):
                act.wait_ge(s_yn, 3 * (KT_N - 1) + w + 1)
                nc.scalar.activation(yrs[w][:, :], Z[w][:, 0:WIN], ACT.Ln, scale=-1.0 / D, bias=eps_col).then_inc(s_yl, 1)
                act.wait_ge(s_yl, w + 1)
                nc.scalar.activation(yrs[w][:, :], yrs[w][:, :], ACT.Exp, scale=-0.5).then_inc(s_yr, 1)

        @block.vector
        def _(dve):
            V = nc.vector

            def split_weights(g):
                dve.wait_ge(s_raw[g % 3], 16 * (g // 3 + 1))
                chunk_done(dve, g - 2)
                V.tensor_copy(wh[g % 2][:, :, :], wr[g % 3][:, :, :]).then_inc(s_whi, 1)
                dve.wait_ge(s_whi, g + 1)
                V.tensor_tensor(wl[g % 3][:, :, :], wr[g % 3][:, :, :], wh[g % 2][:, :, :].bitcast(F32),
                                ALU.subtract).then_inc(s_wlo, 1)

            def turned(idx, dst, waits):
                for s, v in waits:
                    need(dve, s, v)
                dve.wait_ge(s_tr, idx + 1)
                V.tensor_copy(dst, TB[:, 0:WIN]).then_inc(s_te, 1)

            def window_attention(pp, w12):
                c, w = divmod(w12, 3)
                if w == 0:
                    split_weights((8 * pp if pp else 0) + c + 1)

            def turn_attention(pp, w12):
                c, w = divmod(w12, 3)
                if c == 2:
                    turned(6 * pp + w, v_nat[:, w * WIN:(w + 1) * WIN], ((s_av, NS * pp), (s_vout, 16 * pp), (s_cp, 5 * pp)))

            def window_recurrence(p, w12):
                c, w = divmod(w12, 3)
                if w == 0:
                    split_weights(4 + 8 * p + c + 1)

            def turn_recurrence(p, w12):
                c, w = divmod(w12, 3)
                if c == 2:
                    turned(6 * p + 3 + w, i_nat[:, w * WIN:(w + 1) * WIN], ((s_h3, NT * p), (s_im, NT * p)))

            dve.wait_ge(s_c, 32)
            V.memset(qbd[:, :, :, :], 0.0).then_inc(s_qz, 1)
            V.tensor_scalar(ngate[:, :], bgate, -1.0, None, ALU.mult)
            V.tensor_tensor(lbv[:, 0, :], lbraw[:, 0:4], lbraw[:, 4:8], ALU.max).then_inc(s_lb, 1)
            dve.wait_ge(s_lb, 1)
            for r in range(2):
                V.tensor_tensor(lbv[:, 1 + r, :], lbraw[:, 4 * r:4 * r + 4], lbv[:, 0, :], ALU.subtract).then_inc(s_lb, 1)
            dve.wait_ge(s_lbe, 1)
            V.tensor_tensor(lbv[:, 3, :], lbv[:, 1, :], lbv[:, 2, :], ALU.add).then_inc(s_lb, 1)
            dve.wait_ge(s_lb, 4)
            V.reciprocal(lbv[:, 3, :], lbv[:, 3, :]).then_inc(s_lb, 1)
            dve.wait_ge(s_lb, 5)
            V.tensor_tensor(lbv[:, 4, :], lbv[:, 2, :], lbv[:, 3, :], ALU.mult).then_inc(s_lb, 1)
            split_weights(0)
            for w in range(NW):
                def low(k):
                    dve.wait_ge(s_xhi, KT_N * w + k + 1)
                    cols = slice(w * WIN, (w + 1) * WIN)
                    V.tensor_tensor(xl[:, k, cols], xw[w % 2][:, k, :], xh[:, k, cols].bitcast(F32), ALU.subtract).then_inc(s_xlo, 1)

                dve.wait_ge(s_xrs, w + 1)
                for k in range(KT_N):
                    V.scalar_tensor_tensor(xw[w % 2][:, k, :], xw[w % 2][:, k, :], gpre[:, k:k + 1], xrs[:, 0:WIN],
                                           ALU.mult, ALU.mult).then_inc(s_xn, 1)
                    if k:
                        low(k - 1)
                low(KT_N - 1)
            for w12 in range(12):
                window_attention(0, w12)
                if w12:
                    turn_attention(0, w12 - 1)
            turn_attention(0, 11)

            for p in range(PAIRS):
                recurrence_over(dve, p - 1)
                late = []
                for n in range(B_STEPS):
                    if n < NS:
                        c0, t = first_col(n), NS * p + n
                        dve.wait_ge(s_L, t + 1)
                        need(dve, s_cum, t - 2)
                        need(dve, s_S, SUMS * p + (sums_until(n - 3) if n >= 3 else 0))
                        i = V.scalar_tensor_tensor(SPb[n % 3][:, c0:QW], E[n % 2][:, c0:QW], 88.0, Z[n % 3][:, c0:QW],
                                                   ALU.min, ALU.max)
                        if diagonal(n):
                            i.then_inc(s_sp1, 1)
                            dve.wait_ge(s_sp1, DIAGS * p + diagonals_until(n))
                            V.tensor_tensor(SPb[n % 3][:, c0:c0 + P], SPb[n % 3][:, c0:c0 + P], causal, ALU.mult).then_inc(s_sp, 1)
                        else:
                            i.then_inc(s_sp, 1)
                    if n >= 2:
                        wd, j, h = STEPS[n - 2]
                        if j == 0 and h == 1:
                            dve.wait_ge(s_silu, 6 * p + 3)
                            dve.wait_ge(s_av, NS * p + n - 1)
                            V.tensor_tensor(zA[:, wd * QW:(wd + 1) * QW], OB[:, :], zA[:, wd * QW:(wd + 1) * QW],
                                            ALU.mult).then_inc(s_gA, 1)
                    if n == 12:
                        dve.wait_ge(s_te, 6 * p + 3)
                        dve.wait_ge(s_silu, 6 * p + 3)
                        dve.wait_ge(s_ev, win_of(8 * p if p else 0) + 12)
                        need(dve, s_zs, 3 * p)
                        need(dve, s_os, p)
                        need(dve, s_spA, 32 * p)
                        dve.wait_ge(s_qz, 1)
                        for h in range(2):
                            r = slice(DH * h, DH * h + DH)
                            V.tensor_copy(qbd[r, :, h, :], qT[r, SEQ:TOK].rearrange("d (i t) -> d i t", t=DSEQ)).then_inc(s_cp, 1)
                        V.tensor_copy(kTs[:, :], kT[:, SEQ:TOK]).then_inc(s_cp, 1)
                        V.tensor_copy(vs[:, :], v_nat[:, SEQ:TOK]).then_inc(s_cp, 1)
                        V.tensor_copy(zAs[:, :], zA[:, SEQ:TOK]).then_inc(s_cp, 1)
                    for w12 in late:
                        turn_recurrence(p, w12)
                    late = ended(B_PIECES[n])
                    for w12 in late:
                        window_recurrence(p, w12)
                for w12 in late:
                    turn_recurrence(p, w12)

                attention_over(dve, p)
                late = []
                for m in range(A_STEPS):
                    if m == 0:
                        dve.wait_ge(s_zs, 3 * (p + 1))
                        need(dve, s_so, 16 * p)
                        V.memset(St[0][:, :], 0.0).then_inc(s_S0, 1)
                        dve.wait_ge(s_lf, 3 * (p + 1))
                        for c in range(NT):
                            cols = slice(c * P, (c + 1) * P)
                            V.tensor_tensor_scan(lf[:, cols], reset if c < 8 else reset_s, lf[:, cols], 0.0,
                                                 ALU.mult, ALU.add).then_inc(s_scan, 1)
                        dve.wait_ge(s_scan, NT * (p + 1))
                        bp = lf[:, 0:SEQ].rearrange("c (n t) -> c n t", t=BLK)
                        bs = lf[:, SEQ:TOK].rearrange("c (n t) -> c n t", t=DSEQ)
                        V.tensor_copy(bm[:, 0:NBLK], bp[:, :, BLK // 2 - 1]).then_inc(s_bmc, 1)
                        V.tensor_copy(bm[:, NBLK:], bs[:, :, DSEQ // 2 - 1]).then_inc(s_bmc, 1)
                        V.tensor_copy(be[:, 0:NBLK], bp[:, :, BLK - 1]).then_inc(s_bmc, 1)
                        V.tensor_copy(be[:, NBLK:], bs[:, :, DSEQ - 1]).then_inc(s_bmc, 1)
                        dve.wait_ge(s_bmc, 4 * (p + 1))
                        V.tensor_tensor(bp, bp, bm[:, 0:NBLK, None].broadcast_to([P, NBLK, BLK]), ALU.subtract).then_inc(s_A, 1)
                        V.tensor_tensor(bs, bs, bm[:, NBLK:, None].broadcast_to([P, STREAMS, DSEQ]), ALU.subtract).then_inc(s_A, 1)
                        V.tensor_tensor(be[:, :], be[:, :], bm[:, :], ALU.subtract).then_inc(s_ge, 1)
                        dve.wait_ge(s_ge, 2 * p + 1)
                        V.tensor_tensor(be[:, 0:NBLK - 1], be[:, 0:NBLK - 1], bm[:, 1:NBLK], ALU.add).then_inc(s_ge, 1)
                        for r, (bk, lo, n) in enumerate(((Z[2], 4, 1), (Z[1], 2, 2), (Z[0], 0, 2))):
                            dve.wait_ge(s_Ls, 3 * p + r + 1)
                            V.scalar_tensor_tensor(SPs[:, lo:lo + n, :].rearrange("s j c -> s (j c)"),
                                                   Es[:, lo:lo + n, :].rearrange("s j c -> s (j c)"), 88.0, bk[:, 0:256 * n],
                                                   ALU.min, ALU.max).then_inc(s_sps, 1)
                            if r == 0:
                                dve.wait_ge(s_sps, 3 * p + 1)
                                V.tensor_tensor(SPs[:, 4, :], SPs[:, 4, :], smask, ALU.mult).then_inc(s_spm, 1)
                    if m == 1:
                        dve.wait_ge(s_as, 3 * p + 1)
                        V.tensor_tensor(Es[:, 4, :], Es[:, 4, :], smask, ALU.mult).then_inc(s_asm, 1)
                        dve.wait_ge(s_EX, 4 * (p + 1))
                        V.tensor_tensor(kb[:, :], kb[:, :], EK[:, :], ALU.mult).then_inc(s_hki, 1)
                        dve.wait_ge(s_hki, p + 1)
                        V.tensor_tensor(lf[:, 0:SEQ].rearrange("c (n t) -> c n t", t=BLK), kb[:, 0:SEQ].rearrange("c (n t) -> c n t", t=BLK),
                                        gg[:, 0:NBLK, None].broadcast_to([P, NBLK, BLK]), ALU.mult).then_inc(s_hke, 1)
                        V.tensor_tensor(lf[:, SEQ:TOK].rearrange("c (n t) -> c n t", t=DSEQ), kb[:, SEQ:TOK].rearrange("c (n t) -> c n t", t=DSEQ),
                                        gg[:, NBLK:, None].broadcast_to([P, STREAMS, DSEQ]), ALU.mult).then_inc(s_hke, 1)
                    if m == 2:
                        dve.wait_ge(s_os, p + 1)
                        dve.wait_ge(s_cp, 5 * (p + 1))
                        ob = OB[:, 0:256].rearrange("d (i h t) -> d i h t", h=2, t=DSEQ)
                        for h in range(2):
                            r = slice(DH * h, DH * h + DH)
                            z = zAs[r, :].rearrange("d (i t) -> d i t", t=DSEQ)
                            V.tensor_tensor(z, ob[r, :, h, :], z, ALU.mult).then_inc(s_gs, 1)
                        dve.wait_ge(s_S0l, 16 * (p + 1))
                        V.tensor_tensor(S0s[:, :, :], S0s[:, :, :], em[:, :, None].broadcast_to([P, STREAMS, P]), ALU.mult).then_inc(s_S0m, 1)
                    if m >= 3:
                        c = m - 3
                        if c < NT:
                            dve.wait_ge(s_at, NT * p + c + 1)
                            if c >= 2:
                                dve.wait_ge(s_h3, NT * p + c - 1)
                            V.scalar_tensor_tensor(attm[c % 2][:, :], Z[2][:, 0:P], BIG, hgmask if c < 8 else hgmask_s,
                                                   ALU.min, ALU.mult).then_inc(s_atm, 1)
                        if 1 <= c <= 8:
                            b = c - 1
                            dve.wait_ge(s_KV, NT * p + b + 1)
                            if b == 0:
                                dve.wait_ge(s_S0, p + 1)
                            for s in range(4):
                                n = 4 * b + s
                                need(dve, s_ch, NBLK * p + n)
                                if n >= 7:
                                    dve.wait_ge(s_h3, NT * p + (n - 7) // 4 + 1)
                                V.scalar_tensor_tensor(St[(n + 1) % 8][:, :], St[n % 8][:, :], gg[:, n:n + 1],
                                                       Z[b % 2][:, s * P:(s + 1) * P], ALU.mult, ALU.add).then_inc(s_ch, 1)
                        if c in MS_STEP:
                            g = MS_STEP.index(c)
                            t0, t1 = GROUPS[g]
                            n = P * (t1 - t0)
                            dve.wait_ge(s_hr, 3 * p + g + 1)
                            V.tensor_tensor(oc[:, 0:n], oc[:, 0:n], hrs[:, 0:n], ALU.mult).then_inc(s_hg1, 1)
                            dve.wait_ge(s_hg1, 3 * p + g + 1)
                            dve.wait_ge(s_silu, 6 * p + 6)
                            V.scalar_tensor_tensor(zB[:, t0 * P:t1 * P], oc[:, 0:n], hgn[:, p:p + 1], zB[:, t0 * P:t1 * P],
                                                   ALU.mult, ALU.mult).then_inc(s_hg, 1)
                        if c == NT + 2:
                            dve.wait_ge(s_h3, NT * (p + 1))
                            V.tensor_tensor(S0s[:, :, :], S0s[:, :, :], gg[:, NBLK:, None].broadcast_to([P, STREAMS, P]),
                                            ALU.mult).then_inc(s_ss1, 1)
                            dve.wait_ge(s_ss1, p + 1)
                            dve.wait_ge(s_KV, NT * (p + 1))
                            for half in range(2):
                                s = S0s[:, 4 * half:4 * half + 4, :].rearrange("c i v -> c (i v)")
                                V.tensor_tensor(s, Z[half][:, :], s, ALU.add).then_inc(s_ss, 1)
                    if p + 1 < PAIRS:
                        for w12 in late:
                            turn_attention(p + 1, w12)
                        late = ended(A_PIECES[m])
                        for w12 in late:
                            window_attention(p + 1, w12)
                    else:
                        for w12 in ended(A_PIECES[m]):
                            if w12 % 3 == 0:
                                split_weights(32 + w12 // 3 + 1)
                if p + 1 < PAIRS:
                    for w12 in late:
                        turn_attention(p + 1, w12)

            def products(dm, w):
                n = 3 * dm + w
                cols = slice(w * WIN, (w + 1) * WIN)
                dve.wait_ge(s_u, n + 1)
                dve.wait_ge(s_sig, 6 * dm + 3 + w + 1)
                a, b = slots[dm][:, cols], slots[gate_b_slot(dm)][:, cols]
                V.tensor_tensor(a, UA[n % 2][:, 0:WIN], a, ALU.mult).then_inc(s_ma, 1)
                V.tensor_tensor(b, UB[n % 2][:, 0:WIN], b, ALU.mult).then_inc(s_mb, 1)

            def merged_low(dm):
                dve.wait_ge(s_mh, dm + 1)
                V.tensor_tensor(xl[:, dm, :], slots[dm][:, :], xh[:, dm, :].bitcast(F32), ALU.subtract).then_inc(s_ml, 1)

            for kk in range(8):
                dve.wait_ge(s_gh, kk + 1)
                V.tensor_tensor(gl[:, kk, :], slots[2 + kk % 5][:, :], gh[:, kk, :].bitcast(F32), ALU.subtract).then_inc(s_gl, 1)
            for g in range(36, 56):
                dm = branch_of(g) if is_branch(g) else (g - 38) // 3 + 2
                for w in range(NW):
                    if is_branch(g):
                        products(dm, w)
                        if dm == 7:
                            merged_low(2 * w)
                            merged_low(2 * w + 1)
                    if w == 0:
                        split_weights(g + 1)
            for dm in (6, 7):
                merged_low(dm)
            dve.wait_ge(s_u, 24)
            V.memset(no4[:, :], -1.0).then_inc(s_no, 1)
            for n in range(3 * KT_N):
                if n % 3 == 0 and n // 3 + 57 < 64:
                    dve.wait_ge(s_win, OUT_W0 + n + 1)
                    split_weights(57 + n // 3)
            for w in range(NW):
                dve.wait_ge(s_yr, w + 1)
                for k in range(KT_N):
                    s = yb[:, k, w * WIN:(w + 1) * WIN]
                    V.scalar_tensor_tensor(s, s, gpost[:, k:k + 1], yrs[w][:, :], ALU.mult, ALU.mult).then_inc(s_yg, 1)

        @block.gpsimd
        def _(pool):
            G = nc.gpsimd

            def silu_product(n, idx, half, z):
                pool.wait_ge(s_sg, half + 1)
                pool.wait_ge(s_ev, n + 1)
                G.tensor_tensor(z, z, tmpT[idx % 2][:, :], ALU.mult).then_inc(s_silu, 1)

            def window_attention(pp, w12):
                c, w = divmod(w12, 3)
                if c == 3:
                    silu_product(win_of(8 * pp if pp else 0) + w12, 12 * pp + 3 + w, 6 * pp + w, zA[:, w * WIN:(w + 1) * WIN])

            def window_recurrence(p, w12):
                c, w = divmod(w12, 3)
                if c == 3:
                    silu_product(win_of(4 + 8 * p) + w12, 12 * p + 9 + w, 6 * p + 3 + w, zB[:, w * WIN:(w + 1) * WIN])

            for w12 in range(12):
                window_attention(0, w12)
            for p in range(PAIRS):
                recurrence_over(pool, p - 1)
                for n in range(B_STEPS):
                    if n < NS and STEPS[n][1] > 0:
                        wd, j, h = STEPS[n]
                        c0, t, q = first_col(n), NS * p + n, 4 * wd + 3 - STEPS[n][1]
                        src, dst, last = SPb[n % 3], SUM[h][(q + 1) % 2], SUM[h][q % 2]
                        pool.wait_ge(s_sp, t + 1)
                        need(pool, s_cum, t - 1)
                        if q == 0:
                            G.tensor_copy(dst[:, c0:QW], src[:, c0:QW]).then_inc(s_S, 1)
                        else:
                            pool.wait_ge(s_S, SUMS * p + sums_until(n - 2))
                            lo = first_col(n - 2)
                            if lo > c0:
                                G.tensor_copy(dst[:, c0:lo], src[:, c0:lo])
                            G.tensor_tensor(dst[:, lo:QW], last[:, lo:QW], src[:, lo:QW], ALU.add).then_inc(s_S, 1)
                    if 1 <= n <= NS and diagonal(n - 1):
                        m = n - 1
                        c0 = first_col(m)
                        pool.wait_ge(s_a, NS * p + m + 1)
                        G.tensor_tensor(Aw[m % 2][:, c0:c0 + P], Aw[m % 2][:, c0:c0 + P], causal, ALU.mult).then_inc(s_am, 1)
                    for w12 in ended(B_PIECES[n]):
                        window_recurrence(p, w12)
                attention_over(pool, p)
                for m in range(A_STEPS):
                    if m == 0:
                        pool.wait_ge(s_spm, p + 1)
                        for q, j in enumerate((3, 2, 1)):
                            if q == 0:
                                pool.wait_ge(s_sps, 3 * p + 2)
                                last = SPs[:, 4, :]
                            else:
                                pool.wait_ge(s_sps, 3 * p + (2 if j >= 2 else 3))
                                pool.wait_ge(s_Ss, 3 * p + q)
                                last = SUs[:, q - 1, :]
                            G.tensor_tensor(SUs[:, q, :], last, SPs[:, j, :], ALU.add).then_inc(s_Ss, 1)
                    if m == 1:
                        pool.wait_ge(s_EX, 4 * (p + 1))
                        G.tensor_tensor(hq[:, :], hq[:, :], EQ[:, :], ALU.mult).then_inc(s_hqd, 1)
                    if 2 <= m < NT + 2:
                        c = m - 2
                        blocks, rows = (4, rows4) if c < 8 else (8, rows8)
                        if c == 0:
                            pool.wait_ge(s_te, 6 * (p + 1))
                            pool.wait_ge(s_zs, 3 * (p + 1))
                        if c >= 2:
                            pool.wait_ge(s_KV, NT * p + (c - 1 if c < 8 else 8))
                        b0 = 4 * (c % 2)
                        G.tensor_tensor(imask[:, b0:b0 + blocks, :],
                                        i_nat[:, None, c * P:(c + 1) * P].broadcast_to([P, blocks, P]),
                                        rows[:, :, None].broadcast_to([P, blocks, P]), ALU.mult).then_inc(s_im, 1)
                    if p + 1 < PAIRS:
                        for w12 in ended(A_PIECES[m]):
                            window_attention(p + 1, w12)
            for dm in range(8):
                for w in range(NW):
                    cols = slice(w * WIN, (w + 1) * WIN)
                    pool.wait_ge(s_mb, 3 * dm + w + 1)
                    pool.wait_ge(s_ma, 3 * dm + w + 1)
                    G.tensor_tensor(slots[dm][:, cols], slots[dm][:, cols], slots[gate_b_slot(dm)][:, cols], ALU.add).then_inc(s_mg, 1)
            pool.wait_ge(s_xr, 16)
            for w in range(NW):
                for k in range(KT_N):
                    cols = slice(w * WIN, (w + 1) * WIN)
                    pool.wait_ge(s_yg, KT_N * w + k + 1)
                    G.tensor_tensor(yb[:, k, cols], yb[:, k, cols], xres[:, k, cols], ALU.add).then_inc(s_yo, 1)


def constants():
    c2 = np.zeros((P, C2_W), np.float32)
    s, t = np.arange(P)[:, None], np.arange(P)[None, :]

    def put(name, value):
        o, n = C2[name]
        c2[:, o:o + n] = value

    put("negtri", -(s >= t).astype(np.float32))
    put("negones", -1.0)
    put("causal", s < t)
    put("hgmask", (s <= t) & (s // BLK == t // BLK))
    put("hgmask_s", (s <= t) & (s // DSEQ == t // DSEQ))
    col = np.arange(256)[None, :]
    put("smask", (s // DSEQ == col // 32) & (s % DSEQ < col % DSEQ))
    put("reset", np.broadcast_to(t % BLK != 0, (P, P)))
    put("reset_s", np.broadcast_to(t % DSEQ != 0, (P, P)))
    put("rows4", s // BLK == np.arange(4)[None, :])
    put("rows8", s // DSEQ == np.arange(8)[None, :])
    return c2


def chunk_weights(w_in, wa, wb, w_out):
    def cols(m, c):
        return m[:, c * P:(c + 1) * P].reshape(KT_N, P, P).transpose(1, 0, 2).reshape(P, KT_N * P)

    def w_in_chunk(group, p):
        return cols(w_in, 4 * group + p)

    out = []

    def attention(p):
        out.extend(w_in_chunk(g, p) for g in (0, 1, 2, 3))

    def gates(dm):
        out.extend((cols(w_in, 32 + dm), cols(w_in, 40 + dm)))

    branches = np.concatenate([wa, wb], axis=0)
    attention(0)
    for p in range(PAIRS):
        out.extend(w_in_chunk(g, p) for g in (4, 5, 6, 7))
        if p + 1 < PAIRS:
            attention(p + 1)
        else:
            gates(0)
            gates(1)
    for dm in range(8):
        if dm >= 2:
            gates(dm)
        out.append(cols(branches, dm))
    out.extend(cols(w_out, n) for n in range(8))
    return np.ascontiguousarray(np.stack(out))


def kernel(x_prompt, x_sample, cache_sb_k, cache_sb_v, state_hgrn, g_pre, w_in, b_gate, hg_lb_raw, hg_norm_g,
           w_branch_a, w_branch_b, w_out, g_post):
    import concourse.bacc as bacc
    from concourse.bass_utils import run_bass_kernel_spmd

    x = np.concatenate([np.asarray(x_prompt)[0], np.asarray(x_sample).reshape(-1, D)], axis=0)
    c1 = np.zeros((P, C1_W), np.float32)
    for name, value in (("ident", np.eye(P, dtype=np.float32)), ("bgate", np.asarray(b_gate)[0].reshape(16, P).T),
                        ("lbraw", np.asarray(hg_lb_raw).reshape(8, P).T), ("hgn", np.asarray(hg_norm_g)[0].T),
                        ("gpre", np.asarray(g_pre)[0].reshape(8, P).T), ("gpost", np.asarray(g_post)[0].reshape(8, P).T),
                        ("eps", np.float32(EPS))):
        o, n = C1[name]
        c1[:, o:o + n] = value
    ck = np.asarray(cache_sb_k)[0].reshape(STREAMS, PAST, PAIRS, P)
    cv = np.asarray(cache_sb_v)[0].reshape(STREAMS, PAST // P, P, PAIRS, P)
    arrays = {
        "xT": x.reshape(TOK, KT_N, P).transpose(2, 1, 0),
        "wch": chunk_weights(np.asarray(w_in)[0], np.asarray(w_branch_a)[0], np.asarray(w_branch_b)[0], np.asarray(w_out)[0]),
        "ckT": ck.transpose(2, 0, 3, 1),
        "cv": cv.transpose(3, 0, 2, 1, 4).reshape(PAIRS, STREAMS, P, 4 * P),
        "st": np.asarray(state_hgrn)[0].transpose(1, 0, 2, 3),
        "c1": c1,
        "c2": constants(),
    }
    arrays = {k: np.ascontiguousarray(v) for k, v in arrays.items()}
    outs = {"yT": (P, KT_N, TOK), "okT": (PAIRS, P, TOK), "ov": (PAIRS, TOK, P), "osp": (PAIRS, P, P),
            "oss": (PAIRS, STREAMS, P, P)}
    nc = bacc.Bacc("TRN2", target_bir_lowering=False, num_devices=1)
    args = [nc.dram_tensor(k, v.shape, F32, kind="ExternalInput").ap() for k, v in arrays.items()]
    args += [nc.dram_tensor(k, s, F32, kind="ExternalOutput").ap() for k, s in outs.items()]
    spill = nc.dram_tensor("gated", (2 * PAIRS, P, TOK), F32, kind="Internal").ap()
    build(nc, *args, spill)
    r = run_bass_kernel_spmd(nc, [arrays], core_ids=[0]).results[0]
    y = np.asarray(r["yT"]).transpose(2, 1, 0).reshape(TOK, D)
    k = np.asarray(r["okT"]).transpose(2, 0, 1).reshape(TOK, 8, DH)
    v = np.asarray(r["ov"]).transpose(1, 0, 2).reshape(TOK, 8, DH)
    c = np.ascontiguousarray
    return (c(y[None, :SEQ]), c(y[SEQ:].reshape(STREAMS, DSEQ, D)),
            c(k[None, None, :SEQ]), c(v[None, None, :SEQ]), c(np.asarray(r["osp"])[None, None]),
            c(k[SEQ:].reshape(1, STREAMS, DSEQ, 8, DH)), c(v[SEQ:].reshape(1, STREAMS, DSEQ, 8, DH)),
            c(np.asarray(r["oss"]).transpose(1, 0, 2, 3)[None]))
```

```python
from contextlib import ExitStack

import numpy as np

import concourse.bass as bass
from concourse import mybir

F32 = mybir.dt.float32
F32R = mybir.dt.float32r
ALU = mybir.AluOpType
ACT = mybir.ActivationFunctionType

P = 128
D = 1024
SEQ, STREAMS, DSEQ, PAST = 1024, 8, 16, 512
TOK = SEQ + STREAMS * DSEQ
WIN = 384
NW = TOK // WIN
KT_N = D // P
PAIRS = 4
DH = 64
QW = 512
NS = 24
PIECES = 3
EPS = 1e-6
BIG = 3.0e38
BLK = 32
NBLK = SEQ // BLK
NT = TOK // P

GATE_G0 = 4 * 2 * PAIRS
OUT_G0 = GATE_G0 + 3 * 8
OUT_W0 = 3 * (GATE_G0 + 2 * 8)

C1 = {"ident": (0, 128), "bgate": (128, 16), "lbraw": (144, 8), "hgn": (152, 4), "gpre": (156, 8), "gpost": (164, 8),
      "eps": (172, 1)}
C1_W = 173
C2 = {"negtri": (0, 128), "negones": (128, 128), "causal": (256, 128), "hgmask": (384, 128), "hgmask_s": (512, 128),
      "smask": (640, 256), "reset": (896, 128), "reset_s": (1024, 128), "rows4": (1152, 4), "rows8": (1156, 8)}
C2_W = 1164


def attention_steps():
    return [(wd, j, h) for wd in range(SEQ // QW) for j in range(4 * wd + 3, -1, -1) for h in range(2)]


STEPS = attention_steps()
assert len(STEPS) == NS


def diagonal(n):
    wd, j, _ = STEPS[n]
    return j >= 4 * wd


def first_col(n):
    wd, j, _ = STEPS[n]
    return P * max(j - 4 * wd, 0)


def diagonals_until(n):
    return sum(diagonal(i) for i in range(n + 1))


DIAGS = diagonals_until(NS - 1)


def sums_until(n):
    return sum(STEPS[i][1] > 0 for i in range(n + 1))


SUMS = sums_until(NS - 1)


def spread(weights, total):
    out, acc, done = [], 0.0, 0
    for w in weights:
        acc += w
        upto = int(round(total * acc / sum(weights)))
        out.append(list(range(done, upto)))
        done = upto
    return out


B_STEPS = NS + 2
B_PIECES = spread([max(QW - first_col(n), 200) if n < NS else 300 for n in range(B_STEPS)], 12 * PIECES)
A_STEPS = 3 + NT + 3
A_PIECES = spread([4, 4, 4] + [2] * (A_STEPS - 3), 12 * PIECES)


def ended(pieces):
    return [x // PIECES for x in pieces if x % PIECES == PIECES - 1]


MERGE = [("gate", dm, kind) for dm in range(3) for kind in range(2)] + [("branch", dm, 0) for dm in range(3)]
for _dm in range(3, 8):
    MERGE += [("gate", _dm, 0), ("gate", _dm, 1), ("branch", _dm, 0)]


def gate_window_no(dm, kind, w):
    return 3 * GATE_G0 + 6 * dm + 3 * kind + w


def win_of(g):
    if g < GATE_G0:
        return 3 * g
    if g >= OUT_G0:
        return OUT_W0 + 3 * (g - OUT_G0)
    what, dm, kind = MERGE[g - GATE_G0]
    assert what == "gate"
    return gate_window_no(dm, kind, 0)


GATE_B_SLOT = (8, 7, 6, 8, 7, 8, 7, 8)


def slot_user_before(dm, kind):
    slot = dm if kind == 0 else GATE_B_SLOT[dm]
    return max([d for d in range(dm) if GATE_B_SLOT[d] == slot], default=-1)


ROW_OF = (4, 5, 6, 3, 0, 1, 2, 7)


def prologue_window(i):
    return (i % 2, i // 2) if i < 6 else (i // 3, i % 3)


def rows_until(n):
    return sum(tile_rank(i) > 0 for i in range(n + 1))


def tile_rank(n):
    wd, j, _ = STEPS[n]
    return 4 * wd + 3 - j


def sum_rows_until(n):
    return sum(tile_rank(i) > 1 for i in range(n + 1))


SPLITS, SUM_SPLITS = rows_until(NS - 1), sum_rows_until(NS - 1)


def x_use_tile(c):
    return c if c <= 6 else c + 1


X_USE_MS = (7, 10, 11)
STACK_STEPS = (9, 10, 11)
MS_STEP = (6, 10, 11)
GROUPS = ((0, 4), (4, 8), (8, 9))


def build(nc, xT, wch, ckT, cv, st, c1, c2, yT, okT, ov, osp, oss, spill):
    with ExitStack() as ctx:
        off = [0]
        base = nc.sbuf_base + (-nc.sbuf_base) % 32
        arena = ctx.enter_context(nc.sbuf_tensor("arena", [P, (nc.sbuf_usable_end - base) // 4 - 16], F32))
        limit = (nc.sbuf_usable_end - base) - 64

        def at(name, shape, dt, offset):
            size = 4 * int(np.prod(shape[1:]))
            assert offset + size <= limit, (name, offset + size, limit)
            return nc.alloc_sbuf_tensor_at(name, shape, dt, offset=base + offset)

        def take(name, shape, dt=F32):
            o = off[0]
            off[0] += 4 * int(np.prod(shape[1:]))
            off[0] += (-off[0]) % 32
            return at(name, shape, dt, o), o

        def sem(name):
            return ctx.enter_context(nc.semaphore(name))

        xh, _ = take("xh", [P, KT_N, TOK], F32R)
        xl, _ = take("xl", [P, KT_N, TOK], F32R)
        wr, wl, wh = [], [], []
        for i in range(3):
            t, o = take(f"wr{i}", [P, KT_N, P])
            wr.append(t)
            wl.append(at(f"wl{i}", [P, KT_N, P], F32R, o))
        for i in range(2):
            wh.append(take(f"wh{i}", [P, KT_N, P], F32R)[0])
        k1, _ = take("k1", [P, C1_W])
        lbv, _ = take("lbv", [P, 5, 4])
        ngate, _ = take("ngate", [P, 16])
        slot_order = (0, 1, 7, 8, 2, 3, 4, 5, 6)
        stage, slots = [], {}
        for name, m in zip(("qT", "kT", "zA", "v_nat", "hq", "kb", "lf", "i_nat", "zB"), slot_order):
            t, o = take(name, [P, TOK])
            stage.append(t)
            slots[m] = at(f"slot{m}", [P, TOK], F32, o)
            if m == 0:
                slots_base = o
        qT, kT, zA, v_nat, hq, kb, lf, i_nat, zB = stage
        qlo = at("qlo", [P, TOK], F32R, slots_base)
        xres = at("xres", [P, KT_N, TOK], F32, slots_base)
        work = off[0]
        KT_, kt_o = take("KTc", [P, STREAMS, PAST])
        V_, v_o = take("Vc", [P, STREAMS, 4, P])
        KS = [at(f"KS{h}", [P, SEQ], F32R, v_o + 4 * SEQ * h) for h in range(2)]
        QS = [at(f"QS{h}", [P, SEQ], F32R, v_o + 4 * SEQ * (2 + h)) for h in range(2)]
        k2, _ = take("k2", [P, C2_W])
        qbd, _ = take("qbd", [P, STREAMS, 2, DSEQ])
        kTs, _ = take("kTs", [P, P])
        vs, _ = take("vs", [P, P])
        zAs, _ = take("zAs", [P, P])
        tmpT = [take(f"tmpT{i}", [P, WIN])[0] for i in range(2)]
        negtri_r, _ = take("negtri_r", [P, P], F32R)
        negones_r, _ = take("negones_r", [P, P], F32R)
        bm, _ = take("bm", [P, NBLK + STREAMS])
        be, _ = take("be", [P, NBLK + STREAMS])
        gg, _ = take("gg", [P, NBLK + STREAMS])
        em, _ = take("em", [P, STREAMS])
        bt_o = off[0]
        E = [take(f"E{i}", [P, QW])[0] for i in range(3)]
        SPH = [take(f"SPH{i}", [P, QW], F32R)[0] for i in range(2)]
        SPL = [take(f"SPL{i}", [P, QW], F32R)[0] for i in range(2)]
        SUM = [take(f"SUM{h}", [P, QW])[0] for h in range(2)]
        SUH = [take(f"SUH{h}", [P, QW], F32R)[0] for h in range(2)]
        SUL = [take(f"SUL{h}", [P, QW], F32R)[0] for h in range(2)]
        aw_o = off[0]
        Aw = [take(f"Aw{i}", [P, QW])[0] for i in range(2)]
        Es = at("Es", [P, 5, 256], F32, bt_o)
        SPs = at("SPs", [P, 5, 256], F32, bt_o + 5120)
        hsq = at("hsq", [P, 4 * P], F32, aw_o)
        hrs = at("hrs", [P, 4 * P], F32, aw_o + 2048)
        SUs = at("SUs", [P, 3, 256], F32, bt_o + 10240)
        EK = at("EK", [P, TOK], F32, bt_o + 13312)
        EQ = at("EQ", [P, TOK], F32, bt_o + 17920)
        St = [at(f"St{i}", [P, P], F32, kt_o + 512 * i) for i in range(8)]
        kendN = [at(f"kendN{i}", [P, P], F32, kt_o + 4096 + 512 * i) for i in range(2)]
        attm = [at(f"attm{i}", [P, P], F32, kt_o + 5120 + 512 * i) for i in range(2)]
        imask = at("imask", [P, 8, P], F32, kt_o + 6144)
        S0s = at("S0s", [P, STREAMS, P], F32, kt_o + 10240)
        oc = at("oc", [P, 4 * P], F32, kt_o + 14336)
        xw = [at(f"xw{w}", [P, KT_N, WIN], F32, (kt_o, kt_o + 12288, bt_o + 4608)[w]) for w in range(NW)]
        xsq = [at(f"xsq{i}", [P, 2, WIN], F32, kt_o + 24576 + 3072 * i) for i in range(2)]
        xsa = at("xsa", [P, 2, WIN], F32, bt_o)
        xrs = at("xrs", [P, WIN], F32, bt_o + 3072)
        gh = at("gh", [P, KT_N, TOK], F32R, work)
        gl = at("gl", [P, KT_N, TOK], F32R, work + 4 * KT_N * TOK)
        graw = at("graw", [P, KT_N, TOK], F32, work + 4 * KT_N * TOK)
        yb = at("yb", [P, KT_N, TOK], F32, work)
        y_o = work + 4 * KT_N * TOK
        ysq = [at(f"ysq{i}", [P, WIN], F32, y_o + 1536 * i) for i in range(3)]
        ysa = [at(f"ysa{i}", [P, WIN], F32, y_o + 1536 * (3 + i)) for i in range(3)]
        yrs = [at(f"yrs{i}", [P, WIN], F32, y_o + 1536 * (6 + i)) for i in range(3)]
        no4 = at("no4", [P, P], F32, y_o + 1536 * 9)

        bank = [ctx.enter_context(nc.psum_tensor(f"bank{i}", [P, 512], F32)) for i in range(8)]
        CH, Z, OB, TB, XB = bank[0:2], bank[2:5], bank[5], bank[6], bank[7]
        UA, UB = (bank[2], bank[4]), (bank[3], bank[5])

        def cst(d, t, name):
            o, n = d[name]
            return t[:, o:o + n]

        ident = cst(C1, k1, "ident")
        bgate, lbraw, hgn, gpre, gpost, eps_col = (cst(C1, k1, n) for n in ("bgate", "lbraw", "hgn", "gpre", "gpost", "eps"))
        negtri, negones, causal, hgmask, hgmask_s, smask, reset, reset_s, rows4, rows8 = (
            cst(C2, k2, n) for n in ("negtri", "negones", "causal", "hgmask", "hgmask_s", "smask", "reset", "reset_s", "rows4", "rows8"))

        s_c = sem("consts_loaded")
        s_x = [[sem(f"x_loaded{w}{h}") for h in range(2)] for w in range(NW)]
        s_xsa = sem("x_squares_summed")
        s_raw = [sem(f"chunk_loaded{i}") for i in range(3)]
        s_whi = sem("weights_high")
        s_wlo = sem("weights_low")
        s_xsq = sem("x_squared")
        s_xms = sem("x_meansq_step")
        s_xln = sem("x_log")
        s_xrs = sem("x_rstd")
        s_xn = sem("x_normed")
        s_xhi = sem("x_high")
        s_xlo = sem("x_low")
        s_win = sem("window_product")
        s_ev = sem("window_out_of_psum")
        s_ex = sem("window_exp")
        s_tr = sem("window_transposed")
        s_te = sem("transposed_in_sbuf")
        s_sg1 = sem("silu_plus_one")
        s_sg = sem("silu_reciprocal")
        s_silu = sem("silu_done")
        s_f1 = sem("forget_denominator")
        s_f = sem("forget_complement")
        s_lf = sem("forget_log")
        s_lb = sem("lower_bound_step")
        s_lbe = sem("lower_bound_exp")
        s_qkh = sem("keys_queries_high")
        s_qkl = sem("keys_queries_low")
        s_qk = sem("scores")
        s_E = sem("scores_exp")
        s_L = sem("scores_log")
        s_sp1 = sem("softplus_raw")
        s_sp = sem("softplus")
        s_S = sem("later_sum")
        s_sph = sem("softplus_high")
        s_spl = sem("softplus_low")
        s_Sh = sem("later_sum_high")
        s_Sl = sem("later_sum_low")
        s_cr = sem("masks_rounded")
        s_cum = sem("log_weights")
        s_a = sem("weights")
        s_am = sem("weights_masked")
        s_av = sem("values_added")
        s_gA = sem("attention_gated")
        s_cp = sem("sample_copies")
        s_qz = sem("qbd_zeroed")
        s_kv = [sem("keysT_cached"), sem("values_cached")]
        s_kout = sem("k_stored")
        s_vout = sem("v_stored")
        s_spA = sem("gated_a_spilled")
        s_spB = sem("gated_b_spilled")
        s_zs = sem("sample_scores")
        s_Es = sem("sample_exp")
        s_Ls = sem("sample_log")
        s_sps = sem("sample_softplus")
        s_spm = sem("sample_softplus_masked")
        s_Ss = sem("sample_later_sum")
        s_cs = sem("sample_log_weights")
        s_as = sem("sample_weights")
        s_asm = sem("sample_weights_masked")
        s_os = sem("sample_values_added")
        s_gs = sem("sample_gated")
        s_scan = sem("decay_scanned")
        s_bmc = sem("block_ends_copied")
        s_A = sem("decay_centred")
        s_ge = sem("block_decay_log")
        s_EX = sem("decay_exp")
        s_hqd = sem("queries_decayed")
        s_hki = sem("keys_grown")
        s_hke = sem("keys_to_block_end")
        s_S0 = sem("state_zeroed")
        s_S0l = sem("state_loaded")
        s_S0m = sem("state_scaled")
        s_im = sem("values_by_block")
        s_kt = sem("keys_transposed")
        s_kn = sem("keys_natural")
        s_at = sem("hgrn_scores")
        s_atm = sem("hgrn_scores_masked")
        s_KV = sem("block_updates")
        s_ch = sem("state_step")
        s_h3 = sem("hgrn_out")
        s_oc = sem("hgrn_out_copied")
        s_hs = sem("hgrn_squared")
        s_hm = sem("hgrn_meansq")
        s_hl = sem("hgrn_log")
        s_hr = sem("hgrn_rstd")
        s_hg1 = sem("hgrn_normed")
        s_hg = sem("hgrn_gated")
        s_ss1 = sem("sample_state_decayed")
        s_ss = sem("sample_state")
        s_so = sem("prompt_state_stored")
        s_sso = sem("sample_state_stored")
        s_gr = [sem(f"gated_reloaded{i}") for i in range(8)]
        s_gh = sem("gated_high")
        s_gl = sem("gated_low")
        s_g1 = sem("gate_plus_one")
        s_sig = sem("gate_sigmoid")
        s_u = sem("branch_products")
        s_ma = sem("branch_a_gated")
        s_mb = sem("branch_b_gated")
        s_mg = sem("merged")
        s_mh = sem("merged_high")
        s_ml = sem("merged_low")
        s_xr = sem("residual_loaded")
        s_no = sem("minus_ones")
        s_yq = sem("y_squared")
        s_ya = sem("y_squares_summed")
        s_yn = sem("y_meansq")
        s_yl = sem("y_log")
        s_yr = sem("y_rstd")
        s_yg = sem("y_scaled")
        s_yo = sem("y_done")
        s_yg3 = sem("y_scaled_gpsimd")
        s_yo3 = sem("y_done_gpsimd")
        s_out = sem("y_stored")

        def need(eng, s, v):
            if v > 0:
                eng.wait_ge(s, v)

        def chunk_done(eng, g):
            if g < 0:
                return
            if g == 0:
                eng.wait_ge(s_win, 5)
            elif GATE_G0 <= g < OUT_G0 and MERGE[g - GATE_G0][0] == "branch":
                eng.wait_ge(s_u, 3 * MERGE[g - GATE_G0][1] + 3)
            else:
                eng.wait_ge(s_win, win_of(g) + 3)

        def attention_over(eng, p):
            need(eng, s_a, NS * (p + 1))
            need(eng, s_am, DIAGS * (p + 1))
            need(eng, s_av, NS * (p + 1))
            need(eng, s_gA, 2 * (p + 1))
            need(eng, s_S, SUMS * (p + 1))

        def recurrence_over(eng, p, norm=True):
            need(eng, s_ss, 2 * (p + 1))
            if norm:
                need(eng, s_hg, 3 * (p + 1))
            need(eng, s_gs, 2 * (p + 1))
            need(eng, s_ch, NBLK * (p + 1))
            need(eng, s_hki, p + 1)
            need(eng, s_hqd, p + 1)

        block = ctx.enter_context(nc.Block())

        @block.sync
        def _(sp):
            def load_chunk(g):
                chunk_done(sp, g - 3)
                sp.dma_start(wr[g % 3][:, :, :], wch[g].rearrange("p (k c) -> p k c", c=P)).then_inc(s_raw[g % 3], 16)

            def load_x(w, half):
                r = slice(4 * half, 4 * half + 4)
                sp.dma_start(xw[w][:, r, :], xT[:, r, w * WIN:(w + 1) * WIN]).then_inc(s_x[w][half], 16)

            def store_kv(pp):
                sp.wait_ge(s_ev, win_of(1 + (8 * pp if pp else 0)) + 3)
                sp.dma_start(okT[pp], kT[:, :]).then_inc(s_kout, 16)
                sp.wait_ge(s_te, 6 * pp + 3)
                sp.dma_start(ov[pp].rearrange("(t s) c -> s t c", s=P), v_nat[:, :].rearrange("s (t c) -> s t c", c=P)).then_inc(s_vout, 16)

            load_x(0, 0)
            load_x(0, 1)
            sp.dma_start(k1[:, :], c1).then_inc(s_c, 16)
            sp.dma_start(k2[:, :], c2).then_inc(s_c, 16)
            load_chunk(0)
            load_x(1, 0)
            load_x(1, 1)
            load_chunk(1)
            load_x(2, 0)
            load_x(2, 1)
            for g in range(2, 7):
                load_chunk(g)
            store_kv(0)
            for p in range(PAIRS):
                recurrence_over(sp, p - 1)
                if p:
                    sp.wait_ge(s_sso, 16 * p)
                    sp.wait_ge(s_so, 16 * p)
                    sp.wait_ge(s_os, p)
                else:
                    sp.wait_ge(s_xlo, NW * 4)
                    sp.wait_ge(s_xsa, NW * 3)
                sp.dma_start(KT_[:, :, :], ckT[p].rearrange("i d s -> d i s")).then_inc(s_kv[0], 16)
                for g in range(4 + 8 * p + 3, 8 + 8 * p + 2):
                    load_chunk(g)
                sp.wait_ge(s_qk, NS * (p + 1))
                sp.dma_start(V_[:, :, :, :].rearrange("s i j c -> s i (j c)"), cv[p].rearrange("i s n -> s i n")).then_inc(s_kv[1], 16)
                load_chunk(8 + 8 * p + 2)
                sp.wait_ge(s_gA, 2 * (p + 1))
                sp.dma_start(spill[p, :, 0:SEQ], zA[:, 0:SEQ]).then_inc(s_spA, 16)
                sp.wait_ge(s_zs, 3 * (p + 1))
                recurrence_over(sp, p - 1)
                sp.dma_start(S0s[:, :, :], st[p].rearrange("i c v -> c i v")).then_inc(s_S0l, 16)
                sp.wait_ge(s_gs, 2 * (p + 1))
                sp.dma_start(spill[p, :, SEQ:TOK], zAs[:, :]).then_inc(s_spA, 16)
                if p == PAIRS - 1:
                    sp.wait_ge(s_os, PAIRS)
                    sp.wait_ge(s_hki, PAIRS)
                    sp.wait_ge(s_hqd, PAIRS)
                    sp.wait_ge(s_spA, 32 * (PAIRS - 1))
                    for t in range(3):
                        sp.dma_start(graw[:, ROW_OF[t], :], spill[t]).then_inc(s_gr[t], 16)
                for g in range(8 + 8 * p + 3, 12 + 8 * p + 3):
                    load_chunk(g)
                sp.wait_ge(s_ch, NBLK * (p + 1))
                sp.dma_start(osp[p], St[NBLK % 8][:, :]).then_inc(s_so, 16)
                sp.wait_ge(s_hg, 3 * (p + 1))
                sp.dma_start(spill[PAIRS + p], zB[:, :]).then_inc(s_spB, 16)
                sp.wait_ge(s_ss, 2 * (p + 1))
                sp.dma_start(oss[p].rearrange("i c v -> c i v"), S0s[:, :, :]).then_inc(s_sso, 16)
                if p + 1 < PAIRS:
                    store_kv(p + 1)
            recurrence_over(sp, PAIRS - 1)
            sp.wait_ge(s_h3, NT * PAIRS)
            sp.wait_ge(s_hm, 3 * PAIRS)
            sp.wait_ge(s_spA, 32 * PAIRS)
            sp.wait_ge(s_spB, 16 * PAIRS)
            for t in range(3, 8):
                sp.dma_start(graw[:, ROW_OF[t], :], spill[t]).then_inc(s_gr[t], 16)
            for g in range(39, 64):
                load_chunk(g)
            sp.wait_ge(s_ml, 10)
            sp.dma_start(xres[:, :, :], xT).then_inc(s_xr, 16)
            for w in range(NW):
                for half in range(2):
                    sp.wait_ge(s_yo, 2 * w + half + 1)
                    r = slice(4 * half, 4 * half + 4)
                    sp.dma_start(yT[:, r, w * WIN:(w + 1) * WIN], yb[:, r, w * WIN:(w + 1) * WIN]).then_inc(s_out, 16)
            sp.wait_ge(s_out, 16 * 2 * NW)
            sp.wait_ge(s_kout, 16 * PAIRS)
            sp.wait_ge(s_vout, 16 * PAIRS)
            sp.wait_ge(s_so, 16 * PAIRS)
            sp.wait_ge(s_sso, 16 * PAIRS)

        @block.tensor
        def _(pe):
            def product(g, w, q, n=None):
                n = win_of(g) + w if n is None else n
                if q == 0:
                    if w == 0:
                        pe.wait_ge(s_whi, g + 1)
                        pe.wait_ge(s_wlo, g + 1)
                    need(pe, s_ev, n - 1)
                for m in range(8 * q, 8 * q + 8):
                    k, part = m // 3, m % 3
                    if g == 0 and part == 0:
                        pe.wait_ge(s_xhi, 4 * w + k // 2 + 1)
                    if g == 0 and part == 1:
                        pe.wait_ge(s_xlo, 4 * w + k // 2 + 1)
                    if g == OUT_G0 and part == 0 and (w == 0 or k == 7):
                        pe.wait_ge(s_mh, k + 1 + w)
                        pe.wait_ge(s_ml, k + 1 + w)
                    weights = wl[g % 3] if part == 2 else wh[g % 2]
                    rows = xl if part == 1 else xh
                    i = nc.tensor.matmul(CH[n % 2][:, 0:WIN], weights[:, k, :], rows[:, k, w * WIN:(w + 1) * WIN],
                                         start=(m == 0), stop=(m == 23))
                    if m == 23:
                        i.then_inc(s_win, 1)

            def transpose_window(n, idx, src):
                pe.wait_ge(s_ev, n + 1)
                need(pe, s_te, idx)
                for t in range(3):
                    i = nc.tensor.transpose(TB[:, t * P:(t + 1) * P], src[:, t * P:(t + 1) * P], ident)
                i.then_inc(s_tr, 1)

            def turn_attention(pp, w12):
                c, w = divmod(w12, 3)
                if c == 2:
                    transpose_window(win_of(8 * pp if pp else 0) + w12, 6 * pp + w, tmpT[(12 * pp + w) % 2])

            def turn_recurrence(p, w12):
                c, w = divmod(w12, 3)
                if c == 2:
                    transpose_window(win_of(4 + 8 * p) + w12, 6 * p + 3 + w, tmpT[(12 * p + 6 + w) % 2])

            def x_square_sum(w):
                pe.wait_ge(s_xsa, 3 * (w + 1))
                for r in range(2):
                    i = nc.tensor.matmul(Z[w][:, 0:WIN], negones, xsa[:, r, :], start=(r == 0), stop=(r == 1))
                i.then_inc(s_xms, 1)

            pe.wait_ge(s_c, 32)
            x_square_sum(0)
            for i12 in range(12):
                c, w = prologue_window(i12)
                if i12 == 1:
                    x_square_sum(1)
                for q in range(PIECES):
                    if i12 == 2 and q == 2:
                        x_square_sum(2)
                    product(c, w, q, i12)
                if i12:
                    turn_attention(0, i12 - 1)
            turn_attention(0, 11)

            for p in range(PAIRS):
                need(pe, s_ch, NBLK * p)
                need(pe, s_atm, NT * p)
                need(pe, s_ss, 2 * p)
                late = []
                for n in range(B_STEPS):
                    if n < NS:
                        wd, j, h = STEPS[n]
                        c0, t = first_col(n), NS * p + n
                        if n == 0:
                            pe.wait_ge(s_qkh, 6 * (p + 1))
                            pe.wait_ge(s_qkl, 4 * (p + 1))
                        need(pe, s_a, t - 2)
                        c0 = min(c0, QW // 2)
                        keys, queries = slice(j * P, (j + 1) * P), slice(wd * QW + c0, (wd + 1) * QW)
                        head = slice(DH * h, DH * h + DH)
                        nc.tensor.matmul(Z[n % 3][:, c0:QW], KS[h][:, keys], QS[h][:, queries], start=True, stop=False)
                        nc.tensor.matmul(Z[n % 3][:, c0:QW], KS[h][head, keys], qlo[head, queries],
                                         start=False, stop=True).then_inc(s_qk, 1)
                    mid = len(B_PIECES[n]) // 2
                    for x in B_PIECES[n][:mid]:
                        product(4 + 8 * p + x // 9, x // 3 % 3, x % 3)
                    if 1 <= n <= NS:
                        m = n - 1
                        wd, j, h = STEPS[m]
                        c0, t, q = first_col(m), NS * p + m, tile_rank(m)

                        def add(weights, rows, lo):
                            return nc.tensor.matmul(Z[m % 3][:, lo:QW], weights, rows[:, lo:QW], start=False, stop=True,
                                                    skip_group_check=True)

                        if q == 0:
                            pe.wait_ge(s_cr, 2)
                            pe.wait_ge(s_sp, t + 1)
                            i = add(negtri, E[m % 3], c0)
                        else:
                            pe.wait_ge(s_sph, SPLITS * p + rows_until(m))
                            add(negtri_r[:, :], SPH[m % 2], c0)
                            cs = first_col(m - 2)
                            if q == 1:
                                pe.wait_ge(s_S, SUMS * p + sums_until(m - 2))
                                add(negones, SUM[h], cs)
                            else:
                                pe.wait_ge(s_Sh, SUM_SPLITS * p + sum_rows_until(m))
                                add(negones_r[:, :], SUH[h], cs)
                                pe.wait_ge(s_Sl, SUM_SPLITS * p + sum_rows_until(m))
                                add(negones_r[:, :], SUL[h], cs)
                            pe.wait_ge(s_spl, SPLITS * p + rows_until(m))
                            i = add(negtri_r[:, :], SPL[m % 2], c0)
                        i.then_inc(s_cum, 1)
                    for x in B_PIECES[n][mid:]:
                        product(4 + 8 * p + x // 9, x // 3 % 3, x % 3)
                    if n >= 2:
                        m = n - 2
                        wd, j, h = STEPS[m]
                        c0, t = first_col(m), NS * p + m
                        if m == 0:
                            need(pe, s_oc, 3 * p)
                            pe.wait_ge(s_te, 6 * p + 3)
                        if j == 4 * wd + 3 and h == 0:
                            need(pe, s_gA, 2 * p + wd)
                        pe.wait_ge(s_a, t + 1)
                        if diagonal(m):
                            pe.wait_ge(s_am, DIAGS * p + diagonals_until(m))
                        nc.tensor.matmul(OB[DH * h:DH * h + DH, c0:QW], v_nat[:, j * P + DH * h:j * P + DH * h + DH],
                                         Aw[m % 2][:, c0:QW], start=(j == 4 * wd + 3), stop=(j == 0),
                                         skip_group_check=True).then_inc(s_av, 1)
                    for w12 in late:
                        turn_recurrence(p, w12)
                    late = ended(B_PIECES[n])
                for w12 in late:
                    turn_recurrence(p, w12)

                late = []
                for m in range(A_STEPS):
                    if m == 0:
                        attention_over(pe, p)
                        pe.wait_ge(s_cp, 5 * (p + 1))
                        pe.wait_ge(s_kv[0], 16 * (p + 1))
                        qall = qbd[:, :, :, :].rearrange("p i h t -> p (i h t)")
                        nc.tensor.matmul(Z[2][:, 0:256], kTs[:, :], qall, start=True, stop=True).then_inc(s_zs, 1)
                        for half in (1, 0):
                            for j2 in range(2):
                                for s in range(STREAMS):
                                    o = 256 * j2 + 32 * s
                                    i = nc.tensor.matmul(Z[half][:, o:o + 32], KT_[:, s, P * (2 * half + j2):P * (2 * half + j2 + 1)],
                                                         qall[:, 32 * s:32 * s + 32], start=(j2 == 0 and s == 0), stop=True,
                                                         skip_group_check=True)
                            i.then_inc(s_zs, 1)
                    if m == 1:
                        pe.wait_ge(s_spm, p + 1)
                        nc.tensor.matmul(Z[2][:, 0:256], negtri, SPs[:, 4, :], start=False, stop=True,
                                         skip_group_check=True).then_inc(s_cs, 1)
                        pe.wait_ge(s_sps, 3 * (p + 1))
                        for j in (3, 2, 1, 0):
                            bk = Z[j // 2][:, 256 * (j % 2):256 * (j % 2) + 256]
                            nc.tensor.matmul(bk, negtri, SPs[:, j, :], start=False, stop=True, skip_group_check=True)
                            if j < 3:
                                pe.wait_ge(s_Ss, 3 * p + 3 - j)
                            i = nc.tensor.matmul(bk, negones, SPs[:, 4, :] if j == 3 else SUs[:, 2 - j, :],
                                                 start=False, stop=True, skip_group_check=True)
                            if j % 2 == 0:
                                i.then_inc(s_cs, 1)
                    if m == 2:
                        pe.wait_ge(s_asm, p + 1)
                        nc.tensor.matmul(OB[:, 0:256], vs[:, :], Es[:, 4, :], start=True, stop=True)
                        pe.wait_ge(s_kv[1], 16 * (p + 1))
                        pe.wait_ge(s_as, 3 * (p + 1))
                        for j in (3, 2, 1, 0):
                            for s in range(STREAMS):
                                i = nc.tensor.matmul(OB[:, 32 * s:32 * s + 32], V_[:, s, j, :], Es[:, j, 32 * s:32 * s + 32],
                                                     start=False, stop=True, skip_group_check=True)
                        i.then_inc(s_os, 1)
                    if m >= 3:
                        c = m - 3
                        if c < NT:
                            u = 12 * p + x_use_tile(c)
                            pe.wait_ge(s_hke, 2 * (p + 1))
                            need(pe, s_kn, 9 * p + c)
                            if c >= 7:
                                pe.wait_ge(s_hl, 3 * p + 1)
                            nc.tensor.transpose(XB[:, 0:P], lf[:, c * P:(c + 1) * P], ident).then_inc(s_kt, 1)
                            pe.wait_ge(s_hqd, p + 1)
                            pe.wait_ge(s_hki, p + 1)
                            if c == 0:
                                pe.wait_ge(s_as, 3 * (p + 1))
                            need(pe, s_atm, 9 * p + c)
                            nc.tensor.matmul(Z[2][:, 0:P], kb[:, c * P:(c + 1) * P], hq[:, c * P:(c + 1) * P],
                                             start=True, stop=True).then_inc(s_at, 1)
                        mid = len(A_PIECES[m]) // 2
                        for x in A_PIECES[m][:mid]:
                            product(8 + 8 * p + x // 9, x // 3 % 3, x % 3)
                        if 1 <= c <= NT:
                            b = c - 1
                            pe.wait_ge(s_kn, 9 * p + b + 1)
                            pe.wait_ge(s_im, 9 * p + b + 1)
                            if b < 8:
                                if b >= 2:
                                    pe.wait_ge(s_ch, NBLK * p + 4 * (b - 1))
                                nc.tensor.matmul(Z[b % 2][:, :], kendN[b % 2][:, :],
                                                 imask[:, 4 * (b % 2):4 * (b % 2) + 4, :].rearrange("s b v -> s (b v)"),
                                                 start=True, stop=True).then_inc(s_KV, 1)
                            else:
                                pe.wait_ge(s_ch, NBLK * (p + 1))
                                for half in range(2):
                                    i = nc.tensor.matmul(Z[half][:, :], kendN[b % 2][:, :],
                                                         imask[:, 4 * half:4 * half + 4, :].rearrange("s b v -> s (b v)"),
                                                         start=True, stop=True)
                                i.then_inc(s_KV, 1)
                        for x in A_PIECES[m][mid:]:
                            product(8 + 8 * p + x // 9, x // 3 % 3, x % 3)
                        if 2 <= c <= NT + 1:
                            b = c - 2
                            if b == 0:
                                pe.wait_ge(s_gs, 2 * (p + 1))
                                pe.wait_ge(s_S0, p + 1)
                            if b in (4, 8):
                                pe.wait_ge(s_oc, 3 * p + b // 4)
                            pe.wait_ge(s_atm, 9 * p + b + 1)
                            o0 = P * (b % 4)
                            nc.tensor.matmul(OB[:, o0:o0 + P], i_nat[:, b * P:(b + 1) * P], attm[b % 2][:, :],
                                             start=True, stop=True)
                            if b < 8:
                                for s in range(4):
                                    nb = 4 * b + s
                                    if nb:
                                        pe.wait_ge(s_ch, NBLK * p + nb)
                                    i = nc.tensor.matmul(OB[:, o0 + BLK * s:o0 + BLK * s + BLK], St[nb % 8][:, :],
                                                         hq[:, nb * BLK:(nb + 1) * BLK], start=False, stop=True,
                                                         skip_group_check=True)
                            else:
                                pe.wait_ge(s_S0m, p + 1)
                                for s in range(STREAMS):
                                    i = nc.tensor.matmul(OB[:, o0 + DSEQ * s:o0 + DSEQ * s + DSEQ], S0s[:, s, :],
                                                         hq[:, SEQ + DSEQ * s:SEQ + DSEQ * s + DSEQ], start=False, stop=True,
                                                         skip_group_check=True)
                            i.then_inc(s_h3, 1)
                        if c in MS_STEP:
                            g = MS_STEP.index(c)
                            n = P * (GROUPS[g][1] - GROUPS[g][0])
                            pe.wait_ge(s_hs, 3 * p + g + 1)
                            pe.wait_ge(s_kn, 9 * p + (7 if g == 0 else 9))
                            if g:
                                pe.wait_ge(s_hl, 3 * p + g)
                            nc.tensor.matmul(XB[:, 0:n], negones, hsq[:, 0:n], start=True, stop=True).then_inc(s_hm, 1)
                    else:
                        for x in A_PIECES[m]:
                            product(8 + 8 * p + x // 9, x // 3 % 3, x % 3)
                    if p + 1 < PAIRS:
                        for w12 in late:
                            turn_attention(p + 1, w12)
                        late = ended(A_PIECES[m])
                if p + 1 < PAIRS:
                    for w12 in late:
                        turn_attention(p + 1, w12)

            for g in range(GATE_G0 + 4, OUT_G0):
                what, dm, kind = MERGE[g - GATE_G0]
                if what == "gate":
                    for w in range(NW):
                        for q in range(PIECES):
                            product(g, w, q)
                    continue
                if dm == 0:
                    recurrence_over(pe, PAIRS - 1)
                pe.wait_ge(s_whi, g + 1)
                pe.wait_ge(s_wlo, g + 1)
                for w in range(NW):
                    n = 3 * dm + w
                    need(pe, s_mb, n - 1)
                    need(pe, s_ma, n - 1)
                    for half, bk in ((0, UA[n % 2]), (1, UB[n % 2])):
                        for m in range(12):
                            t, part = 4 * half + m // 3, m % 3
                            if n == 0 and part == 0:
                                pe.wait_ge(s_gh, t + 1)
                                pe.wait_ge(s_gl, t + 1)
                            weights = wl[g % 3] if part == 2 else wh[g % 2]
                            rows = gl if part == 1 else gh
                            i = nc.tensor.matmul(bk[:, 0:WIN], weights[:, t, :], rows[:, ROW_OF[t], w * WIN:(w + 1) * WIN],
                                                 start=(m == 0), stop=(m == 11))
                    i.then_inc(s_u, 1)

            def y_square_sum(w):
                pe.wait_ge(s_ya, 3 * (KT_N - 3) + w + 1)
                nc.tensor.matmul(Z[w][:, 0:WIN], no4[:, :], ysa[w][:, :], start=True, stop=False)
                pe.wait_ge(s_yq, 3 * (KT_N - 1) + w + 1)
                nc.tensor.matmul(Z[w][:, 0:WIN], no4[:, :], ysq[w][:, :], start=False, stop=True).then_inc(s_yn, 1)

            for n in range(3 * KT_N):
                for q in range(PIECES):
                    product(OUT_G0 + n // 3, n % 3, q)
                if n == 3 * KT_N - 3:
                    pe.wait_ge(s_no, 1)
                    pe.wait_ge(s_mb, 3 * KT_N)
                    pe.wait_ge(s_ma, 3 * KT_N)
                if n > 3 * KT_N - 3:
                    y_square_sum(n - 3 * KT_N + 2)
            y_square_sum(2)

        @block.scalar
        def _(act):
            def evacuate(n, dst, waits):
                for s, v in waits:
                    need(act, s, v)
                act.wait_ge(s_win, n + 1)
                nc.scalar.activation(dst, CH[n % 2][:, 0:WIN], ACT.Copy).then_inc(s_ev, 1)

            def tmp_free(idx):
                pair, r = divmod(idx - 2, 12)
                if idx < 2:
                    return
                half, r = divmod(r, 6)
                act.wait_ge(s_silu if r >= 3 else s_tr, 6 * pair + 3 * half + r % 3 + 1)

            def silu(n, idx, half, dst, waits):
                t = tmpT[idx % 2][:, :]
                tmp_free(idx)
                act.wait_ge(s_win, n + 1)
                nc.scalar.activation(t, CH[n % 2][:, 0:WIN], ACT.Exp, scale=-1.0).then_inc(s_ex, 1)
                evacuate(n, dst, waits)
                act.wait_ge(s_ex, half + 1)
                nc.scalar.activation(t, t, ACT.Ln, bias=1.0).then_inc(s_sg1, 1)
                act.wait_ge(s_sg1, half + 1)
                nc.scalar.activation(t, t, ACT.Exp, scale=-1.0).then_inc(s_sg, 1)

            def window_attention(pp, w12):
                c, w = prologue_window(w12) if pp == 0 else divmod(w12, 3)
                n = win_of(8 * pp if pp else 0) + w12
                cols = slice(w * WIN, (w + 1) * WIN)
                copies = (s_cp, 5 * pp)
                if c == 0:
                    for s, v in ((s_qk, NS * pp), copies):
                        need(act, s, v)
                    act.wait_ge(s_win, n + 1)
                    nc.scalar.activation(qT[:, cols], CH[n % 2][:, 0:WIN], ACT.Copy, scale=DH ** -0.5).then_inc(s_ev, 1)
                elif c == 1:
                    evacuate(n, kT[:, cols], ((s_qk, NS * pp), copies, (s_kout, 16 * pp)))
                elif c == 2:
                    tmp_free(12 * pp + w)
                    evacuate(n, tmpT[(12 * pp + w) % 2][:, :], ())
                else:
                    silu(n, 12 * pp + 3 + w, 6 * pp + w, zA[:, cols], (copies, (s_spA, 32 * pp)))

            def high_parts(pp, what):
                if what == 0:
                    act.wait_ge(s_ev, win_of(8 * pp if pp else 0) + 6)
                    if pp:
                        act.wait_ge(s_os, pp)
                    else:
                        act.wait_ge(s_xlo, 4 * NW)
                        act.wait_ge(s_xsa, 3 * NW)
                for h in range(2):
                    own, other = slice(DH * h, DH * h + DH), slice(DH * (1 - h), DH * (1 - h) + DH)
                    dst, src = ((KS[h][own, :], kT), (QS[h][own, :], qT), (QS[h][other, :], qT))[what]
                    nc.scalar.activation(dst, src[own, 0:SEQ], ACT.Copy).then_inc(s_qkh, 1)

            def window_recurrence(p, w12):
                c, w = divmod(w12, 3)
                n = win_of(4 + 8 * p) + w12
                cols = slice(w * WIN, (w + 1) * WIN)
                if c == 0:
                    evacuate(n, hq[:, cols], ((s_h3, NT * p),))
                elif c == 1:
                    need(act, s_at, NT * p)
                    need(act, s_hke, 2 * p)
                    act.wait_ge(s_win, n + 1)
                    nc.scalar.activation(kb[:, cols], CH[n % 2][:, 0:WIN], ACT.Exp).then_inc(s_ev, 1)
                elif c == 2:
                    tmp_free(12 * p + 6 + w)
                    evacuate(n, tmpT[(12 * p + 6 + w) % 2][:, :], ())
                else:
                    silu(n, 12 * p + 9 + w, 6 * p + 3 + w, zB[:, cols], ((s_spB, 16 * p),))

            def forget(p, w):
                k = kb[:, w * WIN:(w + 1) * WIN]
                act.wait_ge(s_ev, win_of(5 + 8 * p) + w + 1)
                nc.scalar.activation(k, k, ACT.Ln, bias=1.0).then_inc(s_f1, 1)
                act.wait_ge(s_f1, 3 * p + w + 1)
                nc.scalar.activation(k, k, ACT.Exp, scale=-1.0, bias=lbv[:, 4, p:p + 1]).then_inc(s_f, 1)
                act.wait_ge(s_f, 3 * p + w + 1)
                need(act, s_kt, NT * p)
                nc.scalar.activation(lf[:, w * WIN:(w + 1) * WIN], k, ACT.Ln, scale=-1.0, bias=1.0).then_inc(s_lf, 1)

            def window_gate(dm, kind, w):
                n = gate_window_no(dm, kind, w)
                s = slots[dm if kind == 0 else GATE_B_SLOT[dm]][:, w * WIN:(w + 1) * WIN]
                if w == 0:
                    gate_slot_free(dm, kind)
                act.wait_ge(s_win, n + 1)
                nc.scalar.activation(s, CH[n % 2][:, 0:WIN], ACT.Exp, scale=-1.0,
                                     bias=ngate[:, 8 * kind + dm:8 * kind + dm + 1]).then_inc(s_ev, 1)
                act.wait_ge(s_ev, n + 1)
                nc.scalar.activation(s, s, ACT.Ln, bias=1.0).then_inc(s_g1, 1)
                act.wait_ge(s_g1, 6 * dm + 3 * kind + w + 1)
                nc.scalar.activation(s, s, ACT.Exp, scale=-1.0).then_inc(s_sig, 1)

            def gate_slot_free(dm, kind):
                if dm < 2:
                    act.wait_ge(s_qk, NS * PAIRS)
                    act.wait_ge(s_av, NS * PAIRS)
                    act.wait_ge(s_cp, 5 * PAIRS)
                    act.wait_ge(s_kout, 16 * PAIRS)
                    act.wait_ge(s_vout, 16 * PAIRS)
                    act.wait_ge(s_spA, 16 * (2 * PAIRS - 1))
                if dm == 2:
                    act.wait_ge(s_h3, NT * PAIRS)
                    act.wait_ge(s_spB, 16 * PAIRS)
                need(act, s_mg, 3 * (slot_user_before(dm, kind) + 1))

            def gated_high(t):
                act.wait_ge(s_gr[t], 16)
                nc.scalar.activation(gh[:, ROW_OF[t], :], graw[:, ROW_OF[t], :], ACT.Copy).then_inc(s_gh, 1)

            nc.scalar.preload_act_table_set("natural_log_exp_and_others")
            def square_x(w, r):
                act.wait_ge(s_x[w][r // 2], 16)
                if r == 0:
                    need(act, s_xms, w)
                else:
                    need(act, s_xsa, 3 * w + r - 2)
                dst = xsa if r == 0 else xsq[(3 * w + r) % 2]
                nc.scalar.activation(dst[:, :, :], xw[w][:, 2 * r:2 * r + 2, :], ACT.Square).then_inc(s_xsq, 1)

            for r in range(4):
                square_x(0, r)
            act.wait_ge(s_c, 32)
            act.wait_ge(s_lb, 3)
            nc.scalar.activation(lbv[:, 1:3, :], lbv[:, 1:3, :], ACT.Exp).then_inc(s_lbe, 1)
            act.wait_ge(s_lb, 6)
            nc.scalar.activation(lbv[:, 4, :], lbv[:, 4, :], ACT.Ln).then_inc(s_lbe, 1)
            for w in range(NW):
                act.wait_ge(s_xms, w + 1)
                need(act, s_xn, KT_N * w)
                nc.scalar.activation(xrs[:, :], Z[w][:, 0:WIN], ACT.Ln, scale=-1.0 / D, bias=eps_col).then_inc(s_xln, 1)
                act.wait_ge(s_xln, w + 1)
                nc.scalar.activation(xrs[:, :], xrs[:, :], ACT.Exp, scale=-0.5).then_inc(s_xrs, 1)
                for r in range(4):
                    act.wait_ge(s_xn, KT_N * w + 2 * r + 2)
                    nc.scalar.activation(xh[:, 2 * r:2 * r + 2, w * WIN:(w + 1) * WIN], xw[w][:, 2 * r:2 * r + 2, :],
                                         ACT.Copy).then_inc(s_xhi, 1)
                    if w + 1 < NW:
                        square_x(w + 1, r)
                    if w and r in (0, 2):
                        window_attention(0, 2 * (w - 1) + r // 2)
            for w12 in range(4, 12):
                window_attention(0, w12)
                if w12 in (6, 7, 8):
                    high_parts(0, w12 - 6)

            for p in range(PAIRS):
                recurrence_over(act, p - 1, norm=False)
                late = []
                for n in range(B_STEPS):
                    if n < NS:
                        c0, t = first_col(n), NS * p + n
                        act.wait_ge(s_qk, t + 1)
                        need(act, s_cum, t - 2)
                        need(act, s_S, SUMS * p + (sums_until(n - 3) if n >= 3 else 0))
                        nc.scalar.activation(E[n % 3][:, c0:QW], Z[n % 3][:, c0:QW], ACT.Exp).then_inc(s_E, 1)
                        act.wait_ge(s_E, t + 1)
                        nc.scalar.activation(E[n % 3][:, c0:QW], E[n % 3][:, c0:QW], ACT.Ln, bias=1.0).then_inc(s_L, 1)
                    if 1 <= n <= NS:
                        m = n - 1
                        c0, t = first_col(m), NS * p + m
                        act.wait_ge(s_cum, t + 1)
                        need(act, s_av, t - 1)
                        if m < 2:
                            need(act, s_hg, 3 * p)
                        nc.scalar.activation(Aw[m % 2][:, c0:QW], Z[m % 3][:, c0:QW], ACT.Exp).then_inc(s_a, 1)
                    for c, w in late:
                        if c == 1:
                            forget(p, w)
                    late = []
                    for w12 in ended(B_PIECES[n]):
                        window_recurrence(p, w12)
                        late.append(divmod(w12, 3))
                attention_over(act, p)
                for m in range(A_STEPS):
                    if m == 0:
                        for r, (bk, lo, n) in enumerate(((Z[2], 4, 1), (Z[1], 2, 2), (Z[0], 0, 2))):
                            e = Es[:, lo:lo + n, :].rearrange("s j c -> s (j c)")
                            act.wait_ge(s_zs, 3 * p + r + 1)
                            nc.scalar.activation(e, bk[:, 0:256 * n], ACT.Exp).then_inc(s_Es, 1)
                            act.wait_ge(s_Es, 3 * p + r + 1)
                            nc.scalar.activation(e, e, ACT.Ln, bias=1.0).then_inc(s_Ls, 1)
                        act.wait_ge(s_ge, 2 * (p + 1))
                        nc.scalar.activation(gg[:, :], be[:, :], ACT.Exp).then_inc(s_EX, 1)
                        nc.scalar.activation(em[:, :], bm[:, NBLK:], ACT.Exp).then_inc(s_EX, 1)
                        act.wait_ge(s_A, 2 * (p + 1))
                        nc.scalar.activation(EK[:, :], lf[:, :], ACT.Exp, scale=-1.0).then_inc(s_EX, 1)
                        nc.scalar.activation(EQ[:, :], lf[:, :], ACT.Exp).then_inc(s_EX, 1)
                    if m == 1:
                        act.wait_ge(s_sps, 3 * (p + 1))
                        for r, (bk, lo, n) in enumerate(((Z[2], 4, 1), (Z[1], 2, 2), (Z[0], 0, 2))):
                            act.wait_ge(s_cs, 3 * p + r + 1)
                            nc.scalar.activation(Es[:, lo:lo + n, :].rearrange("s j c -> s (j c)"), bk[:, 0:256 * n],
                                                 ACT.Exp).then_inc(s_as, 1)
                    if m >= 3:
                        c = m - 3
                        if c < NT:
                            act.wait_ge(s_kt, NT * p + c + 1)
                            need(act, s_KV, NT * p + c - 1 if c >= 2 else 0)
                            nc.scalar.activation(kendN[c % 2][:, :], XB[:, 0:P], ACT.Copy).then_inc(s_kn, 1)
                        for g in range(3):
                            if c == MS_STEP[g]:
                                n = P * (GROUPS[g][1] - GROUPS[g][0])
                                act.wait_ge(s_hm, 3 * p + g + 1)
                                need(act, s_hg1, 3 * p + g)
                                nc.scalar.activation(hrs[:, 0:n], XB[:, 0:n], ACT.Ln, scale=-1.0 / P, bias=eps_col).then_inc(s_hl, 1)
                                act.wait_ge(s_hl, 3 * p + g + 1)
                                nc.scalar.activation(hrs[:, 0:n], hrs[:, 0:n], ACT.Exp, scale=-0.5).then_inc(s_hr, 1)
                        if c in (5, 9, 10):
                            g = (5, 9, 10).index(c)
                            n = P * (GROUPS[g][1] - GROUPS[g][0])
                            act.wait_ge(s_h3, NT * p + GROUPS[g][1])
                            need(act, s_hg, 3 * p + g)
                            nc.scalar.activation(oc[:, 0:n], OB[:, 0:n], ACT.Copy).then_inc(s_oc, 1)
                            act.wait_ge(s_oc, 3 * p + g + 1)
                            need(act, s_hm, 3 * p + g)
                            nc.scalar.activation(hsq[:, 0:n], oc[:, 0:n], ACT.Square).then_inc(s_hs, 1)
                    if p + 1 < PAIRS and m in STACK_STEPS:
                        high_parts(p + 1, STACK_STEPS.index(m))
                    for w12 in ended(A_PIECES[m]):
                        if p + 1 < PAIRS:
                            window_attention(p + 1, w12)
                        else:
                            window_gate(w12 // 6, w12 // 3 % 2, w12 % 3)
                    if p == PAIRS - 1 and m in (7, 9, 11):
                        gated_high((m - 7) // 2)
            for kind in range(2):
                for w in range(NW):
                    window_gate(2, kind, w)
                    for t in ((3, 4), (5,), (6,), (7,), (), ())[3 * kind + w]:
                        if t == 3:
                            recurrence_over(act, PAIRS - 1)
                            act.wait_ge(s_h3, NT * PAIRS)
                            act.wait_ge(s_sso, 16 * PAIRS)
                            act.wait_ge(s_so, 16 * PAIRS)
                        gated_high(t)
            for dm in range(3, 8):
                for kind in range(2):
                    for w in range(NW):
                        window_gate(dm, kind, w)
            act.wait_ge(s_win, OUT_W0)
            for dm in range(7):
                act.wait_ge(s_mg, 3 * dm + 3)
                nc.scalar.activation(xh[:, dm, :], slots[dm][:, :], ACT.Copy).then_inc(s_mh, 1)
            for w in range(NW):
                cols = slice(w * WIN, (w + 1) * WIN)
                act.wait_ge(s_mg, 21 + w + 1)
                nc.scalar.activation(xh[:, 7, cols], slots[7][:, cols], ACT.Copy).then_inc(s_mh, 1)
            def y_rstd(w):
                act.wait_ge(s_yn, w + 1)
                nc.scalar.activation(yrs[w][:, :], Z[w][:, 0:WIN], ACT.Ln, scale=-1.0 / D, bias=eps_col).then_inc(s_yl, 1)
                act.wait_ge(s_yl, w + 1)
                nc.scalar.activation(yrs[w][:, :], yrs[w][:, :], ACT.Exp, scale=-0.5).then_inc(s_yr, 1)

            act.wait_ge(s_u, 24)
            for n in range(3 * KT_N):
                k, w = divmod(n, 3)
                act.wait_ge(s_win, OUT_W0 + n + 1)
                need(act, s_ya, n - 5)
                dst = ysa[w] if k == 0 else ysq[w]
                nc.scalar.activation(dst[:, :], CH[n % 2][:, 0:WIN], ACT.Square).then_inc(s_yq, 1)
                nc.scalar.activation(yb[:, k, w * WIN:(w + 1) * WIN], CH[n % 2][:, 0:WIN], ACT.Copy,
                                     scale=gpost[:, k:k + 1]).then_inc(s_ev, 1)
                if n == 3 * KT_N - 2:
                    y_rstd(0)
            y_rstd(1)
            y_rstd(2)

        @block.vector
        def _(dve):
            V = nc.vector

            def split_weights(g):
                dve.wait_ge(s_raw[g % 3], 16 * (g // 3 + 1))
                chunk_done(dve, g - 2)
                V.tensor_copy(wh[g % 2][:, :, :], wr[g % 3][:, :, :]).then_inc(s_whi, 1)
                dve.wait_ge(s_whi, g + 1)
                V.tensor_tensor(wl[g % 3][:, :, :], wr[g % 3][:, :, :], wh[g % 2][:, :, :].bitcast(F32),
                                ALU.subtract).then_inc(s_wlo, 1)

            def turned(idx, dst, waits):
                for s, v in waits:
                    need(dve, s, v)
                dve.wait_ge(s_tr, idx + 1)
                V.tensor_copy(dst, TB[:, 0:WIN]).then_inc(s_te, 1)

            def window_attention(pp, w12):
                c, w = divmod(w12, 3)
                if w == 0:
                    split_weights(8 * pp + c + 1)

            def low_parts(pp, what):
                dve.wait_ge(s_qkh, 6 * pp + (2, 6)[what])
                for h in range(2):
                    own, other = slice(DH * h, DH * h + DH), slice(DH * (1 - h), DH * (1 - h) + DH)
                    dst, src, high = ((KS[h][other, :], kT, KS[h]), (qlo[own, 0:SEQ], qT, QS[h]))[what]
                    V.tensor_tensor(dst, src[own, 0:SEQ], high[own, :].bitcast(F32), ALU.subtract).then_inc(s_qkl, 1)

            def turn_attention(pp, w12):
                c, w = divmod(w12, 3)
                if c == 2:
                    turned(6 * pp + w, v_nat[:, w * WIN:(w + 1) * WIN], ((s_av, NS * pp), (s_vout, 16 * pp), (s_cp, 5 * pp)))

            def window_recurrence(p, w12):
                c, w = divmod(w12, 3)
                if w == 0:
                    split_weights(4 + 8 * p + c + 1)

            def turn_recurrence(p, w12):
                c, w = divmod(w12, 3)
                if c == 2:
                    turned(6 * p + 3 + w, i_nat[:, w * WIN:(w + 1) * WIN], ((s_h3, NT * p), (s_im, NT * p)))

            def gated_low(t):
                dve.wait_ge(s_gh, t + 1)
                r = graw[:, ROW_OF[t], :]
                V.tensor_tensor(gl[:, ROW_OF[t], :], r, gh[:, ROW_OF[t], :].bitcast(F32), ALU.subtract).then_inc(s_gl, 1)

            for r in range(1, 4):
                dve.wait_ge(s_xsq, r + 1)
                need(dve, s_xsa, r - 1)
                V.tensor_tensor(xsa[:, :, :], xsa[:, :, :], xsq[r % 2][:, :, :], ALU.add).then_inc(s_xsa, 1)
            dve.wait_ge(s_c, 32)
            V.memset(qbd[:, :, :, :], 0.0).then_inc(s_qz, 1)
            V.tensor_scalar(ngate[:, :], bgate, -1.0, None, ALU.mult)
            V.tensor_tensor(lbv[:, 0, :], lbraw[:, 0:4], lbraw[:, 4:8], ALU.max).then_inc(s_lb, 1)
            dve.wait_ge(s_lb, 1)
            for r in range(2):
                V.tensor_tensor(lbv[:, 1 + r, :], lbraw[:, 4 * r:4 * r + 4], lbv[:, 0, :], ALU.subtract).then_inc(s_lb, 1)
            dve.wait_ge(s_lbe, 1)
            V.tensor_tensor(lbv[:, 3, :], lbv[:, 1, :], lbv[:, 2, :], ALU.add).then_inc(s_lb, 1)
            dve.wait_ge(s_lb, 4)
            V.reciprocal(lbv[:, 3, :], lbv[:, 3, :]).then_inc(s_lb, 1)
            dve.wait_ge(s_lb, 5)
            V.tensor_tensor(lbv[:, 4, :], lbv[:, 2, :], lbv[:, 3, :], ALU.mult).then_inc(s_lb, 1)
            split_weights(0)
            V.tensor_copy(negtri_r[:, :], negtri).then_inc(s_cr, 1)
            V.tensor_copy(negones_r[:, :], negones).then_inc(s_cr, 1)
            for w in range(NW):
                def low(r):
                    dve.wait_ge(s_xhi, 4 * w + r + 1)
                    t, cols = slice(2 * r, 2 * r + 2), slice(w * WIN, (w + 1) * WIN)
                    V.tensor_tensor(xl[:, t, cols], xw[w][:, t, :], xh[:, t, cols].bitcast(F32), ALU.subtract).then_inc(s_xlo, 1)

                dve.wait_ge(s_xrs, w + 1)
                for k in range(KT_N):
                    V.scalar_tensor_tensor(xw[w][:, k, :], xw[w][:, k, :], gpre[:, k:k + 1], xrs[:, 0:WIN],
                                           ALU.mult, ALU.mult).then_inc(s_xn, 1)
                    if k in (3, 5, 7):
                        low((k - 3) // 2)
                low(3)
                if w == 0:
                    split_weights(1)
            for w12 in range(12):
                if w12 >= 3:
                    window_attention(0, w12)
                if w12:
                    turn_attention(0, w12 - 1)
                if w12 in (8, 10):
                    low_parts(0, w12 // 2 - 4)
            turn_attention(0, 11)

            for p in range(PAIRS):
                recurrence_over(dve, p - 1, norm=False)
                late = []
                for n in range(B_STEPS):
                    if n < NS:
                        c0, t = first_col(n), NS * p + n
                        h, q, e = STEPS[n][2], tile_rank(n), E[n % 3]
                        dve.wait_ge(s_L, t + 1)
                        i = V.scalar_tensor_tensor(e[:, c0:QW], e[:, c0:QW], 88.0, Z[n % 3][:, c0:QW], ALU.min, ALU.max)
                        if diagonal(n):
                            i.then_inc(s_sp1, 1)
                            dve.wait_ge(s_sp1, DIAGS * p + diagonals_until(n))
                            V.tensor_tensor(e[:, c0:c0 + P], e[:, c0:c0 + P], causal, ALU.mult).then_inc(s_sp, 1)
                        else:
                            i.then_inc(s_sp, 1)
                        if q > 0:
                            dve.wait_ge(s_sp, t + 1)
                            need(dve, s_cum, t - 1)
                            V.tensor_copy(SPH[n % 2][:, c0:QW], e[:, c0:QW]).then_inc(s_sph, 1)
                            dve.wait_ge(s_sph, SPLITS * p + rows_until(n))
                            V.tensor_tensor(SPL[n % 2][:, c0:QW], e[:, c0:QW], SPH[n % 2][:, c0:QW].bitcast(F32),
                                            ALU.subtract).then_inc(s_spl, 1)
                        if q > 1:
                            cs = first_col(n - 2)
                            dve.wait_ge(s_S, SUMS * p + sums_until(n - 2))
                            V.tensor_copy(SUH[h][:, cs:QW], SUM[h][:, cs:QW]).then_inc(s_Sh, 1)
                            dve.wait_ge(s_Sh, SUM_SPLITS * p + sum_rows_until(n))
                            V.tensor_tensor(SUL[h][:, cs:QW], SUM[h][:, cs:QW], SUH[h][:, cs:QW].bitcast(F32),
                                            ALU.subtract).then_inc(s_Sl, 1)
                    if n >= 2:
                        wd, j, h = STEPS[n - 2]
                        if j == 0 and h == 1:
                            dve.wait_ge(s_silu, 6 * p + 3)
                            dve.wait_ge(s_av, NS * p + n - 1)
                            V.tensor_tensor(zA[:, wd * QW:(wd + 1) * QW], OB[:, :], zA[:, wd * QW:(wd + 1) * QW],
                                            ALU.mult).then_inc(s_gA, 1)
                    if n == 12:
                        dve.wait_ge(s_te, 6 * p + 3)
                        dve.wait_ge(s_silu, 6 * p + 3)
                        dve.wait_ge(s_ev, win_of(8 * p if p else 0) + 12)
                        need(dve, s_zs, 3 * p)
                        need(dve, s_os, p)
                        need(dve, s_spA, 32 * p)
                        dve.wait_ge(s_qz, 1)
                        for h in range(2):
                            r = slice(DH * h, DH * h + DH)
                            V.tensor_copy(qbd[r, :, h, :], qT[r, SEQ:TOK].rearrange("d (i t) -> d i t", t=DSEQ)).then_inc(s_cp, 1)
                        V.tensor_copy(kTs[:, :], kT[:, SEQ:TOK]).then_inc(s_cp, 1)
                        V.tensor_copy(vs[:, :], v_nat[:, SEQ:TOK]).then_inc(s_cp, 1)
                        V.tensor_copy(zAs[:, :], zA[:, SEQ:TOK]).then_inc(s_cp, 1)
                    for w12 in late:
                        turn_recurrence(p, w12)
                    late = ended(B_PIECES[n])
                    for w12 in late:
                        window_recurrence(p, w12)
                for w12 in late:
                    turn_recurrence(p, w12)

                attention_over(dve, p)
                late = []
                for m in range(A_STEPS):
                    if m == 0:
                        dve.wait_ge(s_zs, 3 * (p + 1))
                        need(dve, s_so, 16 * p)
                        V.memset(St[0][:, :], 0.0).then_inc(s_S0, 1)
                        dve.wait_ge(s_lf, 3 * (p + 1))
                        for c in range(NT):
                            cols = slice(c * P, (c + 1) * P)
                            V.tensor_tensor_scan(lf[:, cols], reset if c < 8 else reset_s, lf[:, cols], 0.0,
                                                 ALU.mult, ALU.add).then_inc(s_scan, 1)
                        dve.wait_ge(s_scan, NT * (p + 1))
                        bp = lf[:, 0:SEQ].rearrange("c (n t) -> c n t", t=BLK)
                        bs = lf[:, SEQ:TOK].rearrange("c (n t) -> c n t", t=DSEQ)
                        V.tensor_copy(bm[:, 0:NBLK], bp[:, :, BLK // 2 - 1]).then_inc(s_bmc, 1)
                        V.tensor_copy(bm[:, NBLK:], bs[:, :, DSEQ // 2 - 1]).then_inc(s_bmc, 1)
                        V.tensor_copy(be[:, 0:NBLK], bp[:, :, BLK - 1]).then_inc(s_bmc, 1)
                        V.tensor_copy(be[:, NBLK:], bs[:, :, DSEQ - 1]).then_inc(s_bmc, 1)
                        dve.wait_ge(s_bmc, 4 * (p + 1))
                        V.tensor_tensor(bp, bp, bm[:, 0:NBLK, None].broadcast_to([P, NBLK, BLK]), ALU.subtract).then_inc(s_A, 1)
                        V.tensor_tensor(bs, bs, bm[:, NBLK:, None].broadcast_to([P, STREAMS, DSEQ]), ALU.subtract).then_inc(s_A, 1)
                        V.tensor_tensor(be[:, :], be[:, :], bm[:, :], ALU.subtract).then_inc(s_ge, 1)
                        dve.wait_ge(s_ge, 2 * p + 1)
                        V.tensor_tensor(be[:, 0:NBLK - 1], be[:, 0:NBLK - 1], bm[:, 1:NBLK], ALU.add).then_inc(s_ge, 1)
                        for r, (bk, lo, n) in enumerate(((Z[2], 4, 1), (Z[1], 2, 2), (Z[0], 0, 2))):
                            dve.wait_ge(s_Ls, 3 * p + r + 1)
                            V.scalar_tensor_tensor(SPs[:, lo:lo + n, :].rearrange("s j c -> s (j c)"),
                                                   Es[:, lo:lo + n, :].rearrange("s j c -> s (j c)"), 88.0, bk[:, 0:256 * n],
                                                   ALU.min, ALU.max).then_inc(s_sps, 1)
                            if r == 0:
                                dve.wait_ge(s_sps, 3 * p + 1)
                                V.tensor_tensor(SPs[:, 4, :], SPs[:, 4, :], smask, ALU.mult).then_inc(s_spm, 1)
                    if m == 1:
                        dve.wait_ge(s_as, 3 * p + 1)
                        V.tensor_tensor(Es[:, 4, :], Es[:, 4, :], smask, ALU.mult).then_inc(s_asm, 1)
                        dve.wait_ge(s_EX, 4 * (p + 1))
                        V.tensor_tensor(kb[:, :], kb[:, :], EK[:, :], ALU.mult).then_inc(s_hki, 1)
                        dve.wait_ge(s_hki, p + 1)
                        V.tensor_tensor(lf[:, 0:SEQ].rearrange("c (n t) -> c n t", t=BLK), kb[:, 0:SEQ].rearrange("c (n t) -> c n t", t=BLK),
                                        gg[:, 0:NBLK, None].broadcast_to([P, NBLK, BLK]), ALU.mult).then_inc(s_hke, 1)
                        V.tensor_tensor(lf[:, SEQ:TOK].rearrange("c (n t) -> c n t", t=DSEQ), kb[:, SEQ:TOK].rearrange("c (n t) -> c n t", t=DSEQ),
                                        gg[:, NBLK:, None].broadcast_to([P, STREAMS, DSEQ]), ALU.mult).then_inc(s_hke, 1)
                    if m == 2:
                        dve.wait_ge(s_os, p + 1)
                        dve.wait_ge(s_cp, 5 * (p + 1))
                        ob = OB[:, 0:256].rearrange("d (i h t) -> d i h t", h=2, t=DSEQ)
                        for h in range(2):
                            r = slice(DH * h, DH * h + DH)
                            z = zAs[r, :].rearrange("d (i t) -> d i t", t=DSEQ)
                            V.tensor_tensor(z, ob[r, :, h, :], z, ALU.mult).then_inc(s_gs, 1)
                        dve.wait_ge(s_S0l, 16 * (p + 1))
                        V.tensor_tensor(S0s[:, :, :], S0s[:, :, :], em[:, :, None].broadcast_to([P, STREAMS, P]), ALU.mult).then_inc(s_S0m, 1)
                    if m >= 3:
                        c = m - 3
                        if c < NT:
                            dve.wait_ge(s_at, NT * p + c + 1)
                            if c >= 2:
                                dve.wait_ge(s_h3, NT * p + c - 1)
                            V.scalar_tensor_tensor(attm[c % 2][:, :], Z[2][:, 0:P], BIG, hgmask if c < 8 else hgmask_s,
                                                   ALU.min, ALU.mult).then_inc(s_atm, 1)
                        if 1 <= c <= 8:
                            b = c - 1
                            dve.wait_ge(s_KV, NT * p + b + 1)
                            if b == 0:
                                dve.wait_ge(s_S0, p + 1)
                            for s in range(4):
                                n = 4 * b + s
                                need(dve, s_ch, NBLK * p + n)
                                if n >= 7:
                                    dve.wait_ge(s_h3, NT * p + (n - 7) // 4 + 1)
                                V.scalar_tensor_tensor(St[(n + 1) % 8][:, :], St[n % 8][:, :], gg[:, n:n + 1],
                                                       Z[b % 2][:, s * P:(s + 1) * P], ALU.mult, ALU.add).then_inc(s_ch, 1)
                        if c == NT + 1:
                            dve.wait_ge(s_h3, NT * (p + 1))
                            V.tensor_tensor(S0s[:, :, :], S0s[:, :, :], gg[:, NBLK:, None].broadcast_to([P, STREAMS, P]),
                                            ALU.mult).then_inc(s_ss1, 1)
                            dve.wait_ge(s_ss1, p + 1)
                            dve.wait_ge(s_KV, NT * (p + 1))
                            for half in range(2):
                                s = S0s[:, 4 * half:4 * half + 4, :].rearrange("c i v -> c (i v)")
                                V.tensor_tensor(s, Z[half][:, :], s, ALU.add).then_inc(s_ss, 1)
                        if c in MS_STEP:
                            g = MS_STEP.index(c)
                            t0, t1 = GROUPS[g]
                            n = P * (t1 - t0)
                            dve.wait_ge(s_hr, 3 * p + g + 1)
                            V.tensor_tensor(oc[:, 0:n], oc[:, 0:n], hrs[:, 0:n], ALU.mult).then_inc(s_hg1, 1)
                            dve.wait_ge(s_hg1, 3 * p + g + 1)
                            dve.wait_ge(s_silu, 6 * p + 6)
                            V.scalar_tensor_tensor(zB[:, t0 * P:t1 * P], oc[:, 0:n], hgn[:, p:p + 1], zB[:, t0 * P:t1 * P],
                                                   ALU.mult, ALU.mult).then_inc(s_hg, 1)
                    if p + 1 < PAIRS and m in STACK_STEPS[1:]:
                        low_parts(p + 1, STACK_STEPS.index(m) - 1)
                    if p + 1 < PAIRS:
                        for w12 in late:
                            turn_attention(p + 1, w12)
                        late = ended(A_PIECES[m])
                        for w12 in late:
                            window_attention(p + 1, w12)
                    else:
                        for w12 in ended(A_PIECES[m]):
                            if w12 % 3 == 0:
                                split_weights(32 + w12 // 3 + 1)
                        if m in (7, 9, 11):
                            gated_low((m - 7) // 2)
                if p + 1 < PAIRS:
                    for w12 in late:
                        turn_attention(p + 1, w12)

            def products(dm, w):
                n = 3 * dm + w
                cols = slice(w * WIN, (w + 1) * WIN)
                dve.wait_ge(s_u, n + 1)
                dve.wait_ge(s_sig, 6 * dm + 3 + w + 1)
                a, b = slots[dm][:, cols], slots[GATE_B_SLOT[dm]][:, cols]
                V.tensor_tensor(a, UA[n % 2][:, 0:WIN], a, ALU.mult).then_inc(s_ma, 1)
                V.tensor_tensor(b, UB[n % 2][:, 0:WIN], b, ALU.mult).then_inc(s_mb, 1)

            def merged_low(dm, cols=slice(0, TOK), n=None):
                dve.wait_ge(s_mh, dm + 1 if n is None else n)
                V.tensor_tensor(xl[:, dm, cols], slots[dm][:, cols], xh[:, dm, cols].bitcast(F32), ALU.subtract).then_inc(s_ml, 1)

            for g in range(GATE_G0 + 4, OUT_G0):
                what, dm, kind = MERGE[g - GATE_G0]
                for w in range(NW):
                    if what == "branch":
                        if dm == 7:
                            merged_low(2 * w)
                            merged_low(2 * w + 1)
                        products(dm, w)
                    if w == 0:
                        split_weights(g + 1)
                    if dm == 2 and what == "gate":
                        for t in ((3, 4), (5,), (6,), (7,), (), ())[3 * kind + w]:
                            gated_low(t)
            merged_low(6)
            for w in range(NW):
                merged_low(7, slice(w * WIN, (w + 1) * WIN), 8 + w)
            dve.wait_ge(s_u, 24)
            V.memset(no4[:, :], -1.0).then_inc(s_no, 1)
            for k in range(KT_N - 1):
                dve.wait_ge(s_win, OUT_W0 + 3 * k + 1)
                split_weights(OUT_G0 + k + 1)
            for w in range(NW):
                y, x = yb[:, 0:5, w * WIN:(w + 1) * WIN], xres[:, 0:5, w * WIN:(w + 1) * WIN]
                dve.wait_ge(s_yr, w + 1)
                dve.wait_ge(s_ev, OUT_W0 + 3 * (KT_N - 1) + w + 1)
                for lo, hi in ((0, 4), (4, 5)):
                    V.tensor_tensor(y[:, lo:hi, :], y[:, lo:hi, :], yrs[w][:, None, :].broadcast_to([P, hi - lo, WIN]),
                                    ALU.mult).then_inc(s_yg, 1)
                    dve.wait_ge(s_yg, 2 * w + (1 if lo == 0 else 2))
                    if w == 0:
                        dve.wait_ge(s_xr, 16)
                    if lo:
                        dve.wait_ge(s_yo3, w + 1)
                    V.tensor_tensor(y[:, lo:hi, :], y[:, lo:hi, :], x[:, lo:hi, :], ALU.add).then_inc(s_yo, 1)

        @block.gpsimd
        def _(pool):
            G = nc.gpsimd

            def silu_product(n, idx, half, z):
                pool.wait_ge(s_sg, half + 1)
                pool.wait_ge(s_ev, n + 1)
                G.tensor_tensor(z, z, tmpT[idx % 2][:, :], ALU.mult).then_inc(s_silu, 1)

            def window_attention(pp, w12):
                c, w = divmod(w12, 3)
                if c == 3:
                    silu_product(win_of(8 * pp if pp else 0) + w12, 12 * pp + 3 + w, 6 * pp + w, zA[:, w * WIN:(w + 1) * WIN])

            def window_recurrence(p, w12):
                c, w = divmod(w12, 3)
                if c == 3:
                    silu_product(win_of(4 + 8 * p) + w12, 12 * p + 9 + w, 6 * p + 3 + w, zB[:, w * WIN:(w + 1) * WIN])

            for m in range(3, 3 * NW):
                w, r = m // 3, m % 3 + 1
                pool.wait_ge(s_xsq, 4 * w + r + 1)
                pool.wait_ge(s_xsa, m)
                G.tensor_tensor(xsa[:, :, :], xsa[:, :, :], xsq[(3 * w + r) % 2][:, :, :], ALU.add).then_inc(s_xsa, 1)
            for w12 in range(12):
                window_attention(0, w12)
            for p in range(PAIRS):
                recurrence_over(pool, p - 1, norm=False)
                for n in range(B_STEPS):
                    if n < NS and STEPS[n][1] > 0:
                        h, q = STEPS[n][2], tile_rank(n)
                        c0, t = first_col(n), NS * p + n
                        src, dst = E[n % 3], SUM[h]
                        pool.wait_ge(s_sp, t + 1)
                        if q == 1:
                            pool.wait_ge(s_cum, t + 1)
                        else:
                            need(pool, s_Sl, SUM_SPLITS * p + sum_rows_until(n))
                        if q == 0:
                            G.tensor_copy(dst[:, c0:QW], src[:, c0:QW]).then_inc(s_S, 1)
                        else:
                            pool.wait_ge(s_S, SUMS * p + sums_until(n - 2))
                            lo = first_col(n - 2)
                            if lo > c0:
                                G.tensor_copy(dst[:, c0:lo], src[:, c0:lo])
                            G.tensor_tensor(dst[:, lo:QW], dst[:, lo:QW], src[:, lo:QW], ALU.add).then_inc(s_S, 1)
                    if 1 <= n <= NS and diagonal(n - 1):
                        m = n - 1
                        c0 = first_col(m)
                        pool.wait_ge(s_a, NS * p + m + 1)
                        G.tensor_tensor(Aw[m % 2][:, c0:c0 + P], Aw[m % 2][:, c0:c0 + P], causal, ALU.mult).then_inc(s_am, 1)
                    for w12 in ended(B_PIECES[n]):
                        window_recurrence(p, w12)
                attention_over(pool, p)
                for m in range(A_STEPS):
                    if m == 0:
                        pool.wait_ge(s_spm, p + 1)
                        for q, j in enumerate((3, 2, 1)):
                            if q == 0:
                                pool.wait_ge(s_sps, 3 * p + 2)
                                last = SPs[:, 4, :]
                            else:
                                pool.wait_ge(s_sps, 3 * p + (2 if j >= 2 else 3))
                                pool.wait_ge(s_Ss, 3 * p + q)
                                last = SUs[:, q - 1, :]
                            G.tensor_tensor(SUs[:, q, :], last, SPs[:, j, :], ALU.add).then_inc(s_Ss, 1)
                    if m == 1:
                        pool.wait_ge(s_EX, 4 * (p + 1))
                        G.tensor_tensor(hq[:, :], hq[:, :], EQ[:, :], ALU.mult).then_inc(s_hqd, 1)
                    if 2 <= m < NT + 2:
                        c = m - 2
                        blocks, rows = (4, rows4) if c < 8 else (8, rows8)
                        if c == 0:
                            pool.wait_ge(s_te, 6 * (p + 1))
                            pool.wait_ge(s_zs, 3 * (p + 1))
                        if c >= 2:
                            pool.wait_ge(s_KV, NT * p + (c - 1 if c < 8 else 8))
                        b0 = 4 * (c % 2)
                        G.tensor_tensor(imask[:, b0:b0 + blocks, :],
                                        i_nat[:, None, c * P:(c + 1) * P].broadcast_to([P, blocks, P]),
                                        rows[:, :, None].broadcast_to([P, blocks, P]), ALU.mult).then_inc(s_im, 1)
                    if p + 1 < PAIRS:
                        for w12 in ended(A_PIECES[m]):
                            window_attention(p + 1, w12)
            for dm in range(8):
                for w in range(NW):
                    cols = slice(w * WIN, (w + 1) * WIN)
                    pool.wait_ge(s_mb, 3 * dm + w + 1)
                    pool.wait_ge(s_ma, 3 * dm + w + 1)
                    G.tensor_tensor(slots[dm][:, cols], slots[dm][:, cols], slots[GATE_B_SLOT[dm]][:, cols], ALU.add).then_inc(s_mg, 1)
            for n in range(3, 3 * (KT_N - 1)):
                w = n % 3
                pool.wait_ge(s_yq, n + 1)
                need(pool, s_ya, n - 5)
                G.tensor_tensor(ysa[w][:, :], ysa[w][:, :], ysq[w][:, :], ALU.add).then_inc(s_ya, 1)
            pool.wait_ge(s_xr, 16)
            for w in range(NW):
                y, x = yb[:, 5:8, w * WIN:(w + 1) * WIN], xres[:, 5:8, w * WIN:(w + 1) * WIN]
                pool.wait_ge(s_yr, w + 1)
                pool.wait_ge(s_ev, OUT_W0 + 3 * (KT_N - 1) + w + 1)
                G.tensor_tensor(y, y, yrs[w][:, None, :].broadcast_to([P, 3, WIN]), ALU.mult).then_inc(s_yg3, 1)
                pool.wait_ge(s_yg3, w + 1)
                G.tensor_tensor(y, y, x, ALU.add).then_inc(s_yo3, 1)


def constants():
    c2 = np.zeros((P, C2_W), np.float32)
    s, t = np.arange(P)[:, None], np.arange(P)[None, :]

    def put(name, value):
        o, n = C2[name]
        c2[:, o:o + n] = value

    put("negtri", -(s >= t).astype(np.float32))
    put("negones", -1.0)
    put("causal", s < t)
    put("hgmask", (s <= t) & (s // BLK == t // BLK))
    put("hgmask_s", (s <= t) & (s // DSEQ == t // DSEQ))
    col = np.arange(256)[None, :]
    put("smask", (s // DSEQ == col // 32) & (s % DSEQ < col % DSEQ))
    put("reset", np.broadcast_to(t % BLK != 0, (P, P)))
    put("reset_s", np.broadcast_to(t % DSEQ != 0, (P, P)))
    put("rows4", s // BLK == np.arange(4)[None, :])
    put("rows8", s // DSEQ == np.arange(8)[None, :])
    return c2


def chunk_weights(w_in, wa, wb, w_out):
    def cols(m, c):
        return m[:, c * P:(c + 1) * P].reshape(KT_N, P, P).transpose(1, 0, 2).reshape(P, KT_N * P)

    def w_in_chunk(group, p):
        return cols(w_in, 4 * group + p)

    out = []

    def attention(p):
        out.extend(w_in_chunk(g, p) for g in (0, 1, 2, 3))

    def gates(dm):
        out.extend((cols(w_in, 32 + dm), cols(w_in, 40 + dm)))

    branches = np.concatenate([wa, wb], axis=0)
    attention(0)
    for p in range(PAIRS):
        out.extend(w_in_chunk(g, p) for g in (4, 5, 6, 7))
        if p + 1 < PAIRS:
            attention(p + 1)
        else:
            for dm in range(3):
                gates(dm)
    out.extend(cols(branches, dm) for dm in range(3))
    for dm in range(3, 8):
        gates(dm)
        out.append(cols(branches, dm))
    out.extend(cols(w_out, n) for n in range(8))
    return np.ascontiguousarray(np.stack(out))


def kernel(x_prompt, x_sample, cache_sb_k, cache_sb_v, state_hgrn, g_pre, w_in, b_gate, hg_lb_raw, hg_norm_g,
           w_branch_a, w_branch_b, w_out, g_post):
    import concourse.bacc as bacc
    from concourse.bass_utils import run_bass_kernel_spmd

    x = np.concatenate([np.asarray(x_prompt)[0], np.asarray(x_sample).reshape(-1, D)], axis=0)
    c1 = np.zeros((P, C1_W), np.float32)
    for name, value in (("ident", np.eye(P, dtype=np.float32)), ("bgate", np.asarray(b_gate)[0].reshape(16, P).T),
                        ("lbraw", np.asarray(hg_lb_raw).reshape(8, P).T), ("hgn", np.asarray(hg_norm_g)[0].T),
                        ("gpre", np.asarray(g_pre)[0].reshape(8, P).T), ("gpost", np.asarray(g_post)[0].reshape(8, P).T),
                        ("eps", np.float32(EPS))):
        o, n = C1[name]
        c1[:, o:o + n] = value
    ck = np.asarray(cache_sb_k)[0].reshape(STREAMS, PAST, PAIRS, P)
    cv = np.asarray(cache_sb_v)[0].reshape(STREAMS, PAST // P, P, PAIRS, P)
    arrays = {
        "xT": x.reshape(TOK, KT_N, P).transpose(2, 1, 0),
        "wch": chunk_weights(np.asarray(w_in)[0], np.asarray(w_branch_a)[0], np.asarray(w_branch_b)[0], np.asarray(w_out)[0]),
        "ckT": ck.transpose(2, 0, 3, 1),
        "cv": cv.transpose(3, 0, 2, 1, 4).reshape(PAIRS, STREAMS, P, 4 * P),
        "st": np.asarray(state_hgrn)[0].transpose(1, 0, 2, 3),
        "c1": c1,
        "c2": constants(),
    }
    arrays = {k: np.ascontiguousarray(v) for k, v in arrays.items()}
    outs = {"yT": (P, KT_N, TOK), "okT": (PAIRS, P, TOK), "ov": (PAIRS, TOK, P), "osp": (PAIRS, P, P),
            "oss": (PAIRS, STREAMS, P, P)}
    nc = bacc.Bacc("TRN2", target_bir_lowering=False, num_devices=1)
    args = [nc.dram_tensor(k, v.shape, F32, kind="ExternalInput").ap() for k, v in arrays.items()]
    args += [nc.dram_tensor(k, s, F32, kind="ExternalOutput").ap() for k, s in outs.items()]
    spill = nc.dram_tensor("gated", (2 * PAIRS, P, TOK), F32, kind="Internal").ap()
    build(nc, *args, spill)
    r = run_bass_kernel_spmd(nc, [arrays], core_ids=[0]).results[0]
    y = np.asarray(r["yT"]).transpose(2, 1, 0).reshape(TOK, D)
    k = np.asarray(r["okT"]).transpose(2, 0, 1).reshape(TOK, 8, DH)
    v = np.asarray(r["ov"]).transpose(1, 0, 2).reshape(TOK, 8, DH)
    c = np.ascontiguousarray
    return (c(y[None, :SEQ]), c(y[SEQ:].reshape(STREAMS, DSEQ, D)),
            c(k[None, None, :SEQ]), c(v[None, None, :SEQ]), c(np.asarray(r["osp"])[None, None]),
            c(k[SEQ:].reshape(1, STREAMS, DSEQ, 8, DH)), c(v[SEQ:].reshape(1, STREAMS, DSEQ, 8, DH)),
            c(np.asarray(r["oss"]).transpose(1, 0, 2, 3)[None]))
```

```python
from contextlib import ExitStack

import numpy as np

import concourse.bass as bass
from concourse import mybir

F32 = mybir.dt.float32
F32R = mybir.dt.float32r
ALU = mybir.AluOpType
ACT = mybir.ActivationFunctionType

P = 128
D = 1024
SEQ, STREAMS, DSEQ, PAST = 1024, 8, 16, 512
TOK = SEQ + STREAMS * DSEQ
WIN = 384
NW = TOK // WIN
KT_N = D // P
PAIRS = 4
DH = 64
QW = 512
NS = 24
PIECES = 3
EPS = 1e-6
BIG = 3.0e38
BLK = 32
NBLK = SEQ // BLK
NT = TOK // P

GATE_G0 = 4 * 2 * PAIRS
OUT_G0 = GATE_G0 + 3 * 8
OUT_W0 = 3 * (GATE_G0 + 2 * 8)

C1 = {"ident": (0, 128), "bgate": (128, 16), "lbraw": (144, 8), "hgn": (152, 4), "gpre": (156, 8), "gpost": (164, 8),
      "eps": (172, 1)}
C1_W = 173
C2 = {"negtri": (0, 128), "negones": (128, 128), "causal": (256, 128), "hgmask": (384, 128), "hgmask_s": (512, 128),
      "smask": (640, 256), "reset": (896, 128), "reset_s": (1024, 128), "rows4": (1152, 4), "rows8": (1156, 8)}
C2_W = 1164


def attention_steps():
    return [(wd, j, h) for wd in range(SEQ // QW) for j in range(4 * wd + 3, -1, -1) for h in range(2)]


STEPS = attention_steps()
assert len(STEPS) == NS


def diagonal(n):
    wd, j, _ = STEPS[n]
    return j >= 4 * wd


def first_col(n):
    wd, j, _ = STEPS[n]
    return P * max(j - 4 * wd, 0)


def diagonals_until(n):
    return sum(diagonal(i) for i in range(n + 1))


DIAGS = diagonals_until(NS - 1)


def sums_until(n):
    return sum(STEPS[i][1] > 0 for i in range(n + 1))


SUMS = sums_until(NS - 1)


def spread(weights, total):
    out, acc, done = [], 0.0, 0
    for w in weights:
        acc += w
        upto = int(round(total * acc / sum(weights)))
        out.append(list(range(done, upto)))
        done = upto
    return out


B_STEPS = NS + 3
B_PIECES = spread([700 if n < 2 else max(QW - first_col(n), 300) if n < NS else 400 for n in range(B_STEPS)], 12 * PIECES)
A_STEPS = 3 + NT + 3
A_PIECES = spread([5, 4, 4] + [2] * (A_STEPS - 3), 12 * PIECES)


def ended(pieces):
    return [x // PIECES for x in pieces if x % PIECES == PIECES - 1]


MERGE = [("gate", dm, kind) for dm in range(3) for kind in range(2)] + [("branch", dm, 0) for dm in range(3)]
for _dm in range(3, 8):
    MERGE += [("gate", _dm, 0), ("gate", _dm, 1), ("branch", _dm, 0)]


def gate_window_no(dm, kind, w):
    return 3 * GATE_G0 + 6 * dm + 3 * kind + w


def win_of(g):
    if g < GATE_G0:
        return 3 * g
    if g >= OUT_G0:
        return OUT_W0 + 3 * (g - OUT_G0)
    what, dm, kind = MERGE[g - GATE_G0]
    assert what == "gate"
    return gate_window_no(dm, kind, 0)


GATE_B_SLOT = (8, 7, 6, 8, 7, 8, 7, 8)


def slot_user_before(dm, kind):
    slot = dm if kind == 0 else GATE_B_SLOT[dm]
    return max([d for d in range(dm) if GATE_B_SLOT[d] == slot], default=-1)


ROW_OF = (4, 5, 6, 3, 0, 1, 2, 7)


def prologue_window(i):
    return (i % 2, i // 2) if i < 6 else (i // 3, i % 3)


def output_product(n):
    return divmod(n, 3) if n < 18 else (6 + n % 2, (n - 18) // 2)


def tile_rank(n):
    wd, j, _ = STEPS[n]
    return 4 * wd + 3 - j


def rows_until(n):
    return sum(tile_rank(i) > 0 for i in range(n + 1))


def sum_rows_until(n):
    return sum(tile_rank(i) > 1 for i in range(n + 1))


SPLITS, SUM_SPLITS = rows_until(NS - 1), sum_rows_until(NS - 1)


GROUPS = ((0, 4), (4, 8), (8, 9))
OUT_STEP = (5, 9, 10)
MS_STEP = (6, 10, 11)
STACK_STEPS = (9, 10, 11)
RELOAD_STEPS = (7, 9, 11)


def build(nc, xT, wch, ckT, cv, st, c1, c2, yT, okT, ov, osp, oss, spill):
    with ExitStack() as ctx:
        off = [0]
        base = nc.sbuf_base + (-nc.sbuf_base) % 32
        ctx.enter_context(nc.sbuf_tensor("arena", [P, (nc.sbuf_usable_end - base) // 4 - 16], F32))
        limit = (nc.sbuf_usable_end - base) - 64

        def at(name, shape, dt, offset):
            size = 4 * int(np.prod(shape[1:]))
            assert offset + size <= limit, (name, offset + size, limit)
            return nc.alloc_sbuf_tensor_at(name, shape, dt, offset=base + offset)

        def take(name, shape, dt=F32):
            o = off[0]
            off[0] += 4 * int(np.prod(shape[1:]))
            off[0] += (-off[0]) % 32
            return at(name, shape, dt, o), o

        def over(offset):
            o = [offset]

            def place(name, shape, dt=F32):
                t = at(name, shape, dt, o[0])
                o[0] += 4 * int(np.prod(shape[1:]))
                return t
            return place

        def sem(name):
            return ctx.enter_context(nc.semaphore(name))

        xh, _ = take("xh", [P, KT_N, TOK], F32R)
        xl, _ = take("xl", [P, KT_N, TOK], F32R)
        wr, wl, wh = [], [], []
        for i in range(3):
            t, o = take(f"wr{i}", [P, KT_N, P])
            wr.append(t)
            wl.append(at(f"wl{i}", [P, KT_N, P], F32R, o))
        for i in range(2):
            wh.append(take(f"wh{i}", [P, KT_N, P], F32R)[0])
        k1, _ = take("k1", [P, C1_W])
        lbv, _ = take("lbv", [P, 5, 4])
        ngate, _ = take("ngate", [P, 16])
        slot_order = (0, 1, 7, 8, 2, 3, 4, 5, 6)
        stage, slots = [], {}
        for name, m in zip(("qT", "kT", "zA", "v_nat", "hq", "kb", "lf", "i_nat", "zB"), slot_order):
            t, o = take(name, [P, TOK])
            stage.append(t)
            slots[m] = at(f"slot{m}", [P, TOK], F32, o)
            if m == 0:
                slots_base = o
        qT, kT, zA, v_nat, hq, kb, lf, i_nat, zB = stage
        qlo = at("qlo", [P, TOK], F32R, slots_base)
        xres = at("xres", [P, KT_N, TOK], F32, slots_base)
        work = off[0]
        KT_, kt_o = take("KTc", [P, STREAMS, PAST])
        V_, v_o = take("Vc", [P, STREAMS, 4, P])
        KS = [at(f"KS{h}", [P, SEQ], F32R, v_o + 4 * SEQ * h) for h in range(2)]
        QS = [at(f"QS{h}", [P, SEQ], F32R, v_o + 4 * SEQ * (2 + h)) for h in range(2)]
        k2, _ = take("k2", [P, C2_W])
        qbd, _ = take("qbd", [P, STREAMS, 2, DSEQ])
        kTs, _ = take("kTs", [P, P])
        vs, _ = take("vs", [P, P])
        zAs, _ = take("zAs", [P, P])
        tmpT = [take(f"tmpT{i}", [P, WIN])[0] for i in range(2)]
        negtri_r, _ = take("negtri_r", [P, P], F32R)
        negones_r, _ = take("negones_r", [P, P], F32R)
        bm, _ = take("bm", [P, NBLK + STREAMS])
        be, _ = take("be", [P, NBLK + STREAMS])
        gg, _ = take("gg", [P, NBLK + STREAMS])
        em, _ = take("em", [P, STREAMS])
        bt_o = off[0]
        E = [take(f"E{i}", [P, QW])[0] for i in range(3)]
        SPH = [take(f"SPH{i}", [P, QW], F32R)[0] for i in range(2)]
        SPL = [take(f"SPL{i}", [P, QW], F32R)[0] for i in range(2)]
        SUM = [take(f"SUM{h}", [P, QW])[0] for h in range(2)]
        SUH = [take(f"SUH{h}", [P, QW], F32R)[0] for h in range(2)]
        SUL = [take(f"SUL{h}", [P, QW], F32R)[0] for h in range(2)]
        aw_o = off[0]
        Aw = [take(f"Aw{i}", [P, QW])[0] for i in range(2)]
        hrs_s, _ = take("hrs_s", [P, P])
        place = over(bt_o)
        Es = place("Es", [P, 5, 256])
        SPs = place("SPs", [P, 5, 256])
        SUs = place("SUs", [P, 3, 256])
        EK = place("EK", [P, TOK])
        EQ = place("EQ", [P, TOK])
        SPsH = place("SPsH", [P, 5, 256], F32R)
        SUsH = place("SUsH", [P, 3, 256], F32R)
        place = over(bt_o + 4 * 5 * 256)
        SPsL = place("SPsL", [P, 5, 256], F32R)
        SUsL = place("SUsL", [P, 3, 256], F32R)
        place = over(kt_o)
        St = [place(f"St{i}", [P, P]) for i in range(8)]
        kendH = [place(f"kendH{i}", [P, P], F32R) for i in range(2)]
        oc_s = place("oc_s", [P, P])
        hsq_s = place("hsq_s", [P, P])
        imaskH = place("imaskH", [P, 8, P], F32R)
        S0s = place("S0s", [P, STREAMS, P])
        oc = place("oc", [P, 4 * P])
        place = over(bt_o)
        imaskL = place("imaskL", [P, 8, P], F32R)
        kendL = [place(f"kendL{i}", [P, P], F32R) for i in range(2)]
        place = over(aw_o)
        hsq = place("hsq", [P, 4 * P])
        hrs = place("hrs", [P, 4 * P])
        place = over(work + 4 * (KT_N + 7) * TOK)
        attm = [place(f"attm{i}", [P, P]) for i in range(3)]
        OC, HSQ, HRS = (oc, oc, oc_s), (hsq, hsq, hsq_s), (hrs, hrs, hrs_s)
        place = over(kt_o)
        xw = [place(f"xw{w}", [P, KT_N, WIN]) for w in range(2)]
        xsq = [place(f"xsq{i}", [P, 2, WIN]) for i in range(2)]
        place = over(bt_o)
        xsa = [place("xsa0", [P, 2, WIN])]
        xrs = place("xrs", [P, WIN])
        xw.append(place("xw2", [P, KT_N, WIN]))
        xsa.append(place("xsa1", [P, 2, WIN]))
        place = over(work)
        gh = place("gh", [P, KT_N, TOK], F32R)
        graw = place("graw", [P, KT_N, TOK])
        gl = at("gl", [P, KT_N, TOK], F32R, work + 4 * KT_N * TOK)
        place = over(work)
        yb = place("yb", [P, KT_N, TOK])
        ysq, ysa, yrs = ([place(f"{name}{w}", [P, WIN]) for w in range(NW)] for name in ("ysq", "ysa", "yrs"))
        no4 = place("no4", [P, P])

        bank = [ctx.enter_context(nc.psum_tensor(f"bank{i}", [P, 512], F32)) for i in range(8)]
        CH, Z, OB, TB, XB = bank[0:2], bank[2:5], bank[5], bank[6], bank[7]
        UA, UB = (bank[2], bank[4]), (bank[3], bank[5])

        def cst(d, t, name):
            o, n = d[name]
            return t[:, o:o + n]

        ident = cst(C1, k1, "ident")
        bgate, lbraw, hgn, gpre, gpost, eps_col = (cst(C1, k1, n) for n in ("bgate", "lbraw", "hgn", "gpre", "gpost", "eps"))
        negtri, negones, causal, hgmask, hgmask_s, smask, reset, reset_s, rows4, rows8 = (
            cst(C2, k2, n) for n in ("negtri", "negones", "causal", "hgmask", "hgmask_s", "smask", "reset", "reset_s", "rows4", "rows8"))

        s_c = sem("consts_loaded")
        s_x = [[sem(f"x_loaded{w}{h}") for h in range(2)] for w in range(NW)]
        s_xsa = sem("x_squares_summed")
        s_raw = [sem(f"chunk_loaded{i}") for i in range(3)]
        s_whi = sem("weights_high")
        s_wlo = sem("weights_low")
        s_xsq = sem("x_squared")
        s_xms = sem("x_meansq_step")
        s_xln = sem("x_log")
        s_xrs = sem("x_rstd")
        s_xn = sem("x_normed")
        s_xhi = sem("x_high")
        s_xlo = sem("x_low")
        s_win = sem("window_product")
        s_ev = sem("window_out_of_psum")
        s_ex = sem("window_exp")
        s_tr = sem("window_transposed")
        s_te = sem("transposed_in_sbuf")
        s_sg1 = sem("silu_plus_one")
        s_sg = sem("silu_reciprocal")
        s_silu = sem("silu_done")
        s_f1 = sem("forget_denominator")
        s_f = sem("forget_complement")
        s_lf = sem("forget_log")
        s_lb = sem("lower_bound_step")
        s_lbe = sem("lower_bound_exp")
        s_qkh = sem("keys_queries_high")
        s_qkl = sem("keys_queries_low")
        s_qk = sem("scores")
        s_E = sem("scores_exp")
        s_L = sem("scores_log")
        s_sp1 = sem("softplus_raw")
        s_sp = sem("softplus")
        s_S = sem("later_sum")
        s_sph = sem("softplus_high")
        s_spl = sem("softplus_low")
        s_Sh = sem("later_sum_high")
        s_Sl = sem("later_sum_low")
        s_cr = sem("masks_rounded")
        s_cum = sem("log_weights")
        s_a = sem("weights")
        s_am = sem("weights_masked")
        s_av = sem("values_added")
        s_gA = sem("attention_gated")
        s_cp = sem("sample_copies")
        s_qz = sem("qbd_zeroed")
        s_kv = [sem("keysT_cached"), sem("values_cached")]
        s_kout = sem("k_stored")
        s_vout = sem("v_stored")
        s_spA = sem("gated_a_spilled")
        s_spB = sem("gated_b_spilled")
        s_zs = sem("sample_scores")
        s_Es = sem("sample_exp")
        s_Ls = sem("sample_log")
        s_sps = sem("sample_softplus")
        s_spm = sem("sample_softplus_masked")
        s_Ss = sem("sample_later_sum")
        s_sphs = sem("sample_softplus_high")
        s_spls = sem("sample_softplus_low")
        s_Shs = sem("sample_later_sum_high")
        s_Sls = sem("sample_later_sum_low")
        s_cs = sem("sample_log_weights")
        s_as = sem("sample_weights")
        s_asm = sem("sample_weights_masked")
        s_os = sem("sample_values_added")
        s_gs = sem("sample_gated")
        s_scan = sem("decay_scanned")
        s_bmc = sem("block_ends_copied")
        s_A = sem("decay_centred")
        s_ge = sem("block_decay_log")
        s_EX = sem("decay_exp")
        s_hqd = sem("queries_decayed")
        s_hki = sem("keys_grown")
        s_hke = sem("keys_to_block_end")
        s_S0 = sem("state_zeroed")
        s_S0l = sem("state_loaded")
        s_S0m = sem("state_scaled")
        s_im = sem("values_by_block_high")
        s_iml = sem("values_by_block_low")
        s_kt = sem("keys_transposed")
        s_kn = sem("keys_natural_high")
        s_knl = sem("keys_natural_low")
        s_at = sem("hgrn_scores")
        s_atm = sem("hgrn_scores_masked")
        s_KV = sem("block_updates")
        s_ch = sem("state_step")
        s_h3 = sem("hgrn_out")
        s_oc = sem("hgrn_out_copied")
        s_hs = sem("hgrn_squared")
        s_hm = sem("hgrn_meansq")
        s_hl = sem("hgrn_log")
        s_hr = sem("hgrn_rstd")
        s_hg1 = sem("hgrn_normed")
        s_hg = sem("hgrn_gated")
        s_ss1 = sem("sample_state_decayed")
        s_ss = sem("sample_state")
        s_so = sem("prompt_state_stored")
        s_sso = sem("sample_state_stored")
        s_gr = [sem(f"gated_reloaded{i}") for i in range(8)]
        s_gh = sem("gated_high")
        s_gl = sem("gated_low")
        s_g1 = sem("gate_plus_one")
        s_sig = sem("gate_sigmoid")
        s_u = sem("branch_products")
        s_ma = sem("branch_a_gated")
        s_mb = sem("branch_b_gated")
        s_mg = sem("merged")
        s_mh = sem("merged_high")
        s_ml = sem("merged_low")
        s_xr = sem("residual_loaded")
        s_no = sem("minus_ones")
        s_yq = sem("y_squared")
        s_ya = sem("y_squares_summed")
        s_yn = sem("y_meansq")
        s_yl = sem("y_log")
        s_yr = sem("y_rstd")
        s_yg = sem("y_scaled")
        s_yo = sem("y_done")
        s_yg3 = sem("y_scaled_gpsimd")
        s_yo3 = sem("y_done_gpsimd")
        s_out = sem("y_stored")

        def need(eng, s, v):
            if v > 0:
                eng.wait_ge(s, v)

        def chunk_done(eng, g):
            if g < 0:
                return
            if g == 0:
                eng.wait_ge(s_win, 5)
            elif GATE_G0 <= g < OUT_G0 and MERGE[g - GATE_G0][0] == "branch":
                eng.wait_ge(s_u, 3 * MERGE[g - GATE_G0][1] + 3)
            else:
                eng.wait_ge(s_win, win_of(g) + 3)

        def attention_over(eng, p):
            need(eng, s_a, NS * (p + 1))
            need(eng, s_S, SUMS * (p + 1))

        def recurrence_over(eng, p, norm=True):
            need(eng, s_ss, 2 * (p + 1))
            if norm:
                need(eng, s_hg, 3 * (p + 1))
            need(eng, s_gs, 2 * (p + 1))
            need(eng, s_ch, NBLK * (p + 1))
            need(eng, s_hki, p + 1)
            need(eng, s_hqd, p + 1)

        block = ctx.enter_context(nc.Block())

        @block.sync
        def _(sp):
            def load_chunk(g):
                chunk_done(sp, g - 3)
                sp.dma_start(wr[g % 3][:, :, :], wch[g].rearrange("p (k c) -> p k c", c=P)).then_inc(s_raw[g % 3], 16)

            def load_x(w, half):
                r = slice(4 * half, 4 * half + 4)
                sp.dma_start(xw[w][:, r, :], xT[:, r, w * WIN:(w + 1) * WIN]).then_inc(s_x[w][half], 16)

            def store_kv(pp):
                sp.wait_ge(s_ev, win_of(1 + (8 * pp if pp else 0)) + 3)
                sp.dma_start(okT[pp], kT[:, :]).then_inc(s_kout, 16)
                sp.wait_ge(s_te, 6 * pp + 3)
                sp.dma_start(ov[pp].rearrange("(t s) c -> s t c", s=P), v_nat[:, :].rearrange("s (t c) -> s t c", c=P)).then_inc(s_vout, 16)

            load_x(0, 0)
            load_x(0, 1)
            sp.dma_start(k1[:, :], c1).then_inc(s_c, 16)
            sp.dma_start(k2[:, :], c2).then_inc(s_c, 16)
            load_chunk(0)
            load_x(1, 0)
            load_x(1, 1)
            load_chunk(1)
            load_x(2, 0)
            load_x(2, 1)
            for g in range(2, 7):
                load_chunk(g)
            store_kv(0)
            for p in range(PAIRS):
                recurrence_over(sp, p - 1)
                if p:
                    sp.wait_ge(s_sso, 16 * p)
                    sp.wait_ge(s_so, 16 * p)
                    sp.wait_ge(s_os, p)
                else:
                    sp.wait_ge(s_xlo, NW * 4)
                    sp.wait_ge(s_xsa, NW * 3)
                sp.dma_start(KT_[:, :, :], ckT[p].rearrange("i d s -> d i s")).then_inc(s_kv[0], 16)
                for g in range(4 + 8 * p + 3, 8 + 8 * p + 2):
                    load_chunk(g)
                sp.wait_ge(s_qk, NS * (p + 1))
                sp.dma_start(V_[:, :, :, :].rearrange("s i j c -> s i (j c)"), cv[p].rearrange("i s n -> s i n")).then_inc(s_kv[1], 16)
                load_chunk(8 + 8 * p + 2)
                sp.wait_ge(s_gA, 2 * (p + 1))
                sp.dma_start(spill[p, :, 0:SEQ], zA[:, 0:SEQ]).then_inc(s_spA, 16)
                sp.wait_ge(s_zs, 3 * (p + 1))
                recurrence_over(sp, p - 1)
                sp.dma_start(S0s[:, :, :], st[p].rearrange("i c v -> c i v")).then_inc(s_S0l, 16)
                sp.wait_ge(s_gs, 2 * (p + 1))
                sp.dma_start(spill[p, :, SEQ:TOK], zAs[:, :]).then_inc(s_spA, 16)
                if p == PAIRS - 1:
                    sp.wait_ge(s_os, PAIRS)
                    sp.wait_ge(s_hki, PAIRS)
                    sp.wait_ge(s_hqd, PAIRS)
                    sp.wait_ge(s_spA, 32 * (PAIRS - 1))
                    for t in range(3):
                        sp.dma_start(graw[:, ROW_OF[t], :], spill[t]).then_inc(s_gr[t], 16)
                for g in range(8 + 8 * p + 3, 12 + 8 * p + 3):
                    load_chunk(g)
                sp.wait_ge(s_ch, NBLK * (p + 1))
                sp.dma_start(osp[p], St[NBLK % 8][:, :]).then_inc(s_so, 16)
                sp.wait_ge(s_hg, 3 * (p + 1))
                sp.dma_start(spill[PAIRS + p], zB[:, :]).then_inc(s_spB, 16)
                sp.wait_ge(s_ss, 2 * (p + 1))
                sp.dma_start(oss[p].rearrange("i c v -> c i v"), S0s[:, :, :]).then_inc(s_sso, 16)
                if p + 1 < PAIRS:
                    store_kv(p + 1)
            recurrence_over(sp, PAIRS - 1)
            sp.wait_ge(s_h3, NT * PAIRS)
            sp.wait_ge(s_hm, 3 * PAIRS)
            sp.wait_ge(s_spA, 32 * PAIRS)
            sp.wait_ge(s_spB, 16 * PAIRS)
            for t in range(3, 8):
                sp.dma_start(graw[:, ROW_OF[t], :], spill[t]).then_inc(s_gr[t], 16)
            for g in range(39, 64):
                load_chunk(g)
            sp.wait_ge(s_ml, 10)
            sp.dma_start(xres[:, :, :], xT).then_inc(s_xr, 16)
            for w in range(NW):
                for lo, hi in ((0, 3), (3, 6), (6, 8)):
                    if lo < 6:
                        sp.wait_ge(s_yo, 2 * w + lo // 3 + 1)
                    else:
                        sp.wait_ge(s_yo3, w + 1)
                    r = slice(lo, hi)
                    sp.dma_start(yT[:, r, w * WIN:(w + 1) * WIN], yb[:, r, w * WIN:(w + 1) * WIN]).then_inc(s_out, 16)
            sp.wait_ge(s_out, 16 * 3 * NW)
            sp.wait_ge(s_kout, 16 * PAIRS)
            sp.wait_ge(s_vout, 16 * PAIRS)
            sp.wait_ge(s_so, 16 * PAIRS)
            sp.wait_ge(s_sso, 16 * PAIRS)

        @block.tensor
        def _(pe):
            def product(g, w, q, n=None):
                n = win_of(g) + w if n is None else n
                if q == 0:
                    if w == 0:
                        pe.wait_ge(s_whi, g + 1)
                        pe.wait_ge(s_wlo, g + 1)
                    need(pe, s_ev, n - 1)
                for m in range(8 * q, 8 * q + 8):
                    k, part = m // 3, m % 3
                    if g == 0 and part == 0:
                        pe.wait_ge(s_xhi, 4 * w + k // 2 + 1)
                    if g == 0 and part == 1:
                        pe.wait_ge(s_xlo, 4 * w + k // 2 + 1)
                    if g == OUT_G0 and part == 0 and (w == 0 or k == 7):
                        pe.wait_ge(s_mh, k + 1 + w)
                        pe.wait_ge(s_ml, k + 1 + w)
                    weights = wl[g % 3] if part == 2 else wh[g % 2]
                    rows = xl if part == 1 else xh
                    i = nc.tensor.matmul(CH[n % 2][:, 0:WIN], weights[:, k, :], rows[:, k, w * WIN:(w + 1) * WIN],
                                         start=(m == 0), stop=(m == 23))
                    if m == 23:
                        i.then_inc(s_win, 1)

            def transpose_window(n, idx, src):
                pe.wait_ge(s_ev, n + 1)
                need(pe, s_te, idx)
                for t in range(3):
                    i = nc.tensor.transpose(TB[:, t * P:(t + 1) * P], src[:, t * P:(t + 1) * P], ident)
                i.then_inc(s_tr, 1)

            def turn_attention(pp, w12):
                c, w = divmod(w12, 3)
                if c == 2:
                    transpose_window(win_of(8 * pp if pp else 0) + w12, 6 * pp + w, tmpT[(12 * pp + w) % 2])

            def turn_recurrence(p, w12):
                c, w = divmod(w12, 3)
                if c == 2:
                    transpose_window(win_of(4 + 8 * p) + w12, 6 * p + 3 + w, tmpT[(12 * p + 6 + w) % 2])

            def x_square_sum(w):
                pe.wait_ge(s_xsa, 3 * (w + 1))
                for r in range(2):
                    i = nc.tensor.matmul(Z[w][:, 0:WIN], negones, xsa[w % 2][:, r, :], start=(r == 0), stop=(r == 1))
                i.then_inc(s_xms, 1)

            pe.wait_ge(s_c, 32)
            x_square_sum(0)
            for i12 in range(12):
                c, w = prologue_window(i12)
                for q in range(PIECES):
                    if (i12, q) in ((0, 2), (2, 1)):
                        x_square_sum(1 + i12 // 2)
                    product(c, w, q, i12)
                if i12:
                    turn_attention(0, i12 - 1)
            turn_attention(0, 11)

            for p in range(PAIRS):
                need(pe, s_ch, NBLK * p)
                need(pe, s_atm, NT * p)
                need(pe, s_ss, 2 * p)
                late = []
                for n in range(B_STEPS):
                    if n < NS:
                        wd, j, h = STEPS[n]
                        c0, t = first_col(n), NS * p + n
                        if n == 0:
                            pe.wait_ge(s_qkh, 6 * (p + 1))
                            pe.wait_ge(s_qkl, 4 * (p + 1))
                        need(pe, s_a, t - 2)
                        c0 = min(c0, QW // 2)
                        keys, queries = slice(j * P, (j + 1) * P), slice(wd * QW + c0, (wd + 1) * QW)
                        head = slice(DH * h, DH * h + DH)
                        nc.tensor.matmul(Z[n % 3][:, c0:QW], KS[h][:, keys], QS[h][:, queries], start=True, stop=False)
                        nc.tensor.matmul(Z[n % 3][:, c0:QW], KS[h][head, keys], qlo[head, queries],
                                         start=False, stop=True).then_inc(s_qk, 1)
                    mid = len(B_PIECES[n]) // 2
                    for x in B_PIECES[n][:mid]:
                        product(4 + 8 * p + x // 9, x // 3 % 3, x % 3)
                    if 2 <= n <= NS + 1:
                        m = n - 2
                        wd, j, h = STEPS[m]
                        c0, t, q = first_col(m), NS * p + m, tile_rank(m)

                        def add(weights, rows, lo):
                            return nc.tensor.matmul(Z[m % 3][:, lo:QW], weights, rows[:, lo:QW], start=False, stop=True,
                                                    skip_group_check=True)

                        if q == 0:
                            pe.wait_ge(s_cr, 2)
                            pe.wait_ge(s_sp, t + 1)
                            i = add(negtri, E[m % 3], c0)
                        else:
                            pe.wait_ge(s_sph, SPLITS * p + rows_until(m))
                            add(negtri_r[:, :], SPH[m % 2], c0)
                            cs = first_col(m - 2)
                            if q == 1:
                                pe.wait_ge(s_S, SUMS * p + sums_until(m - 2))
                                add(negones, SUM[h], cs)
                            else:
                                pe.wait_ge(s_Sh, SUM_SPLITS * p + sum_rows_until(m))
                                add(negones_r[:, :], SUH[h], cs)
                                pe.wait_ge(s_Sl, SUM_SPLITS * p + sum_rows_until(m))
                                add(negones_r[:, :], SUL[h], cs)
                            pe.wait_ge(s_spl, SPLITS * p + rows_until(m))
                            i = add(negtri_r[:, :], SPL[m % 2], c0)
                        i.then_inc(s_cum, 1)
                    for x in B_PIECES[n][mid:]:
                        product(4 + 8 * p + x // 9, x // 3 % 3, x % 3)
                    if n >= 3:
                        m = n - 3
                        wd, j, h = STEPS[m]
                        c0, t = first_col(m), NS * p + m
                        if m == 0:
                            need(pe, s_oc, 3 * p)
                            pe.wait_ge(s_te, 6 * p + 3)
                        if j == 4 * wd + 3 and h == 0:
                            need(pe, s_gA, 2 * p + wd)
                        pe.wait_ge(s_a, t + 1)
                        if diagonal(m):
                            pe.wait_ge(s_am, DIAGS * p + diagonals_until(m))
                        nc.tensor.matmul(OB[DH * h:DH * h + DH, c0:QW], v_nat[:, j * P + DH * h:j * P + DH * h + DH],
                                         Aw[m % 2][:, c0:QW], start=(j == 4 * wd + 3), stop=(j == 0),
                                         skip_group_check=True).then_inc(s_av, 1)
                    for w12 in late:
                        turn_recurrence(p, w12)
                    late = ended(B_PIECES[n])
                for w12 in late:
                    turn_recurrence(p, w12)

                late = []
                for m in range(A_STEPS):
                    if m == 0:
                        attention_over(pe, p)
                        pe.wait_ge(s_cp, 5 * (p + 1))
                        pe.wait_ge(s_kv[0], 16 * (p + 1))
                        qall = qbd[:, :, :, :].rearrange("p i h t -> p (i h t)")
                        nc.tensor.matmul(Z[2][:, 0:256], kTs[:, :], qall, start=True, stop=True).then_inc(s_zs, 1)
                        for half in (1, 0):
                            for j2 in range(2):
                                for s in range(STREAMS):
                                    o = 256 * j2 + 32 * s
                                    i = nc.tensor.matmul(Z[half][:, o:o + 32], KT_[:, s, P * (2 * half + j2):P * (2 * half + j2 + 1)],
                                                         qall[:, 32 * s:32 * s + 32], start=(j2 == 0 and s == 0), stop=True,
                                                         skip_group_check=True)
                            i.then_inc(s_zs, 1)
                    if m == 1:
                        pe.wait_ge(s_sphs, p + 1)
                        pe.wait_ge(s_spls, p + 1)
                        nc.tensor.matmul(Z[2][:, 0:256], negtri_r[:, :], SPsH[:, 4, :], start=False, stop=True,
                                         skip_group_check=True)
                        nc.tensor.matmul(Z[2][:, 0:256], negtri_r[:, :], SPsL[:, 4, :], start=False, stop=True,
                                         skip_group_check=True).then_inc(s_cs, 1)
                        for j in (3, 2, 1, 0):
                            bk = Z[j // 2][:, 256 * (j % 2):256 * (j % 2) + 256]
                            if j == 2:
                                pe.wait_ge(s_Shs, p + 1)
                                pe.wait_ge(s_Sls, p + 1)
                            for weights, rows in ((negtri_r, SPsH[:, j, :]), (negtri_r, SPsL[:, j, :]),
                                                  (negones_r, SPsH[:, 4, :] if j == 3 else SUsH[:, 2 - j, :]),
                                                  (negones_r, SPsL[:, 4, :] if j == 3 else SUsL[:, 2 - j, :])):
                                i = nc.tensor.matmul(bk, weights[:, :], rows, start=False, stop=True, skip_group_check=True)
                            if j % 2 == 0:
                                i.then_inc(s_cs, 1)
                    if m == 2:
                        pe.wait_ge(s_gA, 2 * (p + 1))
                        pe.wait_ge(s_asm, p + 1)
                        nc.tensor.matmul(OB[:, 0:256], vs[:, :], Es[:, 4, :], start=True, stop=True)
                        pe.wait_ge(s_kv[1], 16 * (p + 1))
                        pe.wait_ge(s_as, 3 * (p + 1))
                        for j in (3, 2, 1, 0):
                            for s in range(STREAMS):
                                i = nc.tensor.matmul(OB[:, 32 * s:32 * s + 32], V_[:, s, j, :], Es[:, j, 32 * s:32 * s + 32],
                                                     start=False, stop=True, skip_group_check=True)
                        i.then_inc(s_os, 1)
                    if m >= 3:
                        c = m - 3
                        pieces, mid = A_PIECES[m], len(A_PIECES[m]) // 2
                        before, between, after = {7: (pieces[:mid], [], pieces[mid:]), NT: ([], pieces, [])}.get(
                            c, ([], pieces[:mid], pieces[mid:]))
                        for x in before:
                            product(8 + 8 * p + x // 9, x // 3 % 3, x % 3)
                        if c < NT:
                            pe.wait_ge(s_hke, 2 * (p + 1))
                            need(pe, s_kn, NT * p + c)
                            need(pe, s_knl, NT * p + c)
                            if c >= 7:
                                pe.wait_ge(s_hl, 3 * p + 1)
                            nc.tensor.transpose(XB[:, 0:P], lf[:, c * P:(c + 1) * P], ident).then_inc(s_kt, 1)
                            pe.wait_ge(s_hqd, p + 1)
                            pe.wait_ge(s_hki, p + 1)
                            if c == 0:
                                pe.wait_ge(s_as, 3 * (p + 1))
                            need(pe, s_atm, NT * p + c)
                            nc.tensor.matmul(Z[2][:, 0:P], kb[:, c * P:(c + 1) * P], hq[:, c * P:(c + 1) * P],
                                             start=True, stop=True).then_inc(s_at, 1)
                        for x in between:
                            product(8 + 8 * p + x // 9, x // 3 % 3, x % 3)
                        if 1 <= c <= NT:
                            b = c - 1
                            pe.wait_ge(s_kn, NT * p + b + 1)
                            pe.wait_ge(s_im, NT * p + b + 1)
                            pe.wait_ge(s_knl, NT * p + b + 1)
                            pe.wait_ge(s_iml, NT * p + b + 1)
                            if b < 8:
                                if b >= 2:
                                    pe.wait_ge(s_ch, NBLK * p + 4 * (b - 1))
                                updates = ((Z[b % 2], b % 2),)
                            else:
                                pe.wait_ge(s_ch, NBLK * (p + 1))
                                updates = ((Z[0], 0), (Z[1], 1))
                            for bk, slot in updates:
                                blocks = slice(4 * slot, 4 * slot + 4)
                                for i, (keys, values) in enumerate(((kendH, imaskH), (kendH, imaskL), (kendL, imaskH))):
                                    mm = nc.tensor.matmul(bk[:, :], keys[b % 2][:, :],
                                                          values[:, blocks, :].rearrange("s b v -> s (b v)"),
                                                          start=(i == 0), stop=(i == 2))
                            mm.then_inc(s_KV, 1)
                        for x in after:
                            product(8 + 8 * p + x // 9, x // 3 % 3, x % 3)
                        if 2 <= c <= NT + 1:
                            b = c - 2
                            if b == 0:
                                pe.wait_ge(s_gs, 2 * (p + 1))
                                pe.wait_ge(s_S0, p + 1)
                            if b in (4, 8):
                                pe.wait_ge(s_oc, 3 * p + b // 4)
                            pe.wait_ge(s_atm, NT * p + b + 1)
                            o0 = P * (b % 4)
                            nc.tensor.matmul(OB[:, o0:o0 + P], i_nat[:, b * P:(b + 1) * P], attm[b % 3][:, :],
                                             start=True, stop=True)
                            if b < 8:
                                for s in range(4):
                                    nb = 4 * b + s
                                    if nb:
                                        pe.wait_ge(s_ch, NBLK * p + nb)
                                    i = nc.tensor.matmul(OB[:, o0 + BLK * s:o0 + BLK * s + BLK], St[nb % 8][:, :],
                                                         hq[:, nb * BLK:(nb + 1) * BLK], start=False, stop=True,
                                                         skip_group_check=True)
                            else:
                                pe.wait_ge(s_S0m, p + 1)
                                for s in range(STREAMS):
                                    i = nc.tensor.matmul(OB[:, o0 + DSEQ * s:o0 + DSEQ * s + DSEQ], S0s[:, s, :],
                                                         hq[:, SEQ + DSEQ * s:SEQ + DSEQ * s + DSEQ], start=False, stop=True,
                                                         skip_group_check=True)
                            i.then_inc(s_h3, 1)
                        if c in MS_STEP:
                            g = MS_STEP.index(c)
                            n = P * (GROUPS[g][1] - GROUPS[g][0])
                            pe.wait_ge(s_hs, 3 * p + g + 1)
                            pe.wait_ge(s_kn, NT * p + (7 if g == 0 else 9))
                            pe.wait_ge(s_knl, NT * p + (7 if g == 0 else 9))
                            if g:
                                pe.wait_ge(s_hl, 3 * p + g)
                            nc.tensor.matmul(XB[:, 0:n], negones, HSQ[g][:, 0:n], start=True, stop=True).then_inc(s_hm, 1)
                    else:
                        for x in A_PIECES[m]:
                            product(8 + 8 * p + x // 9, x // 3 % 3, x % 3)
                    if p + 1 < PAIRS:
                        for w12 in late:
                            turn_attention(p + 1, w12)
                        late = ended(A_PIECES[m])
                if p + 1 < PAIRS:
                    for w12 in late:
                        turn_attention(p + 1, w12)

            for g in range(GATE_G0 + 4, OUT_G0):
                what, dm, kind = MERGE[g - GATE_G0]
                if what == "gate":
                    for w in range(NW):
                        for q in range(PIECES):
                            product(g, w, q)
                    continue
                if dm == 0:
                    recurrence_over(pe, PAIRS - 1)
                pe.wait_ge(s_whi, g + 1)
                pe.wait_ge(s_wlo, g + 1)
                for w in range(NW):
                    n = 3 * dm + w
                    need(pe, s_mb, n - 1)
                    need(pe, s_ma, n - 1)
                    for half, bk in ((0, UA[n % 2]), (1, UB[n % 2])):
                        for m in range(12):
                            t, part = 4 * half + m // 3, m % 3
                            if n == 0 and part == 0:
                                pe.wait_ge(s_gh, t + 1)
                                pe.wait_ge(s_gl, t + 1)
                            weights = wl[g % 3] if part == 2 else wh[g % 2]
                            rows = gl if part == 1 else gh
                            i = nc.tensor.matmul(bk[:, 0:WIN], weights[:, t, :], rows[:, ROW_OF[t], w * WIN:(w + 1) * WIN],
                                                 start=(m == 0), stop=(m == 11))
                    i.then_inc(s_u, 1)

            def y_square_sum(w, last):
                if last:
                    pe.wait_ge(s_yq, 20 + 2 * w)
                    nc.tensor.matmul(Z[w][:, 0:WIN], no4[:, :], ysq[w][:, :], start=False, stop=True).then_inc(s_yn, 1)
                else:
                    pe.wait_ge(s_ya, 3 * (KT_N - 3) + w + 1)
                    nc.tensor.matmul(Z[w][:, 0:WIN], no4[:, :], ysa[w][:, :], start=True, stop=False)

            for n in range(3 * KT_N):
                k, w = output_product(n)
                for q in range(PIECES):
                    if k == KT_N - 1 and q == PIECES - 1:
                        if w == 0:
                            pe.wait_ge(s_no, 1)
                            pe.wait_ge(s_mb, 3 * KT_N)
                            pe.wait_ge(s_ma, 3 * KT_N)
                        y_square_sum(w, last=False)
                    product(OUT_G0 + k, w, q, OUT_W0 + n)
                if n in (20, 22):
                    y_square_sum(n // 2 - 10, last=True)
            y_square_sum(2, last=True)

        @block.scalar
        def _(act):
            def evacuate(n, dst, waits):
                for s, v in waits:
                    need(act, s, v)
                act.wait_ge(s_win, n + 1)
                nc.scalar.activation(dst, CH[n % 2][:, 0:WIN], ACT.Copy).then_inc(s_ev, 1)

            def tmp_free(idx):
                pair, r = divmod(idx - 2, 12)
                if idx < 2:
                    return
                half, r = divmod(r, 6)
                act.wait_ge(s_silu if r >= 3 else s_tr, 6 * pair + 3 * half + r % 3 + 1)

            def silu(n, idx, half, dst, waits):
                t = tmpT[idx % 2][:, :]
                tmp_free(idx)
                act.wait_ge(s_win, n + 1)
                nc.scalar.activation(t, CH[n % 2][:, 0:WIN], ACT.Exp, scale=-1.0).then_inc(s_ex, 1)
                evacuate(n, dst, waits)
                act.wait_ge(s_ex, half + 1)
                nc.scalar.activation(t, t, ACT.Ln, bias=1.0).then_inc(s_sg1, 1)
                act.wait_ge(s_sg1, half + 1)
                nc.scalar.activation(t, t, ACT.Exp, scale=-1.0).then_inc(s_sg, 1)

            def window_attention(pp, w12):
                c, w = prologue_window(w12) if pp == 0 else divmod(w12, 3)
                n = win_of(8 * pp if pp else 0) + w12
                cols = slice(w * WIN, (w + 1) * WIN)
                copies = (s_cp, 5 * pp)
                if c == 0:
                    for s, v in ((s_qk, NS * pp), copies):
                        need(act, s, v)
                    act.wait_ge(s_win, n + 1)
                    nc.scalar.activation(qT[:, cols], CH[n % 2][:, 0:WIN], ACT.Copy, scale=DH ** -0.5).then_inc(s_ev, 1)
                elif c == 1:
                    evacuate(n, kT[:, cols], ((s_qk, NS * pp), copies, (s_kout, 16 * pp)))
                elif c == 2:
                    tmp_free(12 * pp + w)
                    evacuate(n, tmpT[(12 * pp + w) % 2][:, :], ())
                else:
                    silu(n, 12 * pp + 3 + w, 6 * pp + w, zA[:, cols], (copies, (s_spA, 32 * pp)))

            def high_parts(pp, what):
                if what == 0:
                    act.wait_ge(s_ev, win_of(8 * pp if pp else 0) + 6)
                    if pp:
                        act.wait_ge(s_os, pp)
                    else:
                        act.wait_ge(s_xlo, 4 * NW)
                        act.wait_ge(s_xsa, 3 * NW)
                for h in range(2):
                    own, other = slice(DH * h, DH * h + DH), slice(DH * (1 - h), DH * (1 - h) + DH)
                    dst, src = ((KS[h][own, :], kT), (QS[h][own, :], qT), (QS[h][other, :], qT))[what]
                    nc.scalar.activation(dst, src[own, 0:SEQ], ACT.Copy).then_inc(s_qkh, 1)

            def window_recurrence(p, w12):
                c, w = divmod(w12, 3)
                n = win_of(4 + 8 * p) + w12
                cols = slice(w * WIN, (w + 1) * WIN)
                if c == 0:
                    evacuate(n, hq[:, cols], ((s_h3, NT * p),))
                elif c == 1:
                    need(act, s_at, NT * p)
                    need(act, s_hke, 2 * p)
                    act.wait_ge(s_win, n + 1)
                    nc.scalar.activation(kb[:, cols], CH[n % 2][:, 0:WIN], ACT.Exp).then_inc(s_ev, 1)
                elif c == 2:
                    tmp_free(12 * p + 6 + w)
                    evacuate(n, tmpT[(12 * p + 6 + w) % 2][:, :], ())
                else:
                    silu(n, 12 * p + 9 + w, 6 * p + 3 + w, zB[:, cols], ((s_spB, 16 * p),))

            def forget(p, w):
                k = kb[:, w * WIN:(w + 1) * WIN]
                act.wait_ge(s_ev, win_of(5 + 8 * p) + w + 1)
                nc.scalar.activation(k, k, ACT.Ln, bias=1.0).then_inc(s_f1, 1)
                act.wait_ge(s_f1, 3 * p + w + 1)
                nc.scalar.activation(k, k, ACT.Exp, scale=-1.0, bias=lbv[:, 4, p:p + 1]).then_inc(s_f, 1)
                act.wait_ge(s_f, 3 * p + w + 1)
                need(act, s_kt, NT * p)
                nc.scalar.activation(lf[:, w * WIN:(w + 1) * WIN], k, ACT.Ln, scale=-1.0, bias=1.0).then_inc(s_lf, 1)

            def window_gate(dm, kind, w):
                n = gate_window_no(dm, kind, w)
                s = slots[dm if kind == 0 else GATE_B_SLOT[dm]][:, w * WIN:(w + 1) * WIN]
                if w == 0:
                    gate_slot_free(dm, kind)
                act.wait_ge(s_win, n + 1)
                nc.scalar.activation(s, CH[n % 2][:, 0:WIN], ACT.Exp, scale=-1.0,
                                     bias=ngate[:, 8 * kind + dm:8 * kind + dm + 1]).then_inc(s_ev, 1)
                act.wait_ge(s_ev, n + 1)
                nc.scalar.activation(s, s, ACT.Ln, bias=1.0).then_inc(s_g1, 1)
                act.wait_ge(s_g1, 6 * dm + 3 * kind + w + 1)
                nc.scalar.activation(s, s, ACT.Exp, scale=-1.0).then_inc(s_sig, 1)

            def gate_slot_free(dm, kind):
                if dm < 2:
                    act.wait_ge(s_qk, NS * PAIRS)
                    act.wait_ge(s_av, NS * PAIRS)
                    act.wait_ge(s_cp, 5 * PAIRS)
                    act.wait_ge(s_kout, 16 * PAIRS)
                    act.wait_ge(s_vout, 16 * PAIRS)
                    act.wait_ge(s_spA, 16 * (2 * PAIRS - 1))
                if dm == 2:
                    act.wait_ge(s_h3, NT * PAIRS)
                    act.wait_ge(s_spB, 16 * PAIRS)
                need(act, s_mg, 3 * (slot_user_before(dm, kind) + 1))

            def gated_high(t):
                act.wait_ge(s_gr[t], 16)
                nc.scalar.activation(gh[:, ROW_OF[t], :], graw[:, ROW_OF[t], :], ACT.Copy).then_inc(s_gh, 1)

            nc.scalar.preload_act_table_set("natural_log_exp_and_others")
            def square_x(w, r):
                act.wait_ge(s_x[w][r // 2], 16)
                if r == 0:
                    need(act, s_xms, w - 1)
                else:
                    need(act, s_xsa, 3 * w + r - 2)
                dst = xsa[w % 2] if r == 0 else xsq[(3 * w + r) % 2]
                nc.scalar.activation(dst[:, :, :], xw[w][:, 2 * r:2 * r + 2, :], ACT.Square).then_inc(s_xsq, 1)

            for r in range(4):
                square_x(0, r)
            act.wait_ge(s_c, 32)
            act.wait_ge(s_lb, 3)
            nc.scalar.activation(lbv[:, 1:3, :], lbv[:, 1:3, :], ACT.Exp).then_inc(s_lbe, 1)
            act.wait_ge(s_lb, 6)
            nc.scalar.activation(lbv[:, 4, :], lbv[:, 4, :], ACT.Ln).then_inc(s_lbe, 1)
            for w in range(NW):
                act.wait_ge(s_xms, w + 1)
                need(act, s_xn, KT_N * w)
                nc.scalar.activation(xrs[:, :], Z[w][:, 0:WIN], ACT.Ln, scale=-1.0 / D, bias=eps_col).then_inc(s_xln, 1)
                act.wait_ge(s_xln, w + 1)
                nc.scalar.activation(xrs[:, :], xrs[:, :], ACT.Exp, scale=-0.5).then_inc(s_xrs, 1)
                if w == 0:
                    square_x(1, 0)
                    square_x(1, 1)
                for r in range(4):
                    act.wait_ge(s_xn, KT_N * w + 2 * r + 2)
                    nc.scalar.activation(xh[:, 2 * r:2 * r + 2, w * WIN:(w + 1) * WIN], xw[w][:, 2 * r:2 * r + 2, :],
                                         ACT.Copy).then_inc(s_xhi, 1)
                    if w == 0 and r < 2:
                        square_x(1, 2 + r)
                    if w and r in (0, 2):
                        window_attention(0, 2 * (w - 1) + r // 2)
                    if w == 1 and r == 0:
                        square_x(2, 3)
                if w == 0:
                    for r in range(3):
                        square_x(2, r)
            for w12 in range(4, 12):
                window_attention(0, w12)
                if w12 in (6, 7, 8):
                    high_parts(0, w12 - 6)

            for p in range(PAIRS):
                recurrence_over(act, p - 1, norm=False)
                late = []
                for n in range(B_STEPS):
                    if n < NS:
                        c0, t = first_col(n), NS * p + n
                        act.wait_ge(s_qk, t + 1)
                        need(act, s_cum, t - 2)
                        need(act, s_S, SUMS * p + (sums_until(n - 3) if n >= 3 else 0))
                        nc.scalar.activation(E[n % 3][:, c0:QW], Z[n % 3][:, c0:QW], ACT.Exp).then_inc(s_E, 1)
                        act.wait_ge(s_E, t + 1)
                        nc.scalar.activation(E[n % 3][:, c0:QW], E[n % 3][:, c0:QW], ACT.Ln, bias=1.0).then_inc(s_L, 1)
                    if 2 <= n <= NS + 1:
                        m = n - 2
                        c0, t = first_col(m), NS * p + m
                        act.wait_ge(s_cum, t + 1)
                        need(act, s_av, t - 1)
                        if m < 2:
                            need(act, s_hg, 3 * p)
                        nc.scalar.activation(Aw[m % 2][:, c0:QW], Z[m % 3][:, c0:QW], ACT.Exp).then_inc(s_a, 1)
                    for c, w in late:
                        if c == 1:
                            forget(p, w)
                    late = []
                    for w12 in ended(B_PIECES[n]):
                        window_recurrence(p, w12)
                        late.append(divmod(w12, 3))
                attention_over(act, p)
                for m in range(A_STEPS):
                    if m == 0:
                        for r, (bk, lo, n) in enumerate(((Z[2], 4, 1), (Z[1], 2, 2), (Z[0], 0, 2))):
                            e = Es[:, lo:lo + n, :].rearrange("s j c -> s (j c)")
                            act.wait_ge(s_zs, 3 * p + r + 1)
                            nc.scalar.activation(e, bk[:, 0:256 * n], ACT.Exp).then_inc(s_Es, 1)
                            act.wait_ge(s_Es, 3 * p + r + 1)
                            nc.scalar.activation(e, e, ACT.Ln, bias=1.0).then_inc(s_Ls, 1)
                        act.wait_ge(s_ge, 2 * (p + 1))
                        nc.scalar.activation(gg[:, :], be[:, :], ACT.Exp).then_inc(s_EX, 1)
                        nc.scalar.activation(em[:, :], bm[:, NBLK:], ACT.Exp).then_inc(s_EX, 1)
                        act.wait_ge(s_A, 2 * (p + 1))
                        nc.scalar.activation(EK[:, :], lf[:, :], ACT.Exp, scale=-1.0).then_inc(s_EX, 1)
                        nc.scalar.activation(EQ[:, :], lf[:, :], ACT.Exp).then_inc(s_EX, 1)
                    if m == 1:
                        act.wait_ge(s_sps, 3 * (p + 1))
                        for r, (bk, lo, n) in enumerate(((Z[2], 4, 1), (Z[1], 2, 2), (Z[0], 0, 2))):
                            act.wait_ge(s_cs, 3 * p + r + 1)
                            nc.scalar.activation(Es[:, lo:lo + n, :].rearrange("s j c -> s (j c)"), bk[:, 0:256 * n],
                                                 ACT.Exp).then_inc(s_as, 1)
                    if m >= 3:
                        c = m - 3
                        if c < NT:
                            act.wait_ge(s_kt, NT * p + c + 1)
                            need(act, s_KV, NT * p + c - 1 if c >= 2 else 0)
                            nc.scalar.activation(kendH[c % 2][:, :], XB[:, 0:P], ACT.Copy).then_inc(s_kn, 1)
                        for g in range(3):
                            if c == MS_STEP[g]:
                                n = P * (GROUPS[g][1] - GROUPS[g][0])
                                act.wait_ge(s_hm, 3 * p + g + 1)
                                need(act, s_hg1, 3 * p + min(g, 1))
                                nc.scalar.activation(HRS[g][:, 0:n], XB[:, 0:n], ACT.Ln, scale=-1.0 / P, bias=eps_col).then_inc(s_hl, 1)
                                act.wait_ge(s_hl, 3 * p + g + 1)
                                nc.scalar.activation(HRS[g][:, 0:n], HRS[g][:, 0:n], ACT.Exp, scale=-0.5).then_inc(s_hr, 1)
                        if c in OUT_STEP:
                            g = OUT_STEP.index(c)
                            n = P * (GROUPS[g][1] - GROUPS[g][0])
                            act.wait_ge(s_h3, NT * p + GROUPS[g][1])
                            need(act, s_hg, 3 * p + min(g, 1))
                            nc.scalar.activation(OC[g][:, 0:n], OB[:, 0:n], ACT.Copy).then_inc(s_oc, 1)
                            act.wait_ge(s_oc, 3 * p + g + 1)
                            need(act, s_hm, 3 * p + min(g, 1))
                            nc.scalar.activation(HSQ[g][:, 0:n], OC[g][:, 0:n], ACT.Square).then_inc(s_hs, 1)
                    if p + 1 < PAIRS and m in STACK_STEPS:
                        high_parts(p + 1, STACK_STEPS.index(m))
                    for w12 in ended(A_PIECES[m]):
                        if p + 1 < PAIRS:
                            window_attention(p + 1, w12)
                        else:
                            window_gate(w12 // 6, w12 // 3 % 2, w12 % 3)
                    if p == PAIRS - 1 and m in RELOAD_STEPS:
                        gated_high(RELOAD_STEPS.index(m))
            for kind in range(2):
                for w in range(NW):
                    window_gate(2, kind, w)
                    for t in ((3, 4), (5,), (6,), (7,), (), ())[3 * kind + w]:
                        if t == 3:
                            recurrence_over(act, PAIRS - 1)
                            act.wait_ge(s_h3, NT * PAIRS)
                            act.wait_ge(s_sso, 16 * PAIRS)
                            act.wait_ge(s_so, 16 * PAIRS)
                        gated_high(t)
            for dm in range(3, 8):
                for kind in range(2):
                    for w in range(NW):
                        window_gate(dm, kind, w)
            act.wait_ge(s_win, OUT_W0)
            for dm in range(7):
                act.wait_ge(s_mg, 3 * dm + 3)
                nc.scalar.activation(xh[:, dm, :], slots[dm][:, :], ACT.Copy).then_inc(s_mh, 1)
            for w in range(NW):
                cols = slice(w * WIN, (w + 1) * WIN)
                act.wait_ge(s_mg, 21 + w + 1)
                nc.scalar.activation(xh[:, 7, cols], slots[7][:, cols], ACT.Copy).then_inc(s_mh, 1)
            def y_rstd(w):
                act.wait_ge(s_yn, w + 1)
                nc.scalar.activation(yrs[w][:, :], Z[w][:, 0:WIN], ACT.Ln, scale=-1.0 / D, bias=eps_col).then_inc(s_yl, 1)
                act.wait_ge(s_yl, w + 1)
                nc.scalar.activation(yrs[w][:, :], yrs[w][:, :], ACT.Exp, scale=-0.5).then_inc(s_yr, 1)

            act.wait_ge(s_u, 24)
            for n in range(3 * KT_N):
                k, w = output_product(n)
                act.wait_ge(s_win, OUT_W0 + n + 1)
                need(act, s_ya, 3 * (k - 2) + w + 1 if k > 1 else 0)
                dst = ysa[w] if k == 0 else ysq[w]
                nc.scalar.activation(dst[:, :], CH[n % 2][:, 0:WIN], ACT.Square).then_inc(s_yq, 1)
                nc.scalar.activation(yb[:, k, w * WIN:(w + 1) * WIN], CH[n % 2][:, 0:WIN], ACT.Copy,
                                     scale=gpost[:, k:k + 1]).then_inc(s_ev, 1)
                if n in (20, 22):
                    y_rstd(n // 2 - 10)
            y_rstd(2)

        @block.vector
        def _(dve):
            V = nc.vector

            def split_weights(g):
                dve.wait_ge(s_raw[g % 3], 16 * (g // 3 + 1))
                chunk_done(dve, g - 2)
                V.tensor_copy(wh[g % 2][:, :, :], wr[g % 3][:, :, :]).then_inc(s_whi, 1)
                dve.wait_ge(s_whi, g + 1)
                V.tensor_tensor(wl[g % 3][:, :, :], wr[g % 3][:, :, :], wh[g % 2][:, :, :].bitcast(F32),
                                ALU.subtract).then_inc(s_wlo, 1)

            def turned(idx, dst, waits):
                for s, v in waits:
                    need(dve, s, v)
                dve.wait_ge(s_tr, idx + 1)
                V.tensor_copy(dst, TB[:, 0:WIN]).then_inc(s_te, 1)

            def window_attention(pp, w12):
                c, w = divmod(w12, 3)
                if w == 0:
                    split_weights(8 * pp + c + 1)

            def low_parts(pp, what):
                dve.wait_ge(s_qkh, 6 * pp + (2, 6)[what])
                for h in range(2):
                    own, other = slice(DH * h, DH * h + DH), slice(DH * (1 - h), DH * (1 - h) + DH)
                    dst, src, high = ((KS[h][other, :], kT, KS[h]), (qlo[own, 0:SEQ], qT, QS[h]))[what]
                    V.tensor_tensor(dst, src[own, 0:SEQ], high[own, :].bitcast(F32), ALU.subtract).then_inc(s_qkl, 1)

            def turn_attention(pp, w12):
                c, w = divmod(w12, 3)
                if c == 2:
                    turned(6 * pp + w, v_nat[:, w * WIN:(w + 1) * WIN], ((s_av, NS * pp), (s_vout, 16 * pp), (s_cp, 5 * pp)))

            def window_recurrence(p, w12):
                c, w = divmod(w12, 3)
                if w == 0:
                    split_weights(4 + 8 * p + c + 1)

            def turn_recurrence(p, w12):
                c, w = divmod(w12, 3)
                if c == 2:
                    turned(6 * p + 3 + w, i_nat[:, w * WIN:(w + 1) * WIN], ((s_h3, NT * p), (s_im, NT * p)))

            def values_low(p, c):
                dve.wait_ge(s_im, NT * p + c + 1)
                blocks, rows, b0 = (4, rows4, 4 * (c % 2)) if c < 8 else (8, rows8, 0)
                for b in range(blocks):
                    i = V.scalar_tensor_tensor(imaskL[:, b0 + b, :], i_nat[:, c * P:(c + 1) * P], rows[:, b:b + 1],
                                               imaskH[:, b0 + b, :].bitcast(F32), ALU.mult, ALU.subtract)
                i.then_inc(s_iml, 1)

            def gated_low(t):
                dve.wait_ge(s_gh, t + 1)
                r = graw[:, ROW_OF[t], :]
                V.tensor_tensor(gl[:, ROW_OF[t], :], r, gh[:, ROW_OF[t], :].bitcast(F32), ALU.subtract).then_inc(s_gl, 1)

            for r in range(1, 4):
                dve.wait_ge(s_xsq, r + 1)
                need(dve, s_xsa, r - 1)
                V.tensor_tensor(xsa[0][:, :, :], xsa[0][:, :, :], xsq[r % 2][:, :, :], ALU.add).then_inc(s_xsa, 1)
            dve.wait_ge(s_c, 32)
            V.memset(qbd[:, :, :, :], 0.0).then_inc(s_qz, 1)
            V.tensor_scalar(ngate[:, :], bgate, -1.0, None, ALU.mult)
            V.tensor_tensor(lbv[:, 0, :], lbraw[:, 0:4], lbraw[:, 4:8], ALU.max).then_inc(s_lb, 1)
            dve.wait_ge(s_lb, 1)
            for r in range(2):
                V.tensor_tensor(lbv[:, 1 + r, :], lbraw[:, 4 * r:4 * r + 4], lbv[:, 0, :], ALU.subtract).then_inc(s_lb, 1)
            dve.wait_ge(s_lbe, 1)
            V.tensor_tensor(lbv[:, 3, :], lbv[:, 1, :], lbv[:, 2, :], ALU.add).then_inc(s_lb, 1)
            dve.wait_ge(s_lb, 4)
            V.reciprocal(lbv[:, 3, :], lbv[:, 3, :]).then_inc(s_lb, 1)
            dve.wait_ge(s_lb, 5)
            V.tensor_tensor(lbv[:, 4, :], lbv[:, 2, :], lbv[:, 3, :], ALU.mult).then_inc(s_lb, 1)
            split_weights(0)
            V.tensor_copy(negtri_r[:, :], negtri).then_inc(s_cr, 1)
            V.tensor_copy(negones_r[:, :], negones).then_inc(s_cr, 1)
            for w in range(NW):
                def low(r):
                    dve.wait_ge(s_xhi, 4 * w + r + 1)
                    t, cols = slice(2 * r, 2 * r + 2), slice(w * WIN, (w + 1) * WIN)
                    V.tensor_tensor(xl[:, t, cols], xw[w][:, t, :], xh[:, t, cols].bitcast(F32), ALU.subtract).then_inc(s_xlo, 1)

                dve.wait_ge(s_xrs, w + 1)
                for k in range(KT_N):
                    V.scalar_tensor_tensor(xw[w][:, k, :], xw[w][:, k, :], gpre[:, k:k + 1], xrs[:, 0:WIN],
                                           ALU.mult, ALU.mult).then_inc(s_xn, 1)
                    if k in (3, 5, 7):
                        low((k - 3) // 2)
                low(3)
                if w == 0:
                    split_weights(1)
            for w12 in range(12):
                if w12 >= 3:
                    window_attention(0, w12)
                if w12:
                    turn_attention(0, w12 - 1)
                if w12 in (8, 10):
                    low_parts(0, w12 // 2 - 4)
            turn_attention(0, 11)

            for p in range(PAIRS):
                recurrence_over(dve, p - 1, norm=False)
                late = []
                for n in range(B_STEPS):
                    if n < NS:
                        c0, t = first_col(n), NS * p + n
                        h, q, e = STEPS[n][2], tile_rank(n), E[n % 3]
                        dve.wait_ge(s_L, t + 1)
                        i = V.scalar_tensor_tensor(e[:, c0:QW], e[:, c0:QW], 88.0, Z[n % 3][:, c0:QW], ALU.min, ALU.max)
                        if diagonal(n):
                            i.then_inc(s_sp1, 1)
                            dve.wait_ge(s_sp1, DIAGS * p + diagonals_until(n))
                            V.tensor_tensor(e[:, c0:c0 + P], e[:, c0:c0 + P], causal, ALU.mult).then_inc(s_sp, 1)
                        else:
                            i.then_inc(s_sp, 1)
                        if q > 0:
                            dve.wait_ge(s_sp, t + 1)
                            need(dve, s_cum, t - 1)
                            V.tensor_copy(SPH[n % 2][:, c0:QW], e[:, c0:QW]).then_inc(s_sph, 1)
                            dve.wait_ge(s_sph, SPLITS * p + rows_until(n))
                            V.tensor_tensor(SPL[n % 2][:, c0:QW], e[:, c0:QW], SPH[n % 2][:, c0:QW].bitcast(F32),
                                            ALU.subtract).then_inc(s_spl, 1)
                        if q > 1:
                            cs = first_col(n - 2)
                            dve.wait_ge(s_S, SUMS * p + sums_until(n - 2))
                            V.tensor_copy(SUH[h][:, cs:QW], SUM[h][:, cs:QW]).then_inc(s_Sh, 1)
                            dve.wait_ge(s_Sh, SUM_SPLITS * p + sum_rows_until(n))
                            V.tensor_tensor(SUL[h][:, cs:QW], SUM[h][:, cs:QW], SUH[h][:, cs:QW].bitcast(F32),
                                            ALU.subtract).then_inc(s_Sl, 1)
                    if n >= 3:
                        wd, j, h = STEPS[n - 3]
                        if j == 0 and h == 1:
                            dve.wait_ge(s_silu, 6 * p + 3)
                            dve.wait_ge(s_av, NS * p + n - 2)
                            V.tensor_tensor(zA[:, wd * QW:(wd + 1) * QW], OB[:, :], zA[:, wd * QW:(wd + 1) * QW],
                                            ALU.mult).then_inc(s_gA, 1)
                    if n == 12:
                        dve.wait_ge(s_te, 6 * p + 3)
                        dve.wait_ge(s_silu, 6 * p + 3)
                        dve.wait_ge(s_ev, win_of(8 * p if p else 0) + 12)
                        need(dve, s_zs, 3 * p)
                        need(dve, s_os, p)
                        need(dve, s_spA, 32 * p)
                        dve.wait_ge(s_qz, 1)
                        for h in range(2):
                            r = slice(DH * h, DH * h + DH)
                            V.tensor_copy(qbd[r, :, h, :], qT[r, SEQ:TOK].rearrange("d (i t) -> d i t", t=DSEQ)).then_inc(s_cp, 1)
                        V.tensor_copy(kTs[:, :], kT[:, SEQ:TOK]).then_inc(s_cp, 1)
                        V.tensor_copy(vs[:, :], v_nat[:, SEQ:TOK]).then_inc(s_cp, 1)
                        V.tensor_copy(zAs[:, :], zA[:, SEQ:TOK]).then_inc(s_cp, 1)
                    for w12 in late:
                        turn_recurrence(p, w12)
                    late = ended(B_PIECES[n])
                    for w12 in late:
                        window_recurrence(p, w12)
                for w12 in late:
                    turn_recurrence(p, w12)

                attention_over(dve, p)
                late = []
                for m in range(A_STEPS):
                    if m == 0:
                        dve.wait_ge(s_lf, 3 * (p + 1))
                        for c in range(NT):
                            cols = slice(c * P, (c + 1) * P)
                            V.tensor_tensor_scan(lf[:, cols], reset if c < 8 else reset_s, lf[:, cols], 0.0,
                                                 ALU.mult, ALU.add).then_inc(s_scan, 1)
                        dve.wait_ge(s_scan, NT * (p + 1))
                        bp = lf[:, 0:SEQ].rearrange("c (n t) -> c n t", t=BLK)
                        bs = lf[:, SEQ:TOK].rearrange("c (n t) -> c n t", t=DSEQ)
                        V.tensor_copy(bm[:, 0:NBLK], bp[:, :, BLK // 2 - 1]).then_inc(s_bmc, 1)
                        V.tensor_copy(bm[:, NBLK:], bs[:, :, DSEQ // 2 - 1]).then_inc(s_bmc, 1)
                        V.tensor_copy(be[:, 0:NBLK], bp[:, :, BLK - 1]).then_inc(s_bmc, 1)
                        V.tensor_copy(be[:, NBLK:], bs[:, :, DSEQ - 1]).then_inc(s_bmc, 1)
                        dve.wait_ge(s_bmc, 4 * (p + 1))
                        V.tensor_tensor(bp, bp, bm[:, 0:NBLK, None].broadcast_to([P, NBLK, BLK]), ALU.subtract).then_inc(s_A, 1)
                        V.tensor_tensor(bs, bs, bm[:, NBLK:, None].broadcast_to([P, STREAMS, DSEQ]), ALU.subtract).then_inc(s_A, 1)
                        V.tensor_tensor(be[:, :], be[:, :], bm[:, :], ALU.subtract).then_inc(s_ge, 1)
                        dve.wait_ge(s_ge, 2 * p + 1)
                        V.tensor_tensor(be[:, 0:NBLK - 1], be[:, 0:NBLK - 1], bm[:, 1:NBLK], ALU.add).then_inc(s_ge, 1)
                        dve.wait_ge(s_zs, 3 * (p + 1))
                        need(dve, s_so, 16 * p)
                        V.memset(St[0][:, :], 0.0).then_inc(s_S0, 1)
                        for r, (bk, lo, n) in enumerate(((Z[2], 4, 1), (Z[1], 2, 2), (Z[0], 0, 2))):
                            dve.wait_ge(s_Ls, 3 * p + r + 1)
                            V.scalar_tensor_tensor(SPs[:, lo:lo + n, :].rearrange("s j c -> s (j c)"),
                                                   Es[:, lo:lo + n, :].rearrange("s j c -> s (j c)"), 88.0, bk[:, 0:256 * n],
                                                   ALU.min, ALU.max).then_inc(s_sps, 1)
                            if r == 0:
                                dve.wait_ge(s_sps, 3 * p + 1)
                                V.tensor_tensor(SPs[:, 4, :], SPs[:, 4, :], smask, ALU.mult).then_inc(s_spm, 1)
                        dve.wait_ge(s_spm, p + 1)
                        dve.wait_ge(s_sps, 3 * (p + 1))
                        dve.wait_ge(s_av, NS * (p + 1))
                        V.tensor_copy(SPsH[:, :, :], SPs[:, :, :]).then_inc(s_sphs, 1)
                        dve.wait_ge(s_sphs, p + 1)
                        dve.wait_ge(s_Ss, 3 * (p + 1))
                        V.tensor_tensor(SPsL[:, :, :], SPs[:, :, :], SPsH[:, :, :].bitcast(F32), ALU.subtract).then_inc(s_spls, 1)
                        V.tensor_copy(SUsH[:, :, :], SUs[:, :, :]).then_inc(s_Shs, 1)
                        dve.wait_ge(s_Shs, p + 1)
                        V.tensor_tensor(SUsL[:, :, :], SUs[:, :, :], SUsH[:, :, :].bitcast(F32), ALU.subtract).then_inc(s_Sls, 1)
                    if m == 1:
                        dve.wait_ge(s_as, 3 * p + 1)
                        V.tensor_tensor(Es[:, 4, :], Es[:, 4, :], smask, ALU.mult).then_inc(s_asm, 1)
                        dve.wait_ge(s_EX, 4 * (p + 1))
                        V.tensor_tensor(kb[:, :], kb[:, :], EK[:, :], ALU.mult).then_inc(s_hki, 1)
                        dve.wait_ge(s_hki, p + 1)
                        V.tensor_tensor(lf[:, 0:SEQ].rearrange("c (n t) -> c n t", t=BLK), kb[:, 0:SEQ].rearrange("c (n t) -> c n t", t=BLK),
                                        gg[:, 0:NBLK, None].broadcast_to([P, NBLK, BLK]), ALU.mult).then_inc(s_hke, 1)
                        V.tensor_tensor(lf[:, SEQ:TOK].rearrange("c (n t) -> c n t", t=DSEQ), kb[:, SEQ:TOK].rearrange("c (n t) -> c n t", t=DSEQ),
                                        gg[:, NBLK:, None].broadcast_to([P, STREAMS, DSEQ]), ALU.mult).then_inc(s_hke, 1)
                    if m == 2:
                        dve.wait_ge(s_os, p + 1)
                        dve.wait_ge(s_cp, 5 * (p + 1))
                        ob = OB[:, 0:256].rearrange("d (i h t) -> d i h t", h=2, t=DSEQ)
                        for h in range(2):
                            r = slice(DH * h, DH * h + DH)
                            z = zAs[r, :].rearrange("d (i t) -> d i t", t=DSEQ)
                            V.tensor_tensor(z, ob[r, :, h, :], z, ALU.mult).then_inc(s_gs, 1)
                        dve.wait_ge(s_S0l, 16 * (p + 1))
                        V.tensor_tensor(S0s[:, :, :], S0s[:, :, :], em[:, :, None].broadcast_to([P, STREAMS, P]), ALU.mult).then_inc(s_S0m, 1)
                    if m >= 3:
                        c = m - 3
                        if c < NT:
                            dve.wait_ge(s_at, NT * p + c + 1)
                            if c >= 3:
                                dve.wait_ge(s_h3, NT * p + c - 2)
                            V.scalar_tensor_tensor(attm[c % 3][:, :], Z[2][:, 0:P], BIG, hgmask if c < 8 else hgmask_s,
                                                   ALU.min, ALU.mult).then_inc(s_atm, 1)
                            dve.wait_ge(s_kn, NT * p + c + 1)
                            if c >= 2:
                                dve.wait_ge(s_KV, NT * p + c - 1)
                            V.tensor_tensor(kendL[c % 2][:, :], XB[:, 0:P], kendH[c % 2][:, :].bitcast(F32),
                                            ALU.subtract).then_inc(s_knl, 1)
                            if c < 8:
                                values_low(p, c)
                        if 1 <= c <= 8:
                            b = c - 1
                            dve.wait_ge(s_KV, NT * p + b + 1)
                            if b == 0:
                                dve.wait_ge(s_S0, p + 1)
                            for s in range(4):
                                n = 4 * b + s
                                need(dve, s_ch, NBLK * p + n)
                                if n >= 7:
                                    dve.wait_ge(s_h3, NT * p + (n - 7) // 4 + 1)
                                V.scalar_tensor_tensor(St[(n + 1) % 8][:, :], St[n % 8][:, :], gg[:, n:n + 1],
                                                       Z[b % 2][:, s * P:(s + 1) * P], ALU.mult, ALU.add).then_inc(s_ch, 1)
                        if c == NT + 1:
                            dve.wait_ge(s_h3, NT * (p + 1))
                            V.tensor_tensor(S0s[:, :, :], S0s[:, :, :], gg[:, NBLK:, None].broadcast_to([P, STREAMS, P]),
                                            ALU.mult).then_inc(s_ss1, 1)
                            dve.wait_ge(s_ss1, p + 1)
                            dve.wait_ge(s_KV, NT * (p + 1))
                            for half in range(2):
                                s = S0s[:, 4 * half:4 * half + 4, :].rearrange("c i v -> c (i v)")
                                V.tensor_tensor(s, Z[half][:, :], s, ALU.add).then_inc(s_ss, 1)
                        if c == 8:
                            values_low(p, c)
                        if c in MS_STEP:
                            g = MS_STEP.index(c)
                            t0, t1 = GROUPS[g]
                            n = P * (t1 - t0)
                            dve.wait_ge(s_hr, 3 * p + g + 1)
                            V.tensor_tensor(OC[g][:, 0:n], OC[g][:, 0:n], HRS[g][:, 0:n], ALU.mult).then_inc(s_hg1, 1)
                            dve.wait_ge(s_hg1, 3 * p + g + 1)
                            dve.wait_ge(s_silu, 6 * p + 6)
                            V.scalar_tensor_tensor(zB[:, t0 * P:t1 * P], OC[g][:, 0:n], hgn[:, p:p + 1], zB[:, t0 * P:t1 * P],
                                                   ALU.mult, ALU.mult).then_inc(s_hg, 1)
                    if p + 1 < PAIRS and m in STACK_STEPS[1:]:
                        low_parts(p + 1, STACK_STEPS.index(m) - 1)
                    if p + 1 < PAIRS:
                        for w12 in late:
                            turn_attention(p + 1, w12)
                        late = ended(A_PIECES[m])
                        for w12 in late:
                            window_attention(p + 1, w12)
                    else:
                        for w12 in ended(A_PIECES[m]):
                            if w12 % 3 == 0:
                                split_weights(32 + w12 // 3 + 1)
                        if m in RELOAD_STEPS:
                            gated_low(RELOAD_STEPS.index(m))
                if p + 1 < PAIRS:
                    for w12 in late:
                        turn_attention(p + 1, w12)

            def products(dm, w):
                n = 3 * dm + w
                cols = slice(w * WIN, (w + 1) * WIN)
                dve.wait_ge(s_u, n + 1)
                dve.wait_ge(s_sig, 6 * dm + 3 + w + 1)
                a, b = slots[dm][:, cols], slots[GATE_B_SLOT[dm]][:, cols]
                V.tensor_tensor(a, UA[n % 2][:, 0:WIN], a, ALU.mult).then_inc(s_ma, 1)
                V.tensor_tensor(b, UB[n % 2][:, 0:WIN], b, ALU.mult).then_inc(s_mb, 1)

            def merged_low(dm, cols=slice(0, TOK), n=None):
                dve.wait_ge(s_mh, dm + 1 if n is None else n)
                V.tensor_tensor(xl[:, dm, cols], slots[dm][:, cols], xh[:, dm, cols].bitcast(F32), ALU.subtract).then_inc(s_ml, 1)

            for g in range(GATE_G0 + 4, OUT_G0):
                what, dm, kind = MERGE[g - GATE_G0]
                for w in range(NW):
                    if what == "branch":
                        if dm == 7:
                            for d in ((0, 1), (2,), (3, 4))[w]:
                                merged_low(d)
                        products(dm, w)
                    if w == 0:
                        split_weights(g + 1)
                    if dm == 2 and what == "gate":
                        for t in ((3, 4), (5,), (6,), (7,), (), ())[3 * kind + w]:
                            gated_low(t)
            merged_low(5)
            merged_low(6)
            for w in range(NW):
                merged_low(7, slice(w * WIN, (w + 1) * WIN), 8 + w)
            dve.wait_ge(s_u, 24)
            V.memset(no4[:, :], -1.0).then_inc(s_no, 1)
            for k in range(KT_N - 1):
                split_weights(OUT_G0 + k + 1)
            for w in range(NW):
                y, x = yb[:, 0:6, w * WIN:(w + 1) * WIN], xres[:, 0:6, w * WIN:(w + 1) * WIN]
                dve.wait_ge(s_yr, w + 1)
                dve.wait_ge(s_ev, OUT_W0 + 20 + 2 * w)
                for lo, hi in ((0, 3), (3, 6)):
                    V.tensor_tensor(y[:, lo:hi, :], y[:, lo:hi, :], yrs[w][:, None, :].broadcast_to([P, hi - lo, WIN]),
                                    ALU.mult).then_inc(s_yg, 1)
                    dve.wait_ge(s_yg, 2 * w + (1 if lo == 0 else 2))
                    if w == 0:
                        dve.wait_ge(s_xr, 16)
                    V.tensor_tensor(y[:, lo:hi, :], y[:, lo:hi, :], x[:, lo:hi, :], ALU.add).then_inc(s_yo, 1)

        @block.gpsimd
        def _(pool):
            G = nc.gpsimd

            def silu_product(n, idx, half, z):
                pool.wait_ge(s_sg, half + 1)
                pool.wait_ge(s_ev, n + 1)
                G.tensor_tensor(z, z, tmpT[idx % 2][:, :], ALU.mult).then_inc(s_silu, 1)

            def window_attention(pp, w12):
                c, w = divmod(w12, 3)
                if c == 3:
                    silu_product(win_of(8 * pp if pp else 0) + w12, 12 * pp + 3 + w, 6 * pp + w, zA[:, w * WIN:(w + 1) * WIN])

            def window_recurrence(p, w12):
                c, w = divmod(w12, 3)
                if c == 3:
                    silu_product(win_of(4 + 8 * p) + w12, 12 * p + 9 + w, 6 * p + 3 + w, zB[:, w * WIN:(w + 1) * WIN])

            for m in range(3, 3 * NW):
                w, r = m // 3, m % 3 + 1
                pool.wait_ge(s_xsq, 4 * w + r + 1)
                pool.wait_ge(s_xsa, m)
                G.tensor_tensor(xsa[w % 2][:, :, :], xsa[w % 2][:, :, :], xsq[(3 * w + r) % 2][:, :, :], ALU.add).then_inc(s_xsa, 1)
            for w12 in range(12):
                window_attention(0, w12)
            for p in range(PAIRS):
                def later_sum(n):
                    h, q = STEPS[n][2], tile_rank(n)
                    c0, t = first_col(n), NS * p + n
                    src, dst = E[n % 3], SUM[h]
                    pool.wait_ge(s_sp, t + 1)
                    if q == 0:
                        need(pool, s_Sl, SUM_SPLITS * p + sum_rows_until(n))
                        G.tensor_copy(dst[:, c0:QW], src[:, c0:QW]).then_inc(s_S, 1)
                        return
                    if q == 1:
                        pool.wait_ge(s_cum, t + 1)
                    else:
                        pool.wait_ge(s_Sl, SUM_SPLITS * p + sum_rows_until(n))
                    pool.wait_ge(s_S, SUMS * p + sums_until(n - 2))
                    lo = first_col(n - 2)
                    if lo > c0:
                        G.tensor_copy(dst[:, c0:lo], src[:, c0:lo])
                    G.tensor_tensor(dst[:, lo:QW], dst[:, lo:QW], src[:, lo:QW], ALU.add).then_inc(s_S, 1)

                recurrence_over(pool, p - 1, norm=False)
                for n in range(B_STEPS):
                    if 2 <= n <= NS + 1 and diagonal(n - 2):
                        m = n - 2
                        c0 = first_col(m)
                        pool.wait_ge(s_a, NS * p + m + 1)
                        G.tensor_tensor(Aw[m % 2][:, c0:c0 + P], Aw[m % 2][:, c0:c0 + P], causal, ALU.mult).then_inc(s_am, 1)
                    if 1 <= n <= NS and tile_rank(n - 1) == 1:
                        later_sum(n - 1)
                    if n < NS and STEPS[n][1] > 0 and tile_rank(n) != 1:
                        later_sum(n)
                    for w12 in ended(B_PIECES[n]):
                        window_recurrence(p, w12)
                attention_over(pool, p)
                for m in range(A_STEPS):
                    if m == 0:
                        pool.wait_ge(s_spm, p + 1)
                        for q, j in enumerate((3, 2, 1)):
                            if q == 0:
                                pool.wait_ge(s_sps, 3 * p + 2)
                                last = SPs[:, 4, :]
                            else:
                                pool.wait_ge(s_sps, 3 * p + (2 if j >= 2 else 3))
                                pool.wait_ge(s_Ss, 3 * p + q)
                                last = SUs[:, q - 1, :]
                            G.tensor_tensor(SUs[:, q, :], last, SPs[:, j, :], ALU.add).then_inc(s_Ss, 1)
                    if m == 1:
                        pool.wait_ge(s_EX, 4 * (p + 1))
                        G.tensor_tensor(hq[:, :], hq[:, :], EQ[:, :], ALU.mult).then_inc(s_hqd, 1)
                    if 2 <= m < NT + 2:
                        c = m - 2
                        blocks, rows = (4, rows4) if c < 8 else (8, rows8)
                        if c == 0:
                            pool.wait_ge(s_te, 6 * (p + 1))
                            pool.wait_ge(s_zs, 3 * (p + 1))
                        if c >= 2:
                            pool.wait_ge(s_KV, NT * p + (c - 1 if c < 8 else 8))
                        b0 = 4 * (c % 2)
                        G.tensor_tensor(imaskH[:, b0:b0 + blocks, :],
                                        i_nat[:, None, c * P:(c + 1) * P].broadcast_to([P, blocks, P]),
                                        rows[:, :, None].broadcast_to([P, blocks, P]), ALU.mult).then_inc(s_im, 1)
                    if p + 1 < PAIRS:
                        for w12 in ended(A_PIECES[m]):
                            window_attention(p + 1, w12)
            for dm in range(8):
                for w in range(NW):
                    cols = slice(w * WIN, (w + 1) * WIN)
                    pool.wait_ge(s_mb, 3 * dm + w + 1)
                    pool.wait_ge(s_ma, 3 * dm + w + 1)
                    G.tensor_tensor(slots[dm][:, cols], slots[dm][:, cols], slots[GATE_B_SLOT[dm]][:, cols], ALU.add).then_inc(s_mg, 1)
            def add_square(k, w):
                pool.wait_ge(s_yq, (3 * k + w if k < 6 else 18 + 2 * w) + 1)
                need(pool, s_ya, 3 * (k - 2) + w + 1)
                G.tensor_tensor(ysa[w][:, :], ysa[w][:, :], ysq[w][:, :], ALU.add).then_inc(s_ya, 1)

            def finish(w):
                y, x = yb[:, 6:8, w * WIN:(w + 1) * WIN], xres[:, 6:8, w * WIN:(w + 1) * WIN]
                pool.wait_ge(s_yr, w + 1)
                pool.wait_ge(s_ev, OUT_W0 + 20 + 2 * w)
                G.tensor_tensor(y, y, yrs[w][:, None, :].broadcast_to([P, 2, WIN]), ALU.mult).then_inc(s_yg3, 1)
                pool.wait_ge(s_yg3, w + 1)
                G.tensor_tensor(y, y, x, ALU.add).then_inc(s_yo3, 1)

            for k in range(1, KT_N - 2):
                for w in range(NW):
                    add_square(k, w)
            pool.wait_ge(s_xr, 16)
            add_square(KT_N - 2, 0)
            add_square(KT_N - 2, 1)
            finish(0)
            add_square(KT_N - 2, 2)
            finish(1)
            finish(2)


def constants():
    c2 = np.zeros((P, C2_W), np.float32)
    s, t = np.arange(P)[:, None], np.arange(P)[None, :]

    def put(name, value):
        o, n = C2[name]
        c2[:, o:o + n] = value

    put("negtri", -(s >= t).astype(np.float32))
    put("negones", -1.0)
    put("causal", s < t)
    put("hgmask", (s <= t) & (s // BLK == t // BLK))
    put("hgmask_s", (s <= t) & (s // DSEQ == t // DSEQ))
    col = np.arange(256)[None, :]
    put("smask", (s // DSEQ == col // 32) & (s % DSEQ < col % DSEQ))
    put("reset", np.broadcast_to(t % BLK != 0, (P, P)))
    put("reset_s", np.broadcast_to(t % DSEQ != 0, (P, P)))
    put("rows4", s // BLK == np.arange(4)[None, :])
    put("rows8", s // DSEQ == np.arange(8)[None, :])
    return c2


def chunk_weights(w_in, wa, wb, w_out):
    def cols(m, c):
        return m[:, c * P:(c + 1) * P].reshape(KT_N, P, P).transpose(1, 0, 2).reshape(P, KT_N * P)

    def w_in_chunk(group, p):
        return cols(w_in, 4 * group + p)

    out = []

    def attention(p):
        out.extend(w_in_chunk(g, p) for g in (0, 1, 2, 3))

    def gates(dm):
        out.extend((cols(w_in, 32 + dm), cols(w_in, 40 + dm)))

    branches = np.concatenate([wa, wb], axis=0)
    attention(0)
    for p in range(PAIRS):
        out.extend(w_in_chunk(g, p) for g in (4, 5, 6, 7))
        if p + 1 < PAIRS:
            attention(p + 1)
        else:
            for dm in range(3):
                gates(dm)
    out.extend(cols(branches, dm) for dm in range(3))
    for dm in range(3, 8):
        gates(dm)
        out.append(cols(branches, dm))
    out.extend(cols(w_out, n) for n in range(8))
    return np.ascontiguousarray(np.stack(out))


def kernel(x_prompt, x_sample, cache_sb_k, cache_sb_v, state_hgrn, g_pre, w_in, b_gate, hg_lb_raw, hg_norm_g,
           w_branch_a, w_branch_b, w_out, g_post):
    import concourse.bacc as bacc
    from concourse.bass_utils import run_bass_kernel_spmd

    x = np.concatenate([np.asarray(x_prompt)[0], np.asarray(x_sample).reshape(-1, D)], axis=0)
    c1 = np.zeros((P, C1_W), np.float32)
    for name, value in (("ident", np.eye(P, dtype=np.float32)), ("bgate", np.asarray(b_gate)[0].reshape(16, P).T),
                        ("lbraw", np.asarray(hg_lb_raw).reshape(8, P).T), ("hgn", np.asarray(hg_norm_g)[0].T),
                        ("gpre", np.asarray(g_pre)[0].reshape(8, P).T), ("gpost", np.asarray(g_post)[0].reshape(8, P).T),
                        ("eps", np.float32(EPS))):
        o, n = C1[name]
        c1[:, o:o + n] = value
    ck = np.asarray(cache_sb_k)[0].reshape(STREAMS, PAST, PAIRS, P)
    cv = np.asarray(cache_sb_v)[0].reshape(STREAMS, PAST // P, P, PAIRS, P)
    arrays = {
        "xT": x.reshape(TOK, KT_N, P).transpose(2, 1, 0),
        "wch": chunk_weights(np.asarray(w_in)[0], np.asarray(w_branch_a)[0], np.asarray(w_branch_b)[0], np.asarray(w_out)[0]),
        "ckT": ck.transpose(2, 0, 3, 1),
        "cv": cv.transpose(3, 0, 2, 1, 4).reshape(PAIRS, STREAMS, P, 4 * P),
        "st": np.asarray(state_hgrn)[0].transpose(1, 0, 2, 3),
        "c1": c1,
        "c2": constants(),
    }
    arrays = {k: np.ascontiguousarray(v) for k, v in arrays.items()}
    outs = {"yT": (P, KT_N, TOK), "okT": (PAIRS, P, TOK), "ov": (PAIRS, TOK, P), "osp": (PAIRS, P, P),
            "oss": (PAIRS, STREAMS, P, P)}
    nc = bacc.Bacc("TRN2", target_bir_lowering=False, num_devices=1)
    args = [nc.dram_tensor(k, v.shape, F32, kind="ExternalInput").ap() for k, v in arrays.items()]
    args += [nc.dram_tensor(k, s, F32, kind="ExternalOutput").ap() for k, s in outs.items()]
    spill = nc.dram_tensor("gated", (2 * PAIRS, P, TOK), F32, kind="Internal").ap()
    build(nc, *args, spill)
    r = run_bass_kernel_spmd(nc, [arrays], core_ids=[0]).results[0]
    y = np.asarray(r["yT"]).transpose(2, 1, 0).reshape(TOK, D)
    k = np.asarray(r["okT"]).transpose(2, 0, 1).reshape(TOK, 8, DH)
    v = np.asarray(r["ov"]).transpose(1, 0, 2).reshape(TOK, 8, DH)
    c = np.ascontiguousarray
    return (c(y[None, :SEQ]), c(y[SEQ:].reshape(STREAMS, DSEQ, D)),
            c(k[None, None, :SEQ]), c(v[None, None, :SEQ]), c(np.asarray(r["osp"])[None, None]),
            c(k[SEQ:].reshape(1, STREAMS, DSEQ, 8, DH)), c(v[SEQ:].reshape(1, STREAMS, DSEQ, 8, DH)),
            c(np.asarray(r["oss"]).transpose(1, 0, 2, 3)[None]))
```
